# Optimizing a Trainium2 kernel written in Bass

```python
import jax, jax.numpy as jnp
from jax import lax
import numpy as np

D_MODEL = 2048
BATCH = 1
SEQ = 1024
DEPTH = 1

HEAD_DIM = 128
N_HEADS = D_MODEL // HEAD_DIM
SB_HEADS = N_HEADS // 2
DSA_HEADS = N_HEADS - SB_HEADS
DSA_KV_HEADS = 2
D_SB = SB_HEADS * HEAD_DIM
D_DSA = DSA_HEADS * HEAD_DIM
D_KV = DSA_KV_HEADS * HEAD_DIM
D_MIX = D_SB + D_DSA
IDX_HEADS = 16
IDX_DIM = 64
TOPK_MAX = 256
ROPE_THETA = 500000.0
ROPE_FRACTION_DIV = 4
Q_BLOCK = 128
EPS = 1e-6
D_IN = 4 * D_SB + 2 * D_DSA + 2 * D_KV + IDX_HEADS * IDX_DIM + IDX_DIM + IDX_HEADS

kernel_name = "hybrid_stickbreak_dsa_block"

def rmsnorm(x, g):
    xf = x.astype(jnp.float32)
    y = xf * lax.rsqrt(jnp.mean(xf * xf, axis=-1, keepdims=True) + EPS)
    return (y * g.astype(jnp.float32)).astype(x.dtype)

def partial_rope(x, pos):
    d_rot = x.shape[-1] // ROPE_FRACTION_DIV
    half = d_rot // 2
    inv_freq = jnp.power(ROPE_THETA, -jnp.arange(half, dtype=jnp.float32) / half)
    ang = pos.astype(jnp.float32)[..., None] * inv_freq
    cos = jnp.cos(ang)[:, :, None, :]
    sin = jnp.sin(ang)[:, :, None, :]
    xr = x[..., :d_rot].astype(jnp.float32)
    x1, x2 = xr[..., :half], xr[..., half:]
    rot = jnp.concatenate([x1 * cos - x2 * sin, x2 * cos + x1 * sin], axis=-1)
    return jnp.concatenate([rot.astype(x.dtype), x[..., d_rot:]], axis=-1)

def stick_breaking_attention(q, k, v):
    B, S, H, D = q.shape
    nb = S // Q_BLOCK
    scale = D ** -0.5
    key_pos = jnp.arange(S)
    qb = q.reshape(B, nb, Q_BLOCK, H, D).transpose(1, 0, 2, 3, 4)

    def block(args):
        qi, bi = args
        z = jnp.einsum('bthd,bshd->bhts', qi, k, preferred_element_type=jnp.float32) * scale
        q_pos = bi * Q_BLOCK + jnp.arange(Q_BLOCK)
        mask = (key_pos[None, :] < q_pos[:, None])[None, None]
        log_beta = jnp.where(mask, jax.nn.log_sigmoid(z), -jnp.inf)
        log_1m_beta = jnp.where(mask, jax.nn.log_sigmoid(-z), 0.0)
        tail = lax.cumsum(log_1m_beta, axis=3, reverse=True) - log_1m_beta
        w = jnp.exp(log_beta + tail)
        return jnp.einsum('bhts,bshd->bthd', w.astype(v.dtype), v)

    out = lax.map(block, (qb, jnp.arange(nb)))
    return out.transpose(1, 0, 2, 3, 4).reshape(B, S, H, D)

def dsa_sparse_attention(q, k, v, q_idx, k_idx, w_idx):
    B, S, H, D = q.shape
    G = k.shape[2]
    rep = H // G
    Hi, Di = q_idx.shape[2], q_idx.shape[3]
    topk = min(TOPK_MAX, S // 4)
    nb = S // Q_BLOCK
    scale = D ** -0.5
    idx_scale = Di ** -0.5
    key_pos = jnp.arange(S)
    qb = q.reshape(B, nb, Q_BLOCK, H, D).transpose(1, 0, 2, 3, 4)
    qib = q_idx.reshape(B, nb, Q_BLOCK, Hi, Di).transpose(1, 0, 2, 3, 4)
    wb = w_idx.reshape(B, nb, Q_BLOCK, Hi).transpose(1, 0, 2, 3)

    def block(args):
        qi, qii, wi, bi = args
        q_pos = bi * Q_BLOCK + jnp.arange(Q_BLOCK)
        causal = key_pos[None, :] <= q_pos[:, None]
        rel = jax.nn.relu(jnp.einsum('btid,bsd->btis', qii, k_idx,
                                     preferred_element_type=jnp.float32) * idx_scale)
        score = jnp.einsum('btis,bti->bts', rel, wi.astype(jnp.float32))
        score = jnp.where(causal[None], score, -jnp.inf)
        _, sel = lax.top_k(score, topk)
        valid = sel <= q_pos[None, :, None]
        k_sel = jax.vmap(lambda kb, ib: kb[ib])(k, sel)
        v_sel = jax.vmap(lambda vb, ib: vb[ib])(v, sel)
        qg = qi.reshape(B, Q_BLOCK, G, rep, D)
        s = jnp.einsum('btgrd,btkgd->btgrk', qg, k_sel,
                       preferred_element_type=jnp.float32) * scale
        s = jnp.where(valid[:, :, None, None, :], s, -jnp.inf)
        p = jax.nn.softmax(s, axis=-1)
        o = jnp.einsum('btgrk,btkgd->btgrd', p.astype(v.dtype), v_sel)
        return o.reshape(B, Q_BLOCK, H, D)

    out = lax.map(block, (qb, qib, wb, jnp.arange(nb)))
    return out.transpose(1, 0, 2, 3, 4).reshape(B, S, H, D)

def head_rmsnorm(o, g):
    B, S, H, D = o.shape
    return rmsnorm(o, g.reshape(H, D)).reshape(B, S, H * D)

def setup_inputs(seed: int = 0) -> dict:
    key = jax.random.key(seed)
    ks = jax.random.split(key, 8)
    x = jax.random.normal(ks[0], (BATCH, SEQ, D_MODEL), jnp.float32)
    positions = jnp.broadcast_to(jnp.arange(SEQ, dtype=jnp.int32)[None], (BATCH, SEQ))
    norm_g = 1.0 + 0.02 * jax.random.normal(ks[1], (DEPTH, D_MODEL), jnp.float32)
    w_in = jax.random.normal(ks[2], (DEPTH, D_MODEL, D_IN), jnp.float32) * D_MODEL ** -0.5
    sb_out_g = 1.0 + 0.02 * jax.random.normal(ks[3], (DEPTH, D_SB), jnp.float32)
    dsa_out_g = 1.0 + 0.02 * jax.random.normal(ks[4], (DEPTH, D_DSA), jnp.float32)
    w_out = jax.random.normal(ks[5], (DEPTH, D_MIX, D_MODEL), jnp.float32) * D_MIX ** -0.5
    final_g = 1.0 + 0.02 * jax.random.normal(ks[6], (D_MODEL,), jnp.float32)
    return {"x": x, "positions": positions, "norm_g": norm_g, "w_in": w_in,
            "sb_out_g": sb_out_g, "dsa_out_g": dsa_out_g, "w_out": w_out,
            "final_g": final_g}

def reference(x, positions, norm_g, w_in, sb_out_g, dsa_out_g, w_out, final_g):
    B, S, _ = x.shape
    sizes = (D_SB, D_SB, D_SB, D_SB, D_DSA, D_KV, D_KV, D_DSA,
             IDX_HEADS * IDX_DIM, IDX_DIM, IDX_HEADS)
    for layer in range(DEPTH):
        h = rmsnorm(x, norm_g[layer])
        proj = jnp.einsum('bsd,de->bse', h, w_in[layer])
        parts = []
        off = 0
        for n in sizes:
            parts.append(proj[..., off:off + n])
            off += n
        (sb_q, sb_k, sb_v, sb_gate, dq, dk, dv, dsa_gate, iq, ik, iw) = parts

        o_sb = stick_breaking_attention(sb_q.reshape(B, S, SB_HEADS, HEAD_DIM),
                                        sb_k.reshape(B, S, SB_HEADS, HEAD_DIM),
                                        sb_v.reshape(B, S, SB_HEADS, HEAD_DIM))
        o_sb = head_rmsnorm(o_sb, sb_out_g[layer]) * jax.nn.silu(sb_gate)

        q_d = partial_rope(dq.reshape(B, S, DSA_HEADS, HEAD_DIM), positions)
        k_d = partial_rope(dk.reshape(B, S, DSA_KV_HEADS, HEAD_DIM), positions)
        v_d = dv.reshape(B, S, DSA_KV_HEADS, HEAD_DIM)
        q_i = partial_rope(iq.reshape(B, S, IDX_HEADS, IDX_DIM), positions)
        k_i = partial_rope(ik.reshape(B, S, 1, IDX_DIM), positions)[:, :, 0, :]
        w_i = iw * (IDX_HEADS ** -0.5)
        o_dsa = dsa_sparse_attention(q_d, k_d, v_d, q_i, k_i, w_i)
        o_dsa = head_rmsnorm(o_dsa, dsa_out_g[layer]) * jax.nn.silu(dsa_gate)

        mixed = jnp.concatenate([o_sb, o_dsa], axis=-1)
        x = x + jnp.einsum('bse,ed->bsd', mixed, w_out[layer]).astype(x.dtype)
    return rmsnorm(x, final_g)


_drawn_inputs = setup_inputs


def setup_inputs(seed=0):
    import zlib

    import numpy as np

    out = dict(_drawn_inputs(seed))
    spreads = {}
    factors = {}
    for name, (base, spread) in spreads.items():
        noise = np.random.default_rng([zlib.crc32(name.encode()), seed]).standard_normal(out[name].shape)
        drawn = base * np.exp(spread * noise) if base else spread * noise
        out[name] = __import__('jax').numpy.asarray(drawn.astype(out[name].dtype))
    for name, factor in factors.items():
        out[name] = (out[name] * factor).astype(out[name].dtype)
    return out
```

```python
from contextlib import ExitStack

import numpy as np
import concourse.bass as bass
from concourse import mybir

F32 = mybir.dt.float32
F32R = mybir.dt.float32r
BF16 = mybir.dt.bfloat16
I32 = mybir.dt.int32
ALU = mybir.AluOpType
ACT = mybir.ActivationFunctionType
AX = mybir.AxisListType
ds = bass.ds

P = 128
SEQ = 1024
D_MODEL = 2048
HEAD_DIM = 128
SB_HEADS = 8
DSA_HEADS = 8
KV_HEADS = 2
REP = DSA_HEADS // KV_HEADS
IDX_HEADS = 16
IDX_DIM = 64
TOPK = 256
ROPE_THETA = 500000.0
EPS = 1e-6

KT = D_MODEL // P
ST = SEQ // P
HALF = SEQ // 2
QUARTER = SEQ // 4
GRAN = 2
KG = KT // GRAN
NQ = HEAD_DIM // 4 // 2
NI = IDX_DIM // 4 // 2

D_IN = 4 * 1024 + 2 * 1024 + 2 * 256 + IDX_HEADS * IDX_DIM + IDX_DIM + IDX_HEADS
NBLK = -(-D_IN // P)
IQ0 = 52
DQ0 = 32
ROT_BLKS = DSA_HEADS + KV_HEADS
IDX_BLKS = 1 + IDX_HEADS * IDX_DIM // P
ORDER = ([NBLK - 1] + list(range(IQ0, NBLK - 1)) + list(range(DQ0, DQ0 + ROT_BLKS)) + list(range(DQ0))
         + list(range(DQ0 + ROT_BLKS, IQ0)))
B_IK, B_IQ = 0, 1
B_DQ = IDX_BLKS
B_DK = B_DQ + DSA_HEADS
B_SBQ = B_DK + KV_HEADS
B_SBK, B_SBV, B_SBG = B_SBQ + 8, B_SBQ + 16, B_SBQ + 24
B_DV = B_SBQ + 32
B_DG = B_DV + KV_HEADS
FREE_BLKS = 4
SEL0 = TOPK // P
SEL_BLKS = 8
ROUNDS = TOPK // 8
ROUNDS_PER_BLK = ROUNDS // SEL_BLKS
assert IDX_BLKS + FREE_BLKS + (ST - SEL0) * SEL_BLKS == NBLK

ROT_PER_TILE = 2
assert ROT_PER_TILE * (ST - SEL0 - 1) == ROT_BLKS

TRIG_BLKS = 3
TWO_PI = 2 * np.pi
TWO_PI_PARTS = [6.28125, float(np.floor((TWO_PI - 6.28125) * 2.0 ** 17) / 2.0 ** 17)]
TWO_PI_PARTS.append(TWO_PI - sum(TWO_PI_PARTS))
ROUNDER = 1.5 * 2.0 ** 23
PI_BELOW = 3.1415925

MASKED = -1.0e30
TAKEN = -3.0e38
ROWS_DSA = slice(32, 64)


def normalise(nc, sem, x, norm_g, ident_d, y_hi, y_lo):
    with ExitStack() as ctx:
        sb = lambda name, shape, dt=F32: ctx.enter_context(nc.sbuf_tensor(name, shape, dt))
        x_sb = [sb(f"x_sb{b}", [P, D_MODEL]) for b in range(2)]
        y_sb = [sb(f"y_sb{b}", [P, D_MODEL]) for b in range(2)]
        g_sb = sb("g_sb", [P, D_MODEL])
        squares = sb("squares", [P, D_MODEL], BF16)
        sumsq = sb("sumsq", [P, 2])
        root = sb("root", [P, 2])
        rstd = sb("rstd", [P, 2])
        eps = sb("eps_n", [P, 1])
        ident = sb("ident_n", [P, P])
        turned = [ctx.enter_context(nc.psum_tensor(f"turned{j}", [P, 4, P], F32)) for j in range(4)]
        x_in = [sem("x_in0"), sem("x_in1")]
        g_in, ident_in, eps_set = sem("g_in"), sem("ident_in"), sem("eps_set")
        summed, rooted, inverted, y_made = sem("summed"), sem("rooted"), sem("inverted"), sem("y_made")
        tile_turned, hi_made, lo_made = sem("tile_turned"), sem("hi_made"), sem("lo_made")
        block = ctx.enter_context(nc.Block())

        @block.sync
        def _(sp):
            sp.dma_start(x_sb[0][:], x[0:P, :]).then_inc(x_in[0], 16)
            sp.dma_start(g_sb[:], norm_g.partition_broadcast(P)).then_inc(g_in, 16)
            sp.dma_start(ident[:], ident_d).then_inc(ident_in, 16)
            sp.dma_start(x_sb[1][:], x[P:2 * P, :]).then_inc(x_in[1], 16)
            with sp.Fori(1, ST // 2) as i:
                for b in range(2):
                    sp.wait_ge(y_made, 2 * i + b - 1)
                    sp.dma_start(x_sb[b][:], x[ds((2 * i + b) * P, P), :]).then_inc(x_in[b], 16)

        @block.gpsimd
        def _(pool):
            nc.gpsimd.memset(eps[:], EPS).then_inc(eps_set, 1)

        @block.scalar
        def _(act):
            act.wait_ge(eps_set, 1)

            def root_of_mean(i, b):
                t = 2 * i + b
                act.wait_ge(x_in[b], 16 * (i + 1))
                nc.scalar.activation(squares[:], x_sb[b][:], ACT.Square,
                                     accum_out=sumsq[:, b:b + 1]).then_inc(summed, 1)
                act.wait_ge(summed, t + 1)
                nc.scalar.activation(root[:, b:b + 1], sumsq[:, b:b + 1], ACT.Sqrt, bias=eps[:],
                                     scale=1.0 / D_MODEL).then_inc(rooted, 1)

            def hi_parts(t):
                for j in range(4):
                    act.wait_ge(tile_turned, 4 * t + j + 1)
                    nc.scalar.activation(y_hi[:, 4 * j:4 * j + 4, ds(t * P, P)], turned[j][:],
                                         ACT.Copy).then_inc(hi_made, 1)

            root_of_mean(0, 0)
            root_of_mean(0, 1)
            hi_parts(0)
            with act.Fori(1, ST // 2) as i:
                root_of_mean(i, 0)
                hi_parts(2 * i - 1)
                root_of_mean(i, 1)
                hi_parts(2 * i)
            hi_parts(ST - 1)

        @block.vector
        def _(dve):
            dve.wait_ge(g_in, 16)

            def make_y(i, b, first):
                t = 2 * i + b
                dve.wait_ge(rooted, t + 1)
                nc.vector.reciprocal(rstd[:, b:b + 1], root[:, b:b + 1]).then_inc(inverted, 1)
                dve.wait_ge(inverted, t + 1)
                if not first:
                    dve.wait_ge(tile_turned, 4 * (t - 1))
                nc.vector.scalar_tensor_tensor(y_sb[b][:], x_sb[b][:], rstd[:, b:b + 1], g_sb[:],
                                               ALU.mult, ALU.mult).then_inc(y_made, 1)

            def lo_parts(t):
                for j in range(4):
                    dve.wait_ge(hi_made, 4 * t + j + 1)
                    nc.vector.tensor_tensor(y_lo[:, 4 * j:4 * j + 4, ds(t * P, P)], turned[j][:],
                                            y_hi[:, 4 * j:4 * j + 4, ds(t * P, P)].bitcast(F32),
                                            ALU.subtract).then_inc(lo_made, 1)

            make_y(0, 0, True)
            make_y(0, 1, True)
            lo_parts(0)
            with dve.Fori(1, ST // 2) as i:
                make_y(i, 0, False)
                lo_parts(2 * i - 1)
                make_y(i, 1, False)
                lo_parts(2 * i)
            lo_parts(ST - 1)

        @block.tensor
        def _(pe):
            pe.wait_ge(ident_in, 16)

            def turn(i, b, first):
                t = 2 * i + b
                pe.wait_ge(y_made, t + 1)
                for j in range(4):
                    if not first:
                        pe.wait_ge(lo_made, 4 * t + j - 3)
                    for k in range(4):
                        mm = nc.tensor.transpose(turned[j][:, k, :],
                                                 y_sb[b][:, (4 * j + k) * P:(4 * j + k + 1) * P], ident[:])
                    mm.then_inc(tile_turned, 1)

            turn(0, 0, True)
            turn(0, 1, False)
            with pe.Fori(1, ST // 2) as i:
                turn(i, 0, False)
                turn(i, 1, False)


def project(nc, sem, w_in, positions, inv_freq, sin_sign, trig, window, ident_d, y_hi, y_lo, proj, sel_bias):
    with ExitStack() as ctx:
        sb = lambda name, shape, dt=F32: ctx.enter_context(nc.sbuf_tensor(name, shape, dt))
        ps = lambda name, shape: ctx.enter_context(nc.psum_tensor(name, shape, F32))
        w_raw = [sb(f"w_raw{g}", [P, KG, P]) for g in range(GRAN)]
        w_hi = [sb(f"w_hi{g}", [P, KG, P], F32R) for g in range(GRAN)]
        w_lo = [sb(f"w_lo{g}", [P, KG, P], F32R) for g in range(GRAN)]
        stage = sb("stage", [P, SEQ])
        q_idx = sb("q_idx", [P, IDX_BLKS - 1, P])
        q_swap = sb("q_swap", [P, IDX_BLKS - 1, P])
        trig_q = sb("trig_q", [P, 2, P])
        k_idx = [sb(f"k_idx{h}", [P, SEQ]) for h in range(2)]
        iw_t = sb("iw_t", [P, P])
        iw = sb("iw", [P, IDX_HEADS])
        relus = [sb(f"relus{b}", [P, SEQ]) for b in range(2)]
        causal = sb("causal", [P, SEQ])
        work = sb("work", [P, SEQ])
        bias_out = sb("bias_out", [P, SEQ], BF16)
        best = sb("best", [P, 8])
        freq = sb("freq", [P, 1])
        sign = sb("sign", [P, 1])
        pos, angle, turns, half_sin = causal, relus[0], relus[1], k_idx[0]
        rot = sb("rot", [P, ROT_PER_TILE, QUARTER])
        rot_swap = sb("rot_swap", [P, ROT_PER_TILE, QUARTER])
        rot_table = sb("rot_table", [P, 2, QUARTER])
        ident = sb("ident_p", [P, P])
        acc = [ps(f"acc{s}", [P, HALF]) for s in range(2)]
        rel = [ps(f"rel{b}", [P, SEQ]) for b in range(2)]
        iw_ps = ps("iw_ps", [P, HALF])

        w_loaded = [sem(f"w_loaded{g}") for g in range(GRAN)]
        hi_made, lo_made = sem("w_hi_made"), sem("w_lo_made")
        g0_used, half_done, evacuated, stored = sem("g0_used"), sem("half_done"), sem("evacuated"), sem("stored")
        prep_in, prep_set, k_step, k_ready = sem("prep_in"), sem("prep_set"), sem("k_step"), sem("k_ready")
        tile_in, q_step, q_ready = sem("tile_in"), sem("q_step"), sem("q_ready")
        iw_turned, iw_ready = sem("iw_turned"), sem("iw_ready")
        scored, relued, summed = sem("scored"), sem("relued"), sem("head_summed")
        pos_in, trig_step, sines, table_out = sem("pos_in"), sem("trig_step"), sem("sines"), sem("table_out")
        rot_in, rot_step, rot_made, rot_stored = sem("rot_in"), sem("rot_step"), sem("rot_made"), sem("rot_stored")
        topk_step, bias_made, bias_stored = sem("topk_step"), sem("bias_made"), sem("bias_stored")
        block = ctx.enter_context(nc.Block())
        TILE_DMAS = 10

        def width(u):
            return HALF

        GROUPS = [(0, 2, HALF), (2, 4, SEQ)]
        assert SEL0 + 2 == HALF // P and SEL0 + 6 == ST
        N_SEL0 = IDX_BLKS + FREE_BLKS

        @block.sync
        def _(sp):
            def load_block(n, first=False):
                for g in range(GRAN):
                    if not first:
                        sp.wait_ge(lo_made, 2 * n + g - 1)
                    sp.dma_start(w_raw[g][:], w_in[n, g]).then_inc(w_loaded[g], 16)

            def store_block(n):
                sp.wait_ge(evacuated, 2 * n + 2)
                sp.dma_start(proj[n], stage[:]).then_inc(stored, 16)

            def load_keys():
                sp.wait_ge(stored, 16 * IDX_BLKS)
                sp.wait_ge(table_out, 32)
                sp.wait_ge(prep_set, 6)
                for h, half in enumerate((0, IDX_DIM)):
                    sp.dma_start(k_idx[h][half:half + IDX_DIM, :], proj[B_IK, 0:IDX_DIM, :]).then_inc(prep_in, 16)
                    sp.dma_start(work[half:half + NI, :], proj[B_IK, NI:2 * NI, :]).then_inc(prep_in, 16)
                    sp.dma_start(work[half + NI:half + 2 * NI, :], proj[B_IK, 0:NI, :]).then_inc(prep_in, 16)
                for f in range(2):
                    sp.dma_start(relus[f][:], trig[f]).then_inc(prep_in, 16)
                    sp.wait_ge(prep_in, 16 * (7 + 2 * f))
                    sp.dma_start(relus[f][ROWS_DSA, :], trig[f, 96:128, :]).then_inc(prep_in, 16)
                sp.dma_start(ident[:], ident_d).then_inc(prep_in, 16)
                for s in range(4):
                    part = slice(32 * s, 32 * s + 32)
                    cols = slice(QUARTER * s, QUARTER * s + QUARTER)
                    sp.dma_start(rot_table[part], trig.rearrange("f p s -> p f s")[ROWS_DSA, :, cols]).then_inc(prep_in, 16)

            def load_tile(u, first):
                q0 = (u + SEL0) * P
                if not first:
                    sp.wait_ge(scored, IDX_HEADS * u)
                    sp.wait_ge(summed, IDX_HEADS * u)
                queries = proj[B_IQ:B_IQ + IDX_BLKS - 1].rearrange("b p s -> p b s")
                sp.dma_start(q_idx[:], queries[:, :, ds(q0, P)]).then_inc(tile_in, 16)
                for half in (0, IDX_DIM):
                    sp.dma_start(q_swap[half:half + NI], queries[half + NI:half + 2 * NI, :, ds(q0, P)]).then_inc(tile_in, 16)
                    sp.dma_start(q_swap[half + NI:half + 2 * NI], queries[half:half + NI, :, ds(q0, P)]).then_inc(tile_in, 16)
                tables = trig.rearrange("f p s -> p f s")
                sp.dma_start(trig_q[0:32], tables[0:32, :, ds(q0, P)]).then_inc(tile_in, 16)
                sp.dma_start(trig_q[ROWS_DSA], tables[96:128, :, ds(q0, P)]).then_inc(tile_in, 16)
                sp.dma_start(trig_q[64:128], tables[64:128, :, ds(q0, P)]).then_inc(tile_in, 16)
                sp.dma_start(iw_t[0:IDX_HEADS, :], proj[B_IK, IDX_DIM:IDX_DIM + IDX_HEADS, ds(q0, P)]).then_inc(tile_in, 16)
                sp.dma_start(causal[:], window[:, ds(SEQ - P - q0, SEQ)]).then_inc(tile_in, 16)

            def load_rotated(u):
                blocks = proj[ds(B_DQ + ROT_PER_TILE * (u - 1), ROT_PER_TILE)].rearrange("b p s -> p b s")
                for s in range(4):
                    p0 = 32 * s
                    cols = slice(QUARTER * s, QUARTER * s + QUARTER)
                    sp.dma_start(rot[p0:p0 + 32], blocks[0:32, :, cols]).then_inc(rot_in, 16)
                    sp.dma_start(rot_swap[p0:p0 + NQ], blocks[NQ:2 * NQ, :, cols]).then_inc(rot_in, 16)
                    sp.dma_start(rot_swap[p0 + NQ:p0 + 2 * NQ], blocks[0:NQ, :, cols]).then_inc(rot_in, 16)

            def store_rotated(u):
                blocks = proj[ds(B_DQ + ROT_PER_TILE * (u - 1), ROT_PER_TILE)].rearrange("b p s -> p b s")
                sp.wait_ge(rot_made, u)
                for s in range(4):
                    cols = slice(QUARTER * s, QUARTER * s + QUARTER)
                    sp.dma_start(blocks[0:32, :, cols], rot[32 * s:32 * s + 32]).then_inc(rot_stored, 16)
                sp.wait_ge(rot_stored, 64 * u)

            load_block(0, True)
            sp.dma_start(pos[:].bitcast(I32), positions.partition_broadcast(P)).then_inc(pos_in, 16)
            sp.dma_start(freq[:], inv_freq).then_inc(pos_in, 16)
            sp.dma_start(sign[:], sin_sign).then_inc(pos_in, 16)
            with sp.Fori(1, TRIG_BLKS + 1) as n:
                load_block(n)
                store_block(n - 1)
            sp.wait_ge(trig_step, 11)
            sp.dma_start(trig[0], pos[:]).then_inc(table_out, 16)
            sp.dma_start(trig[1], turns[:]).then_inc(table_out, 16)
            with sp.Fori(TRIG_BLKS + 1, IDX_BLKS) as n:
                load_block(n)
                store_block(n - 1)
            load_block(IDX_BLKS)
            store_block(IDX_BLKS - 1)
            load_keys()
            with sp.Fori(IDX_BLKS + 1, N_SEL0) as n:
                load_block(n)
                store_block(n - 1)

            def selected(u, first):
                n = N_SEL0 + SEL_BLKS * u
                load_tile(u, first)
                if not first:
                    load_rotated(u)
                load_block(n)
                if not first:
                    store_rotated(u)
                store_block(n - 1)
                with sp.Fori(1, SEL_BLKS) as j:
                    load_block(n + j)
                    store_block(n + j - 1)
                sp.wait_ge(bias_made, u + 1)
                sp.dma_start(sel_bias[u], bias_out[:]).then_inc(bias_stored, 16)

            selected(0, True)
            with sp.Fori(1, ST - SEL0) as u:
                selected(u, False)
            store_block(NBLK - 1)
            sp.wait_ge(stored, 16 * NBLK)
            sp.wait_ge(bias_stored, 16 * (ST - SEL0))

        @block.gpsimd
        def _(pool):
            pool.wait_ge(trig_step, 9)
            nc.gpsimd.memset(work[:], 0.0).then_inc(prep_set, 1)
            nc.gpsimd.memset(q_swap[:], 0.0).then_inc(prep_set, 1)
            for h in range(2):
                nc.gpsimd.memset(k_idx[h][:], 0.0).then_inc(prep_set, 1)
            nc.gpsimd.memset(iw_t[:], 0.0).then_inc(prep_set, 1)
            nc.gpsimd.memset(bias_out[:], 0.0).then_inc(prep_set, 1)

        @block.scalar
        def _(act):
            def hi_part(n, g, first=False):
                act.wait_ge(w_loaded[g], 16 * (n + 1))
                if not first:
                    if g == 0:
                        act.wait_ge(g0_used, n)
                    else:
                        act.wait_ge(half_done, 2 * n)
                nc.scalar.activation(w_hi[g][:], w_raw[g][:], ACT.Copy).then_inc(hi_made, 1)

            def evacuate(n, s, first=False):
                act.wait_ge(half_done, 2 * n + s + 1)
                if s == 0 and not first:
                    act.wait_ge(stored, 16 * n)
                nc.scalar.activation(stage[:, s * HALF:(s + 1) * HALF], acc[s][:], ACT.Copy).then_inc(evacuated, 1)

            def split_and_finish(n):
                hi_part(n, 0)
                hi_part(n, 1)
                evacuate(n - 1, 1)

            def relu_tile(u, keys, first):
                for h in range(IDX_HEADS):
                    act.wait_ge(scored, IDX_HEADS * u + h + 1)
                    if not (first and h < 2):
                        act.wait_ge(summed, IDX_HEADS * u + h - 1)
                    nc.scalar.activation(relus[h % 2][:, 0:keys], rel[h % 2][:, 0:keys],
                                         ACT.Relu).then_inc(relued, 1)

            hi_part(0, 0, True)
            hi_part(0, 1, True)
            evacuate(0, 0, True)
            for n in range(1, TRIG_BLKS + 1):
                split_and_finish(n)
                evacuate(n, 0)
                if n == TRIG_BLKS - 1:
                    act.wait_ge(trig_step, 8)
                    nc.scalar.activation(turns[:], angle[:], ACT.Sin).then_inc(sines, 1)
                    nc.scalar.activation(half_sin[:], angle[:], ACT.Sin, scale=0.5).then_inc(sines, 1)
            with act.Fori(TRIG_BLKS + 1, N_SEL0) as n:
                split_and_finish(n)
                evacuate(n, 0)

            def selected(u, keys, first):
                n = N_SEL0 + SEL_BLKS * u
                split_and_finish(n)
                if first:
                    act.wait_ge(k_ready, 2)
                relu_tile(u, keys, first)
                evacuate(n, 0)
                with act.Fori(1, SEL_BLKS) as j:
                    split_and_finish(n + j)
                    evacuate(n + j, 0)

            for u0, count, keys in GROUPS:
                if u0 == 0:
                    selected(0, keys, True)
                    u0, count = 1, count - 1
                with act.Fori(u0, u0 + count) as u:
                    selected(u, keys, False)
            evacuate(NBLK - 1, 1)

        @block.vector
        def _(dve):
            def lo_part(n, g):
                dve.wait_ge(hi_made, 2 * n + g + 1)
                nc.vector.tensor_tensor(w_lo[g][:], w_raw[g][:], w_hi[g][:].bitcast(F32),
                                        ALU.subtract).then_inc(lo_made, 1)

            def trig_tables():
                done = [0]

                def link(ins):
                    done[0] += 1
                    ins.then_inc(trig_step, 1)
                    dve.wait_ge(trig_step, done[0])

                def part(which):
                    if which == 0:
                        dve.wait_ge(pos_in, 48)
                        link(nc.vector.tensor_copy(pos[:], pos[:].bitcast(I32)))
                        link(nc.vector.tensor_scalar(angle[:], pos[:], freq[:], None, ALU.mult))
                        link(nc.vector.tensor_scalar(turns[:], angle[:], 1.0 / TWO_PI, ROUNDER, ALU.mult, ALU.add))
                        link(nc.vector.tensor_scalar(turns[:], turns[:], ROUNDER, None, ALU.subtract))
                    elif which == 1:
                        for two_pi_part in TWO_PI_PARTS:
                            link(nc.vector.scalar_tensor_tensor(angle[:], turns[:], -two_pi_part, angle[:],
                                                                ALU.mult, ALU.add))
                        link(nc.vector.tensor_scalar(angle[:], angle[:], PI_BELOW, -PI_BELOW, ALU.min, ALU.max))
                    elif which == 2:
                        dve.wait_ge(sines, 2)
                        link(nc.vector.tensor_tensor(pos[:], half_sin[:], half_sin[:], ALU.mult))
                        link(nc.vector.tensor_scalar(pos[:], pos[:], -2.0, 1.0, ALU.mult, ALU.add))
                        nc.vector.tensor_scalar(turns[:], turns[:], sign[:], None, ALU.mult).then_inc(trig_step, 1)

                return part

            def rotate_keys():
                dve.wait_ge(prep_in, 16 * 15)
                nc.vector.tensor_tensor(work[:], work[:], relus[1][:], ALU.mult).then_inc(k_step, 1)
                for h in range(2):
                    rows = slice(IDX_DIM * h, IDX_DIM * h + IDX_DIM)
                    nc.vector.tensor_tensor(k_idx[h][rows, :], k_idx[h][rows, :], relus[0][rows, :],
                                            ALU.mult).then_inc(k_step, 1)
                dve.wait_ge(k_step, 3)
                for h in range(2):
                    rows = slice(IDX_DIM * h, IDX_DIM * h + IDX_DIM)
                    nc.vector.tensor_tensor(k_idx[h][rows, :], k_idx[h][rows, :], work[rows, :],
                                            ALU.add).then_inc(k_ready, 1)

            def rotate_queries(u):
                dve.wait_ge(tile_in, 16 * TILE_DMAS * (u + 1))
                for f, q in ((0, q_idx), (1, q_swap)):
                    table = trig_q[:, f:f + 1, :].broadcast_to([P, IDX_BLKS - 1, P])
                    nc.vector.tensor_tensor(q[:], q[:], table, ALU.mult).then_inc(q_step, 1)
                dve.wait_ge(q_step, 2 * (u + 1))
                nc.vector.tensor_tensor(q_idx[:], q_idx[:], q_swap[:], ALU.add).then_inc(q_ready, 1)

            def rotate_blocks(u):
                dve.wait_ge(rot_in, 16 * 12 * u)
                for f, q in ((0, rot), (1, rot_swap)):
                    table = rot_table[:, f:f + 1, :].broadcast_to([P, ROT_PER_TILE, QUARTER])
                    nc.vector.tensor_tensor(q[:], q[:], table, ALU.mult).then_inc(rot_step, 1)
                dve.wait_ge(rot_step, 2 * u)
                nc.vector.tensor_tensor(rot[:], rot[:], rot_swap[:], ALU.add).then_inc(rot_made, 1)

            def sum_heads(u, keys):
                dve.wait_ge(iw_turned, u + 1)
                nc.vector.tensor_scalar(iw[:], iw_ps[:, 0:IDX_HEADS], IDX_DIM ** -0.5 * IDX_HEADS ** -0.5,
                                        None, ALU.mult).then_inc(iw_ready, 1)
                dve.wait_ge(iw_ready, u + 1)
                for h in range(IDX_HEADS):
                    dve.wait_ge(relued, IDX_HEADS * u + h + 1)
                    if h:
                        dve.wait_ge(summed, IDX_HEADS * u + h)
                    so_far = work if h else causal
                    nc.vector.scalar_tensor_tensor(work[:, 0:keys], relus[h % 2][:, 0:keys], iw[:, h:h + 1],
                                                   so_far[:, 0:keys], ALU.mult, ALU.add).then_inc(summed, 1)

            def rounds(m, keys):
                for r in range(m):
                    nc.vector.max(best[:], work[:, 0:keys]).then_inc(topk_step, 1)
                    dve.wait_ge(topk_step, 2 * r + 1)
                    nc.vector.match_replace(work[:, 0:keys], best[:], work[:, 0:keys], TAKEN).then_inc(topk_step, 1)
                    dve.wait_ge(topk_step, 2 * r + 2)
                dve.sem_clear(topk_step)

            lo_part(0, 0)
            lo_part(0, 1)
            trig_ops = trig_tables()
            for n in range(1, TRIG_BLKS + 1):
                lo_part(n, 0)
                lo_part(n, 1)
                trig_ops(n - 1)
            with dve.Fori(TRIG_BLKS + 1, IDX_BLKS + 1) as n:
                lo_part(n, 0)
                lo_part(n, 1)
            rotate_keys()
            with dve.Fori(IDX_BLKS + 1, N_SEL0) as n:
                lo_part(n, 0)
                lo_part(n, 1)

            def selected(u, keys, first):
                n = N_SEL0 + SEL_BLKS * u
                rotate_queries(u)
                if not first:
                    rotate_blocks(u)
                lo_part(n, 0)
                sum_heads(u, keys)
                dve.wait_ge(summed, IDX_HEADS * (u + 1))
                lo_part(n, 1)
                rounds(ROUNDS_PER_BLK, keys)
                with dve.Fori(1, SEL_BLKS) as j:
                    lo_part(n + j, 0)
                    rounds(ROUNDS_PER_BLK // 2, keys)
                    lo_part(n + j, 1)
                    rounds(ROUNDS_PER_BLK // 2, keys)
                if not first:
                    dve.wait_ge(bias_stored, 16 * u)
                nc.vector.tensor_scalar(bias_out[:, 0:keys], work[:, 0:keys], 0.5 * TAKEN, MASKED,
                                        ALU.is_gt, ALU.mult).then_inc(bias_made, 1)

            for u0, count, keys in GROUPS:
                if u0 == 0:
                    selected(0, keys, True)
                    u0, count = 1, count - 1
                with dve.Fori(u0, u0 + count) as u:
                    selected(u, keys, False)

        @block.tensor
        def _(pe):
            def project_block(n, first=False):
                for s in range(2):
                    cols = slice(s * HALF, (s + 1) * HALF)
                    if not first:
                        pe.wait_ge(evacuated, 2 * n + s - 1)
                    for g in range(GRAN):
                        if s == 0:
                            pe.wait_ge(lo_made, 2 * n + g + 1)
                        for k in range(KG):
                            kk = g * KG + k
                            nc.tensor.matmul(acc[s][:], w_hi[g][:, k, :], y_hi[:, kk, cols],
                                             start=kk == 0, stop=False)
                            nc.tensor.matmul(acc[s][:], w_hi[g][:, k, :], y_lo[:, kk, cols],
                                             start=False, stop=False)
                            mm = nc.tensor.matmul(acc[s][:], w_lo[g][:, k, :], y_hi[:, kk, cols],
                                                  start=False, stop=kk == KT - 1)
                        if g == 0 and s == 1:
                            mm.then_inc(g0_used, 1)
                    mm.then_inc(half_done, 1)

            def score_tile(u, keys, first):
                pe.wait_ge(q_ready, u + 1)
                if first:
                    pe.wait_ge(k_ready, 2)
                else:
                    pe.wait_ge(iw_ready, u)
                nc.tensor.transpose(iw_ps[:, 0:P], iw_t[:], ident[:]).then_inc(iw_turned, 1)
                for h in range(IDX_HEADS):
                    if not (first and h < 2):
                        pe.wait_ge(relued, IDX_HEADS * u + h - 1)
                    for c in range(0, keys, HALF):
                        mm = nc.tensor.matmul(rel[h % 2][:, c:c + HALF], q_idx[:, h // 2, :],
                                              k_idx[h % 2][:, c:c + HALF], start=True, stop=True)
                    mm.then_inc(scored, 1)

            project_block(0, True)
            with pe.Fori(1, N_SEL0) as n:
                project_block(n)

            def selected(u, keys, first):
                n = N_SEL0 + SEL_BLKS * u
                score_tile(u, keys, first)
                with pe.Fori(0, SEL_BLKS) as j:
                    project_block(n + j)

            for u0, count, keys in GROUPS:
                if u0 == 0:
                    selected(0, keys, True)
                    u0, count = 1, count - 1
                with pe.Fori(u0, u0 + count) as u:
                    selected(u, keys, False)


LAG = 3
HEADS_PER_PASS = 2
UNITS = HEADS_PER_PASS * ST
RING = 8
SCALE = HEAD_DIM ** -0.5
CH = HALF // P


def events_of_pass(pe):
    ev = []
    for u in range(UNITS):
        ev.append((u, 1 if pe else 5, "scores", u))
        ev.append((u + 2, 0, "norm", u))
        ev.append((u + LAG, 2, "turn", u))
    for b in range(HEADS_PER_PASS):
        ev.append((ST * b + LAG - 1, 4, "turn_v", b))
        for c in range(2):
            last = ST * b + CH * c + CH - 1
            ev.append((last + LAG + 1, 3 if pe else 6, "values", (b, c)))
            ev.append((last + LAG + 4 - c, 7, "sumsq", (b, c)))
            ev.append((ST * b + ST - 1 + LAG + 5 + 2 * c, 9, "spread", (b, c)))
        ev.append((ST * b + ST - 1 + LAG + 3, 8, "root", b))
    return sorted(ev, key=lambda e: (e[0] % UNITS, e[1], -e[0]))


EVENTS = {pe: events_of_pass(pe) for pe in (False, True)}
IN_TIME = sorted(EVENTS[True], key=lambda e: e[:2])


def groups_of(kind, arg):
    if kind == "turn_v":
        return [0, CH]
    return [0, CH] if arg % ST >= CH else [0]


GROUP_NO = {}
for _, _, kind_, arg_ in IN_TIME:
    if kind_ in ("turn", "turn_v"):
        for j0_ in groups_of(kind_, arg_):
            GROUP_NO[kind_, arg_, j0_] = len(GROUP_NO)
GROUPS_PER_PASS = len(GROUP_NO)
assert GROUPS_PER_PASS % 2 == 0
STAT_NO = {(kind_, arg_): n_ for n_, (_, _, kind_, arg_) in
           enumerate(e for e in IN_TIME if e[2] in ("sumsq", "spread"))}
STATS = len(STAT_NO)
ROOT_STEPS = 10


def in_order(p, first, pe=False):
    for step, _, kind, arg in EVENTS[pe]:
        if step < UNITS:
            yield kind, p, arg
        elif not first:
            yield kind, p - 1, arg


def left_over(p, pe=False):
    for step, _, kind, arg in EVENTS[pe]:
        if step >= UNITS:
            yield kind, p, arg


def attend(nc, sem, kind_of_heads, b_q, b_k, b_v, b_g, proj, mixed_t, head_g, ident_d, strict_d, window,
           sel_bias):
    sb_heads = kind_of_heads == "sb"
    n_pass = 4
    k_ = kind_of_heads
    half_groups = GROUPS_PER_PASS // 2
    with ExitStack() as ctx:
        sb = lambda name, shape, dt=F32: ctx.enter_context(nc.sbuf_tensor(f"{k_}_{name}", shape, dt))
        ps = lambda name, shape: ctx.enter_context(nc.psum_tensor(f"{k_}_{name}", shape, F32))
        sm = lambda name: sem(f"{k_}_{name}")
        both = range(HEADS_PER_PASS)
        q = [sb(f"q{b}", [P, SEQ]) for b in both]
        k = [sb(f"k{b}", [P, SEQ]) for b in both]
        v_t = [sb(f"v_t{b}", [P, SEQ]) for b in both]
        gate = [sb(f"gate{b}", [P, SEQ]) for b in both]
        v = [sb(f"v{b}", [P, ST, P]) for b in both]
        w = [sb(f"w{r}", [P, SEQ]) for r in range(RING)]
        stay = [sb(f"stay{r}", [P, SEQ]) for r in range(RING)] if sb_heads else None
        w_t = [sb(f"w_t{c}", [P, ST, HALF]) for c in range(2)]
        o = [sb(f"o{b}", [P, SEQ]) for b in both]
        var = [sb(f"var{b}", [P, ST]) for b in both]
        rstd = [sb(f"rstd{b}", [P, ST]) for b in both]
        newton = sb("newton", [P, ST])
        silu = [sb(f"silu{b}", [P, SEQ]) for b in both]
        squares = [sb(f"squares{c}", [P, HALF]) for c in range(2)]
        ones = sb("ones", [P, 1])
        ident = sb("ident", [P, P])
        g_sb = sb("g", [P, 8])
        if sb_heads:
            ident16 = sb("ident16", [P, P], BF16)
            strict = sb("strict", [P, P], BF16)
        else:
            bias = sb("bias", [P, ST, SEQ], BF16)
            low = sb("low", [P, RING])
            den = sb("den", [P, RING])
            spare = sb("spare", [P, RING])
            inv = sb("inv", [P, RING])
        sc = [ps(f"sc{r}", [P, SEQ]) for r in range(2)]
        tr = [ps(f"tr{r}", [P, CH, P]) for r in range(2)]
        pv = ps("pv", [P, HALF])
        ss = ps("ss", [P, HALF])

        qkv_in = [sm(f"qkv_in{b}") for b in both]
        gate_in = [sm(f"gate_in{b}") for b in both]
        consts_in, set_up = sm("consts_in"), sm("set_up")
        scored, sc_read, scanned, w_ready = sm("scored"), sm("sc_read"), sm("scanned"), sm("w_ready")
        converted = sm("converted")
        exped, inverted = sm("exped"), sm("inverted")
        turned = [sm(f"turned{r}") for r in range(2)]
        copied = [sm(f"copied{r}") for r in range(2)]
        pv_done, pv_read, squared, ss_done, ss_read = sm("pv_done"), sm("pv_read"), sm("squared"), sm("ss_done"), sm("ss_read")
        sigmoided, root_step, rooted, gated = sm("sigmoided"), sm("root_step"), sm("rooted"), sm("gated")
        fin_step, mixed, stored = sm("fin_step"), sm("mixed"), [sm(f"stored{b}") for b in both]
        block = ctx.enter_context(nc.Block())
        QKV_DMAS = 3
        CONST_DMAS = 4 if sb_heads else 2 + ST

        def wait(eng, s, value):
            if not (isinstance(value, int) and value <= 0):
                eng.wait_ge(s, value)

        def group(p, kind, arg, j0):
            no = GROUP_NO[kind, arg, j0]
            return no % 2, half_groups * p + no // 2 + 1

        def tiles_in(kind, arg, j0):
            return CH if kind == "turn_v" else min(CH, arg % ST + 1 - j0)

        def wait_slot_free(eng, p, u):
            pu, uu = (p, u - RING) if u >= RING else (p - 1, u - RING + UNITS)
            bank, done = group(pu, "turn", uu, groups_of("turn", uu)[-1])
            wait(eng, turned[bank], done)

        def chunk_no(p, b, c):
            return 2 * HEADS_PER_PASS * p + 2 * b + c

        def copy_group(eng, op, bank, p, kind, arg):
            for j0 in groups_of(kind, arg):
                at, done = group(p, kind, arg, j0)
                if at != bank:
                    continue
                n = tiles_in(kind, arg, j0)
                wait(eng, turned[bank], done)
                if kind == "turn_v":
                    dst = v[arg][:, j0:j0 + n, :]
                else:
                    chunk = arg // CH
                    wait(eng, pv_done, 2 * HEADS_PER_PASS * p + chunk - 1)
                    c0 = arg % CH * P
                    dst = w_t[chunk % 2][:, j0:j0 + n, c0:c0 + P]
                op(dst, tr[bank][:, 0:n, :]).then_inc(copied[bank], 1)

        @block.sync
        def _(sp):
            sp.dma_start(ident[:], ident_d).then_inc(consts_in, 16)
            sp.dma_start(g_sb[:], head_g).then_inc(consts_in, 16)
            if sb_heads:
                sp.dma_start(squares[0][:, 0:P], ident_d).then_inc(consts_in, 16)
                sp.dma_start(squares[1][:, 0:P], strict_d).then_inc(consts_in, 16)
            else:
                for i in range(ST):
                    keys = (i + 1) * P
                    if i < SEL0:
                        sp.dma_start(squares[i][:, 0:keys], window[:, SEQ - keys:SEQ]).then_inc(consts_in, 16)
                    else:
                        sp.dma_start(bias[:, i, 0:keys], sel_bias[i - SEL0, :, 0:keys]).then_inc(consts_in, 16)

            def load_head(p, kv, b, first):
                n = HEADS_PER_PASS * p + b
                if not first:
                    sp.wait_ge(scored, UNITS * (p - 1) + ST * (b + 1))
                sp.dma_start(q[b][:], proj[b_q + n]).then_inc(qkv_in[b], 16)
                sp.dma_start(k[b][:], proj[b_k + kv]).then_inc(qkv_in[b], 16)
                sp.dma_start(v_t[b][:], proj[b_v + kv]).then_inc(qkv_in[b], 16)
                if not first:
                    sp.wait_ge(mixed, 2 * n - 2)
                    sp.dma_start(mixed_t[n - 2], o[b][:]).then_inc(stored[b], 16)
                sp.dma_start(gate[b][:], proj[b_g + n]).then_inc(gate_in[b], 16)

            def load_pass(p, g, first=False):
                for b in both:
                    load_head(p, HEADS_PER_PASS * p + b if sb_heads else g, b, first)

            load_pass(0, 0, True)
            if sb_heads:
                with sp.Fori(1, n_pass) as p:
                    load_pass(p, None)
            else:
                load_pass(1, 0)
                with sp.Fori(2, n_pass) as p:
                    load_pass(p, 1)
            for b in both:
                n = HEADS_PER_PASS * n_pass + b
                sp.wait_ge(mixed, 2 * n - 2)
                sp.dma_start(mixed_t[n - 2], o[b][:]).then_inc(stored[b], 16)
            for b in both:
                sp.wait_ge(stored[b], 16 * n_pass)

        def pool_events(pool, events):
            for kind, p, arg in events:
                if kind == "scores" and sb_heads:
                    r, n = arg % RING, (arg % ST + 1) * P
                    pool.wait_ge(scanned, UNITS * p + arg + 1)
                    nc.gpsimd.tensor_tensor(w[r][:, 0:n - 1], w[r][:, 0:n - 1], stay[r][:, 1:n],
                                            ALU.mult).then_inc(w_ready, 1)
                elif kind == "values":
                    b, c = arg
                    no = chunk_no(p, b, c)
                    part = o[b][:, c * HALF:(c + 1) * HALF]
                    pool.wait_ge(pv_read, no + 1)
                    wait(pool, ss_done, no - 1)
                    nc.gpsimd.tensor_tensor(squares[c][:], part, part, ALU.mult).then_inc(squared, 1)
                elif kind == "root":
                    pool.wait_ge(sigmoided, HEADS_PER_PASS * p + arg + 1)
                    nc.gpsimd.tensor_tensor(silu[arg][:], silu[arg][:], gate[arg][:], ALU.mult).then_inc(gated, 1)

        @block.gpsimd
        def _(pool):
            nc.gpsimd.memset(ones[:], 1.0).then_inc(set_up, 1)
            pool.wait_ge(converted, 2)
            pool_events(pool, in_order(0, True))
            with pool.Fori(1, n_pass) as p:
                pool_events(pool, in_order(p, False))
            pool_events(pool, left_over(n_pass - 1))

        @block.scalar
        def _(act):
            def copy(dst, src):
                return nc.scalar.activation(dst, src, ACT.Copy)

            def run(events):
                for kind, p, arg in events:
                    if kind == "scores":
                        r, n = arg % RING, (arg % ST + 1) * P
                        unit = UNITS * p + arg
                        if sb_heads:
                            act.wait_ge(scored, unit + 1)
                            wait_slot_free(act, p, arg)
                            nc.scalar.activation(w[r][:, 0:n], sc[arg % 2][:, 0:n], ACT.Sigmoid, scale=SCALE)
                            nc.scalar.activation(stay[r][:, 0:n], sc[arg % 2][:, 0:n], ACT.Sigmoid,
                                                 scale=-SCALE).then_inc(sc_read, 1)
                        else:
                            act.wait_ge(sc_read, unit + 1)
                            nc.scalar.activation(w[r][:, 0:n], w[r][:, 0:n], ACT.Exp, bias=low[:, r:r + 1],
                                                 scale=-1.0, accum_out=den[:, r:r + 1]).then_inc(exped, 1)
                    elif kind in ("turn", "turn_v"):
                        copy_group(act, copy, 0, p, kind, arg)
                    elif kind == "values":
                        b, c = arg
                        no = chunk_no(p, b, c)
                        act.wait_ge(pv_done, no + 1)
                        if c == 0:
                            wait(act, stored[b], 16 * p)
                        copy(o[b][:, c * HALF:(c + 1) * HALF], pv[:]).then_inc(pv_read, 1)
                    elif kind == "root":
                        b = arg
                        act.wait_ge(gate_in[b], 16 * (p + 1))
                        wait(act, mixed, 2 * (HEADS_PER_PASS * (p - 1) + b + 1))
                        nc.scalar.activation(silu[b][:], gate[b][:], ACT.Sigmoid).then_inc(sigmoided, 1)

            run(in_order(0, True))
            with act.Fori(1, n_pass) as p:
                run(in_order(p, False))
            run(left_over(n_pass - 1))

        @block.vector
        def _(dve):
            def run(events):
                for kind, p, arg in events:
                    r = arg % RING if kind in ("scores", "norm") else None
                    if kind == "scores":
                        n = (arg % ST + 1) * P
                        unit = UNITS * p + arg
                        if sb_heads:
                            dve.wait_ge(sc_read, unit + 1)
                            back = stay[r][:, 0:n][:, ::-1]
                            nc.vector.tensor_tensor_scan(back, back, back, 1.0, ALU.mult, ALU.bypass).then_inc(scanned, 1)
                        else:
                            dve.wait_ge(scored, unit + 1)
                            wait_slot_free(dve, p, arg)
                            nc.vector.memset(spare[:, r:r + 1], 0.0)
                            nc.vector.tensor_tensor_reduce(
                                out=w[r][:, 0:n], in0=sc[arg % 2][:, 0:n], in1=bias[:, arg % ST, 0:n], scale=-SCALE,
                                scalar=3.0e38, op0=ALU.add, op1=ALU.min, accum_out=low[:, r:r + 1]).then_inc(sc_read, 1)
                    elif kind == "norm" and not sb_heads:
                        n = (arg % ST + 1) * P
                        unit = UNITS * p + arg
                        dve.wait_ge(exped, unit + 1)
                        nc.vector.reciprocal(inv[:, r:r + 1], den[:, r:r + 1]).then_inc(inverted, 1)
                        dve.wait_ge(inverted, unit + 1)
                        nc.vector.tensor_scalar(w[r][:, 0:n], w[r][:, 0:n], inv[:, r:r + 1], None,
                                                ALU.mult).then_inc(w_ready, 1)
                    elif kind in ("turn", "turn_v"):
                        copy_group(dve, nc.vector.tensor_copy, 1, p, kind, arg)
                    elif kind == "sumsq":
                        b, c = arg
                        use = STATS * p + STAT_NO[kind, arg]
                        dve.wait_ge(ss_done, use + 1)
                        nc.vector.tensor_scalar(var[b][:, CH * c:CH * c + CH], ss[:, 0:CH], 1.0 / HEAD_DIM, EPS,
                                                ALU.mult, ALU.add).then_inc(ss_read, 1)
                    elif kind == "root":
                        root(p, arg)
                    elif kind == "spread":
                        b, c = arg
                        use = STATS * p + STAT_NO[kind, arg]
                        n = chunk_no(p, b, c)
                        part = o[b][:, c * HALF:(c + 1) * HALF]
                        dve.wait_ge(ss_done, use + 1)
                        nc.vector.scalar_tensor_tensor(part, part, g_sb[:, ds(HEADS_PER_PASS * p + b, 1)], ss[:],
                                                       ALU.mult, ALU.mult).then_inc(ss_read, 1)
                        dve.wait_ge(ss_read, use + 1)
                        dve.wait_ge(gated, HEADS_PER_PASS * p + b + 1)
                        nc.vector.tensor_tensor(part, part, silu[b][:, c * HALF:(c + 1) * HALF],
                                                ALU.mult).then_inc(mixed, 1)

            def root(p, b):
                n = HEADS_PER_PASS * p + b
                x, r, t = var[b][:], rstd[b][:], newton[:]
                done = [ROOT_STEPS * n]

                def link(ins):
                    done[0] = done[0] + 1
                    ins.then_inc(root_step, 1)
                    dve.wait_ge(root_step, done[0])

                dve.wait_ge(ss_read, STATS * p + STAT_NO["sumsq", (b, 1)] + 1)
                link(nc.vector.tensor_scalar(t.bitcast(I32), x.bitcast(I32), 1, None, ALU.logical_shift_right))
                link(nc.vector.tensor_scalar(r.bitcast(I32), t.bitcast(I32), -1.0, float(0x5f3759df), ALU.mult, ALU.add))
                for step in range(3):
                    link(nc.vector.scalar_tensor_tensor(t, r, -0.5, r, ALU.mult, ALU.mult))
                    link(nc.vector.tensor_tensor(t, t, x, ALU.mult))
                    last = nc.vector.scalar_tensor_tensor(r, t, 1.5, r, ALU.add, ALU.mult)
                    if step < 2:
                        link(last)
                last.then_inc(rooted, 1)

            dve.wait_ge(consts_in, 16 * CONST_DMAS)
            if sb_heads:
                nc.vector.tensor_copy(ident16[:], squares[0][:, 0:P]).then_inc(converted, 1)
                nc.vector.tensor_copy(strict[:], squares[1][:, 0:P]).then_inc(converted, 1)
            else:
                for i in range(SEL0):
                    keys = (i + 1) * P
                    nc.vector.tensor_copy(bias[:, i, 0:keys], squares[i][:, 0:keys]).then_inc(converted, 1)
                dve.wait_ge(converted, 2)
            run(in_order(0, True))
            with dve.Fori(1, n_pass) as p:
                run(in_order(p, False))
            run(left_over(n_pass - 1))

        @block.tensor
        def _(pe):
            def run(events):
                for kind, p, arg in events:
                    if kind == "scores":
                        b, i = divmod(arg, ST)
                        unit = UNITS * p + arg
                        if i == 0:
                            pe.wait_ge(qkv_in[b], 16 * QKV_DMAS * (p + 1))
                        wait(pe, sc_read, unit - 1)
                        keys = (i + 1) * P
                        for c in range(0, keys, HALF):
                            end = min(c + HALF, keys)
                            masked = sb_heads and end == keys
                            mm = nc.tensor.matmul(sc[arg % 2][:, c:end], q[b][:, i * P:(i + 1) * P], k[b][:, c:end],
                                                  start=True, stop=not masked)
                            if masked:
                                mm = nc.tensor.matmul(sc[arg % 2][:, i * P:keys], ident16[:], strict[:],
                                                      start=False, stop=True)
                        mm.then_inc(scored, 1)
                    elif kind in ("turn", "turn_v"):
                        if kind == "turn":
                            src = w[arg % RING]
                            pe.wait_ge(w_ready, UNITS * p + arg + 1)
                        else:
                            src = v_t[arg]
                            pe.wait_ge(qkv_in[arg], 16 * QKV_DMAS * (p + 1))
                        for j0 in groups_of(kind, arg):
                            bank, done = group(p, kind, arg, j0)
                            wait(pe, copied[bank], done - 1)
                            for j in range(j0, j0 + tiles_in(kind, arg, j0)):
                                mm = nc.tensor.transpose(tr[bank][:, j - j0, :], src[:, j * P:(j + 1) * P], ident[:])
                            mm.then_inc(turned[bank], 1)
                    elif kind == "values":
                        b, c = arg
                        last = ST * b + CH * c + CH - 1
                        newest = GROUP_NO["turn", last, groups_of("turn", last)[-1]]
                        for no in (newest, newest - 1):
                            pe.wait_ge(copied[no % 2], half_groups * p + no // 2 + 1)
                        wait(pe, pv_read, chunk_no(p, b, c))
                        tiles = CH * c + CH
                        for j in range(tiles):
                            c0 = max(0, j - CH * c) * P
                            mm = nc.tensor.matmul(pv[:, c0:HALF], v[b][:, j, :], w_t[c][:, j, c0:HALF],
                                                  start=j == 0, stop=j == tiles - 1)
                        mm.then_inc(pv_done, 1)
                    elif kind == "sumsq":
                        b, c = arg
                        pe.wait_ge(squared, chunk_no(p, b, c) + 1)
                        wait(pe, ss_read, STATS * p + STAT_NO[kind, arg])
                        for j in range(CH):
                            mm = nc.tensor.matmul(ss[:, j:j + 1], squares[c][:, j * P:(j + 1) * P], ones[:],
                                                  start=True, stop=True)
                        mm.then_inc(ss_done, 1)
                    elif kind == "spread":
                        b, c = arg
                        pe.wait_ge(rooted, HEADS_PER_PASS * p + b + 1)
                        wait(pe, ss_read, STATS * p + STAT_NO[kind, arg])
                        for j in range(CH):
                            i = CH * c + j
                            mm = nc.tensor.matmul(ss[:, j * P:(j + 1) * P], rstd[b][:, i:i + 1].broadcast_to([P, P]),
                                                  ident[:], start=True, stop=True)
                        mm.then_inc(ss_done, 1)

            pe.wait_ge(set_up, 1)
            pe.wait_ge(consts_in, 16 * CONST_DMAS)
            pe.wait_ge(converted, 2)
            run(in_order(0, True, pe=True))
            with pe.Fori(1, n_pass) as p:
                run(in_order(p, False, pe=True))
            run(left_over(n_pass - 1, pe=True))


def output(nc, sem, mixed_t, w_out, x, final_g, out):
    NC = D_MODEL // HALF
    HT = ST // 2
    WR = 4
    RAW = 4
    with ExitStack() as ctx:
        sb = lambda name, shape, dt=F32: ctx.enter_context(nc.sbuf_tensor(name, shape, dt))
        m_raw = sb("m_raw", [P, KT, HALF])
        m_hi = sb("m_hi", [P, KT, HALF], F32R)
        m_lo = sb("m_lo", [P, KT, HALF], F32R)
        w_raw = [sb(f"wo_raw{r}", [P, HALF]) for r in range(WR)]
        w_hi = [sb(f"wo_hi{r}", [P, HALF], F32R) for r in range(WR)]
        w_lo = [sb(f"wo_lo{r}", [P, HALF], F32R) for r in range(WR)]
        x2 = sb("x2", [P, HT, D_MODEL])
        g_sb = sb("final_g_sb", [P, D_MODEL])
        squares = sb("squares_o", [P, D_MODEL], BF16)
        eps = sb("eps_o", [P, 1])
        stat = [sb(f"stat{t}", [P, 8]) for t in range(HT)]
        acc = [ctx.enter_context(nc.psum_tensor(f"oacc{t}", [P, HALF], F32)) for t in range(HT)]
        m_in = [[sem(f"m_in{h}_{k}") for k in range(KT // RAW)] for h in range(2)]
        x_in, g_in, eps_set = sem("x_in"), sem("fg_in"), sem("eps_o_set")
        w_in = [sem(f"wo_in{r}") for r in range(WR)]
        m_hi_made, m_lo_made, w_hi_made, w_lo_made = sem("m_hi_made"), sem("m_lo_made"), sem("wo_hi_made"), sem("wo_lo_made")
        k_done, added = sem("k_done"), sem("added")
        summed, rooted, scaled, fin_step, stored = sem("o_summed"), sem("o_rooted"), sem("o_scaled"), sem("o_fin_step"), sem("o_stored")
        block = ctx.enter_context(nc.Block())

        def load_m_tiles(eng, h, k):
            eng.dma_start(m_raw[:, k:k + RAW, :],
                          mixed_t[k:k + RAW, :, h * HALF:(h + 1) * HALF].rearrange("k p s -> p k s")).then_inc(m_in[h][k // RAW], 16)

        @block.sync
        def _(sp):
            def load_w(it, c):
                for k in range(KT):
                    sp.wait_ge(w_lo_made, KT * it + k - WR + 1)
                    sp.dma_start(w_raw[k % WR][:], w_out[c, k]).then_inc(w_in[k % WR], 16)

            for k in range(0, KT, RAW):
                load_m_tiles(sp, 0, k)
                for kk in range(k, k + RAW):
                    if kk >= WR:
                        sp.wait_ge(w_lo_made, kk - WR + 1)
                    sp.dma_start(w_raw[kk % WR][:], w_out[0, kk]).then_inc(w_in[kk % WR], 16)
            with sp.Fori(1, NC) as c:
                load_w(c, c)
            load_w(NC, 0)
            with sp.Fori(1, NC) as c:
                load_w(NC + c, c)

        @block.gpsimd
        def _(pool):
            nc.gpsimd.memset(eps[:], EPS).then_inc(eps_set, 1)

            def load_x(h):
                if h:
                    pool.wait_ge(stored, 16 * HT)
                for t in range(HT):
                    pool.dma_start(x2[:, t, :], x[(HT * h + t) * P:(HT * h + t + 1) * P, :]).then_inc(x_in, 16)

            def store(h):
                for t in range(HT):
                    pool.wait_ge(scaled, HT * h + t + 1)
                    pool.dma_start(out[(HT * h + t) * P:(HT * h + t + 1) * P, :], x2[:, t, :]).then_inc(stored, 16)

            pool.wait_ge(w_lo_made, KT // 2)
            load_x(0)
            pool.dma_start(g_sb[:], final_g.partition_broadcast(P)).then_inc(g_in, 16)
            pool.wait_ge(m_lo_made, KT)
            for k in range(0, KT, RAW):
                load_m_tiles(pool, 1, k)
            store(0)
            load_x(1)
            store(1)
            pool.wait_ge(stored, 16 * ST)

        @block.scalar
        def _(act):
            act.wait_ge(eps_set, 1)

            def m_part(h, k):
                if k % RAW == 0:
                    act.wait_ge(m_in[h][k // RAW], 16)
                if h:
                    act.wait_ge(k_done, KT * (NC - 1) + k + 1)
                nc.scalar.activation(m_hi[:, k, :], m_raw[:, k, :], ACT.Copy).then_inc(m_hi_made, 1)

            def w_part(it, k, first=False):
                r = k % WR
                act.wait_ge(w_in[r], 16 * ((KT // WR) * it + k // WR + 1))
                if not (first and k < WR):
                    act.wait_ge(k_done, KT * it + k - WR + 1)
                nc.scalar.activation(w_hi[r][:], w_raw[r][:], ACT.Copy).then_inc(w_hi_made, 1)

            def norms(h):
                for t in range(HT):
                    act.wait_ge(added, HT * (NC - 1 + NC * h) + t + 1)
                    nc.scalar.activation(squares[:], x2[:, t, :], ACT.Square,
                                         accum_out=stat[t][:, 0:1]).then_inc(summed, 1)
                    act.wait_ge(summed, HT * h + t + 1)
                    nc.scalar.activation(stat[t][:, 1:2], stat[t][:, 0:1], ACT.Sqrt, bias=eps[:],
                                         scale=1.0 / D_MODEL).then_inc(rooted, 1)

            for h in range(2):
                for k in range(KT):
                    m_part(h, k)
                    w_part(NC * h, k, h == 0)
                if h:
                    norms(0)
                with act.Fori(1, NC) as c:
                    for k in range(KT):
                        w_part(NC * h + c, k)
            norms(1)

        @block.vector
        def _(dve):
            def m_part(h, k):
                dve.wait_ge(m_hi_made, KT * h + k + 1)
                nc.vector.tensor_tensor(m_lo[:, k, :], m_raw[:, k, :], m_hi[:, k, :].bitcast(F32),
                                        ALU.subtract).then_inc(m_lo_made, 1)

            def w_part(it, k):
                r = k % WR
                dve.wait_ge(w_hi_made, KT * it + k + 1)
                nc.vector.tensor_tensor(w_lo[r][:], w_raw[r][:], w_hi[r][:].bitcast(F32),
                                        ALU.subtract).then_inc(w_lo_made, 1)

            def add(it, h, c):
                dve.wait_ge(x_in, 16 * HT * (h + 1))
                dve.wait_ge(k_done, KT * (it + 1))
                for t in range(HT):
                    part = x2[:, t, ds(c * HALF, HALF)]
                    nc.vector.tensor_tensor(part, acc[t][:], part, ALU.add).then_inc(added, 1)

            def norms(h):
                dve.wait_ge(g_in, 16)
                for t in range(HT):
                    s = stat[t]
                    n = 5 * (HT * h + t)
                    dve.wait_ge(rooted, HT * h + t + 1)
                    nc.vector.reciprocal(s[:, 2:3], s[:, 1:2]).then_inc(fin_step, 1)
                    nc.vector.tensor_scalar(s[:, 3:4], s[:, 0:1], 1.0 / D_MODEL, EPS, ALU.mult, ALU.add).then_inc(fin_step, 1)
                    dve.wait_ge(fin_step, n + 2)
                    nc.vector.tensor_scalar(s[:, 4:5], s[:, 2:3], s[:, 2:3], s[:, 3:4], ALU.mult, ALU.mult).then_inc(fin_step, 1)
                    dve.wait_ge(fin_step, n + 3)
                    nc.vector.tensor_scalar(s[:, 5:6], s[:, 4:5], -0.5, 1.5, ALU.mult, ALU.add).then_inc(fin_step, 1)
                    dve.wait_ge(fin_step, n + 4)
                    nc.vector.tensor_tensor(s[:, 6:7], s[:, 5:6], s[:, 2:3], ALU.mult).then_inc(fin_step, 1)
                    dve.wait_ge(fin_step, n + 5)
                    nc.vector.scalar_tensor_tensor(x2[:, t, :], x2[:, t, :], s[:, 6:7], g_sb[:],
                                                   ALU.mult, ALU.mult).then_inc(scaled, 1)

            for h in range(2):
                for k in range(KT):
                    m_part(h, k)
                    w_part(NC * h, k)
                    if h and k == WR - 1:
                        add(NC - 1, 0, NC - 1)
                if h:
                    norms(0)
                with dve.Fori(1, NC) as c:
                    for k in range(WR):
                        w_part(NC * h + c, k)
                    add(NC * h + c - 1, h, c - 1)
                    for k in range(WR, KT):
                        w_part(NC * h + c, k)
            add(2 * NC - 1, 1, NC - 1)
            norms(1)

        @block.tensor
        def _(pe):
            def chunk(it, h, c0, first=False):
                for k in range(KT):
                    r = k % WR
                    pe.wait_ge(w_lo_made, KT * it + k + 1)
                    if c0:
                        pe.wait_ge(m_lo_made, KT * h + k + 1)
                    for t in range(HT):
                        rows = slice(t * P, (t + 1) * P)
                        if k == 0 and not first:
                            pe.wait_ge(added, HT * (it - 1) + t + 1)
                        nc.tensor.matmul(acc[t][:], m_hi[:, k, rows], w_hi[r][:], start=k == 0, stop=False)
                        nc.tensor.matmul(acc[t][:], m_hi[:, k, rows], w_lo[r][:], start=False, stop=False)
                        mm = nc.tensor.matmul(acc[t][:], m_lo[:, k, rows], w_hi[r][:], start=False, stop=k == KT - 1)
                    mm.then_inc(k_done, 1)

            for h in range(2):
                chunk(NC * h, h, True, h == 0)
                with pe.Fori(1, NC) as c:
                    chunk(NC * h + c, h, False)


def hybrid_block(nc, x, positions, norm_g, w_in, head_g, w_out, final_g, inv_freq, sin_sign, ident, strict,
                 window, out):
    proj = nc.dram_tensor("proj", [NBLK, P, SEQ], F32, kind="Internal").ap()
    trig = nc.dram_tensor("trig", [2, P, SEQ], F32, kind="Internal").ap()
    sel_bias = nc.dram_tensor("sel_bias", [ST - SEL0, P, SEQ], BF16, kind="Internal").ap()
    mixed_t = nc.dram_tensor("mixed_t", [KT, P, SEQ], F32, kind="Internal").ap()
    with ExitStack() as ctx:
        sem = lambda name: ctx.enter_context(nc.semaphore(name))
        with ExitStack() as held:
            y_hi = held.enter_context(nc.sbuf_tensor("y_hi", [P, KT, SEQ], F32R))
            y_lo = held.enter_context(nc.sbuf_tensor("y_lo", [P, KT, SEQ], F32R))
            normalise(nc, sem, x, norm_g, ident, y_hi, y_lo)
            project(nc, sem, w_in, positions, inv_freq, sin_sign, trig, window, ident, y_hi, y_lo, proj, sel_bias)
        attend(nc, sem, "sb", B_SBQ, B_SBK, B_SBV, B_SBG, proj, mixed_t[0:SB_HEADS], head_g[0], ident, strict,
               window, sel_bias)
        attend(nc, sem, "dsa", B_DQ, B_DK, B_DV, B_DG, proj, mixed_t[SB_HEADS:KT], head_g[1], ident, strict,
               window, sel_bias)
        output(nc, sem, mixed_t, w_out, x, final_g, out)


def shape_constants():
    inv_freq = np.zeros((P, 1), np.float32)
    sin_sign = np.ones((P, 1), np.float32)

    def rotation(row, half):
        freq = np.power(np.float32(ROPE_THETA), -np.arange(half, dtype=np.float32) / np.float32(half))
        inv_freq[row:row + half, 0] = inv_freq[row + half:row + 2 * half, 0] = freq
        sin_sign[row:row + half, 0] = -1.0

    rotation(0, NI)
    rotation(IDX_DIM, NI)
    rotation(ROWS_DSA.start, NQ)
    rows, cols = np.arange(P)[:, None], np.arange(2 * SEQ - P)[None, :]
    window = np.where(cols <= rows + SEQ - P, 0.0, MASKED).astype(np.float32)
    strict = np.where(np.arange(P)[None, :] < rows, 0.0, MASKED)
    return {
        "inv_freq": inv_freq, "sin_sign": sin_sign, "ident": np.eye(P, dtype=np.float32),
        "strict": strict.astype(np.float32), "window": window,
    }


def kernel(x, positions, norm_g, w_in, sb_out_g, dsa_out_g, w_out, final_g):
    import concourse.bacc as bacc
    from concourse.bass_utils import run_bass_kernel_spmd

    w = np.zeros((D_MODEL, NBLK * P), np.float32)
    w[:, :D_IN] = np.asarray(w_in)[0]
    w = w.reshape(GRAN, KG, P, NBLK, P).transpose(3, 0, 2, 1, 4)[ORDER]
    wo = np.asarray(w_out)[0].reshape(KT, P, D_MODEL // HALF, HALF).transpose(2, 0, 1, 3)
    head_g = np.stack([np.asarray(g)[0].reshape(8, P).T for g in (sb_out_g, dsa_out_g)])
    arrays = {
        "x": np.asarray(x)[0], "positions": np.asarray(positions)[0], "norm_g": np.asarray(norm_g)[0],
        "w_in": w, "head_g": head_g, "w_out": wo, "final_g": np.asarray(final_g), **shape_constants(),
    }
    arrays = {f"in_{n}": np.ascontiguousarray(a) for n, a in arrays.items()}
    nc = bacc.Bacc("TRN2", target_bir_lowering=False, num_devices=1)
    args = {n[3:]: nc.dram_tensor(n, a.shape, mybir.dt.from_np(a.dtype), kind="ExternalInput").ap()
            for n, a in arrays.items()}
    out = nc.dram_tensor("out", (SEQ, D_MODEL), F32, kind="ExternalOutput").ap()
    hybrid_block(nc, out=out, **args)
    r = run_bass_kernel_spmd(nc, [arrays], core_ids=[0])
    return r.results[0]["out"].reshape(1, SEQ, D_MODEL)
```

```python
from contextlib import ExitStack

import numpy as np
import concourse.bass as bass
from concourse import mybir

F32 = mybir.dt.float32
F32R = mybir.dt.float32r
BF16 = mybir.dt.bfloat16
I32 = mybir.dt.int32
ALU = mybir.AluOpType
ACT = mybir.ActivationFunctionType
AX = mybir.AxisListType
ds = bass.ds

P = 128
SEQ = 1024
D_MODEL = 2048
HEAD_DIM = 128
SB_HEADS = 8
DSA_HEADS = 8
KV_HEADS = 2
REP = DSA_HEADS // KV_HEADS
IDX_HEADS = 16
IDX_DIM = 64
TOPK = 256
ROPE_THETA = 500000.0
EPS = 1e-6

KT = D_MODEL // P
ST = SEQ // P
HALF = SEQ // 2
QUARTER = SEQ // 4
GRAN = 2
KG = KT // GRAN
NQ = HEAD_DIM // 4 // 2
NI = IDX_DIM // 4 // 2

D_IN = 4 * 1024 + 2 * 1024 + 2 * 256 + IDX_HEADS * IDX_DIM + IDX_DIM + IDX_HEADS
NBLK = -(-D_IN // P)
IQ0 = 52
DQ0 = 32
ROT_BLKS = DSA_HEADS + KV_HEADS
IDX_BLKS = 1 + IDX_HEADS * IDX_DIM // P
ORDER = ([NBLK - 1] + list(range(IQ0, NBLK - 1)) + list(range(DQ0, DQ0 + ROT_BLKS)) + list(range(DQ0))
         + list(range(DQ0 + ROT_BLKS, IQ0)))
B_IK, B_IQ = 0, 1
B_DQ = IDX_BLKS
B_DK = B_DQ + DSA_HEADS
B_SBQ = B_DK + KV_HEADS
B_SBK, B_SBV, B_SBG = B_SBQ + 8, B_SBQ + 16, B_SBQ + 24
B_DV = B_SBQ + 32
B_DG = B_DV + KV_HEADS
FREE_BLKS = 4
SEL0 = TOPK // P
SEL_BLKS = 8
ROUNDS = TOPK // 8
LATER_ROUNDS = 5
FIRST_ROUNDS = ROUNDS - LATER_ROUNDS * (SEL_BLKS - 2)
HEADS_AT_ONCE = IDX_HEADS // 2
assert IDX_BLKS + FREE_BLKS + (ST - SEL0) * SEL_BLKS == NBLK

ROT_PER_TILE = 2
assert ROT_PER_TILE * (ST - SEL0 - 1) == ROT_BLKS

TRIG_BLKS = 3
TWO_PI = 2 * np.pi
TWO_PI_PARTS = [6.28125, float(np.floor((TWO_PI - 6.28125) * 2.0 ** 17) / 2.0 ** 17)]
TWO_PI_PARTS.append(TWO_PI - sum(TWO_PI_PARTS))
ROUNDER = 1.5 * 2.0 ** 23
PI_BELOW = 3.1415925

MASKED = -1.0e30
TAKEN = -3.0e38
ROWS_DSA = slice(32, 64)


def normalise(nc, sem, x, norm_g, ident_d, y_hi, y_lo):
    with ExitStack() as ctx:
        sb = lambda name, shape, dt=F32: ctx.enter_context(nc.sbuf_tensor(name, shape, dt))
        x_sb = [sb(f"x_sb{b}", [P, D_MODEL]) for b in range(2)]
        y_sb = [sb(f"y_sb{b}", [P, D_MODEL]) for b in range(2)]
        g_sb = sb("g_sb", [P, D_MODEL])
        squares = sb("squares", [P, D_MODEL], BF16)
        sumsq = sb("sumsq", [P, 2])
        root = sb("root", [P, 2])
        rstd = sb("rstd", [P, 2])
        eps = sb("eps_n", [P, 1])
        ident = sb("ident_n", [P, P])
        turned = [ctx.enter_context(nc.psum_tensor(f"turned{j}", [P, 4, P], F32)) for j in range(4)]
        x_in = [sem("x_in0"), sem("x_in1")]
        g_in, ident_in, eps_set = sem("g_in"), sem("ident_in"), sem("eps_set")
        summed, rooted, inverted, y_made = sem("summed"), sem("rooted"), sem("inverted"), sem("y_made")
        tile_turned, hi_made, lo_made = sem("tile_turned"), sem("hi_made"), sem("lo_made")
        block = ctx.enter_context(nc.Block())

        @block.sync
        def _(sp):
            sp.dma_start(x_sb[0][:], x[0:P, :]).then_inc(x_in[0], 16)
            sp.dma_start(g_sb[:], norm_g.partition_broadcast(P)).then_inc(g_in, 16)
            sp.dma_start(ident[:], ident_d).then_inc(ident_in, 16)
            sp.dma_start(x_sb[1][:], x[P:2 * P, :]).then_inc(x_in[1], 16)
            with sp.Fori(1, ST // 2) as i:
                for b in range(2):
                    sp.wait_ge(y_made, 2 * i + b - 1)
                    sp.dma_start(x_sb[b][:], x[ds((2 * i + b) * P, P), :]).then_inc(x_in[b], 16)

        @block.gpsimd
        def _(pool):
            nc.gpsimd.memset(eps[:], EPS).then_inc(eps_set, 1)

        @block.scalar
        def _(act):
            act.wait_ge(eps_set, 1)

            def root_of_mean(i, b):
                t = 2 * i + b
                act.wait_ge(x_in[b], 16 * (i + 1))
                nc.scalar.activation(squares[:], x_sb[b][:], ACT.Square,
                                     accum_out=sumsq[:, b:b + 1]).then_inc(summed, 1)
                act.wait_ge(summed, t + 1)
                nc.scalar.activation(root[:, b:b + 1], sumsq[:, b:b + 1], ACT.Sqrt, bias=eps[:],
                                     scale=1.0 / D_MODEL).then_inc(rooted, 1)

            def hi_parts(t):
                for j in range(4):
                    act.wait_ge(tile_turned, 4 * t + j + 1)
                    nc.scalar.activation(y_hi[:, 4 * j:4 * j + 4, ds(t * P, P)], turned[j][:],
                                         ACT.Copy).then_inc(hi_made, 1)

            root_of_mean(0, 0)
            root_of_mean(0, 1)
            hi_parts(0)
            with act.Fori(1, ST // 2) as i:
                root_of_mean(i, 0)
                hi_parts(2 * i - 1)
                root_of_mean(i, 1)
                hi_parts(2 * i)
            hi_parts(ST - 1)

        @block.vector
        def _(dve):
            dve.wait_ge(g_in, 16)

            def make_y(i, b, first):
                t = 2 * i + b
                dve.wait_ge(rooted, t + 1)
                nc.vector.reciprocal(rstd[:, b:b + 1], root[:, b:b + 1]).then_inc(inverted, 1)
                dve.wait_ge(inverted, t + 1)
                if not first:
                    dve.wait_ge(tile_turned, 4 * (t - 1))
                nc.vector.scalar_tensor_tensor(y_sb[b][:], x_sb[b][:], rstd[:, b:b + 1], g_sb[:],
                                               ALU.mult, ALU.mult).then_inc(y_made, 1)

            def lo_parts(t):
                for j in range(4):
                    dve.wait_ge(hi_made, 4 * t + j + 1)
                    nc.vector.tensor_tensor(y_lo[:, 4 * j:4 * j + 4, ds(t * P, P)], turned[j][:],
                                            y_hi[:, 4 * j:4 * j + 4, ds(t * P, P)].bitcast(F32),
                                            ALU.subtract).then_inc(lo_made, 1)

            make_y(0, 0, True)
            make_y(0, 1, True)
            lo_parts(0)
            with dve.Fori(1, ST // 2) as i:
                make_y(i, 0, False)
                lo_parts(2 * i - 1)
                make_y(i, 1, False)
                lo_parts(2 * i)
            lo_parts(ST - 1)

        @block.tensor
        def _(pe):
            pe.wait_ge(ident_in, 16)

            def turn(i, b, first):
                t = 2 * i + b
                pe.wait_ge(y_made, t + 1)
                for j in range(4):
                    if not first:
                        pe.wait_ge(lo_made, 4 * t + j - 3)
                    for k in range(4):
                        mm = nc.tensor.transpose(turned[j][:, k, :],
                                                 y_sb[b][:, (4 * j + k) * P:(4 * j + k + 1) * P], ident[:])
                    mm.then_inc(tile_turned, 1)

            turn(0, 0, True)
            turn(0, 1, False)
            with pe.Fori(1, ST // 2) as i:
                turn(i, 0, False)
                turn(i, 1, False)


def project(nc, sem, w_in, positions, inv_freq, sin_sign, trig, window, ident_d, y_hi, y_lo, proj, sel_bias):
    with ExitStack() as ctx:
        sb = lambda name, shape, dt=F32: ctx.enter_context(nc.sbuf_tensor(name, shape, dt))
        ps = lambda name, shape: ctx.enter_context(nc.psum_tensor(name, shape, F32))
        w_raw = [sb(f"w_raw{g}", [P, KG, P]) for g in range(GRAN)]
        w_hi = [sb(f"w_hi{g}", [P, KG, P], F32R) for g in range(GRAN)]
        w_lo = [sb(f"w_lo{g}", [P, KG, P], F32R) for g in range(GRAN)]
        stage = sb("stage", [P, SEQ])
        q_idx = sb("q_idx", [P, HEADS_AT_ONCE, P])
        q_swap = sb("q_swap", [P, HEADS_AT_ONCE, P])
        q_parts = sb("q_parts", [P, IDX_HEADS, P], F32R)
        trig_q = sb("trig_q", [P, 2, P])
        k_hi = sb("k_hi", [P, SEQ], F32R)
        k_lo = sb("k_lo", [P, SEQ], F32R)
        iw_t = sb("iw_t", [P, P])
        iw = sb("iw", [P, IDX_HEADS])
        relus = [sb(f"relus{b}", [P, SEQ]) for b in range(2)]
        causal = sb("causal", [P, SEQ])
        work = sb("work", [P, SEQ])
        bias_out = sb("bias_out", [P, SEQ], BF16)
        best = sb("best", [P, 8])
        freq = sb("freq", [P, 1])
        sign = sb("sign", [P, 1])
        pos, angle, turns = causal, relus[0], relus[1]
        half_sin = q_idx[:].rearrange("p h s -> p (h s)")
        keys_in = causal
        rot = sb("rot", [P, ROT_PER_TILE, QUARTER])
        rot_swap = sb("rot_swap", [P, ROT_PER_TILE, QUARTER])
        rot_table = sb("rot_table", [P, 2, QUARTER])
        ident = sb("ident_p", [P, P])
        acc = [ps(f"acc{s}", [P, HALF]) for s in range(2)]
        rel = [ps(f"rel{b}", [P, SEQ]) for b in range(2)]
        iw_ps = ps("iw_ps", [P, HALF])

        w_loaded = [sem(f"w_loaded{g}") for g in range(GRAN)]
        hi_made, lo_made = sem("w_hi_made"), sem("w_lo_made")
        g0_used, half_done, evacuated, stored = sem("g0_used"), sem("half_done"), sem("evacuated"), sem("stored")
        prep_in, prep_set, k_step, k_rotated, k_ready = sem("prep_in"), sem("prep_set"), sem("k_step"), sem("k_rotated"), sem("k_ready")
        k_hi_made = sem("k_hi_made")
        tile_in, queries_in, q_step, q_rotated = sem("tile_in"), sem("queries_in"), sem("q_step"), sem("q_rotated")
        q_hi_made, q_ready = sem("q_hi_made"), sem("q_ready")
        iw_turned, iw_ready = sem("iw_turned"), sem("iw_ready")
        scored, relued, summed = sem("scored"), sem("relued"), sem("head_summed")
        pos_in, trig_step, sines, table_out = sem("pos_in"), sem("trig_step"), sem("sines"), sem("table_out")
        rot_in, rot_step, rot_made, rot_stored = sem("rot_in"), sem("rot_step"), sem("rot_made"), sem("rot_stored")
        topk_step, bias_made, bias_stored = sem("topk_step"), sem("bias_made"), sem("bias_stored")
        block = ctx.enter_context(nc.Block())
        TILE_DMAS = 5
        QUERY_DMAS = 6
        STEP_OF_HEAD0 = 6
        def wait(eng, s, value):
            if not (isinstance(value, int) and value <= 0):
                eng.wait_ge(s, value)

        GROUPS = [(0, 2, HALF), (2, 4, SEQ)]
        assert SEL0 + 2 == HALF // P and SEL0 + 6 == ST
        N_SEL0 = IDX_BLKS + FREE_BLKS

        @block.sync
        def _(sp):
            def load_block(n, first=False):
                for g in range(GRAN):
                    if not first:
                        sp.wait_ge(lo_made, 2 * n + g - 1)
                    sp.dma_start(w_raw[g][:], w_in[n, g]).then_inc(w_loaded[g], 16)

            def store_block(n):
                sp.wait_ge(evacuated, 2 * n + 2)
                sp.dma_start(proj[n], stage[:]).then_inc(stored, 16)

            def load_keys():
                sp.wait_ge(stored, 16 * IDX_BLKS)
                sp.wait_ge(table_out, 32)
                sp.wait_ge(prep_set, 4)
                for half in (0, IDX_DIM):
                    sp.dma_start(keys_in[half:half + IDX_DIM, :], proj[B_IK, 0:IDX_DIM, :]).then_inc(prep_in, 16)
                    sp.dma_start(work[half:half + NI, :], proj[B_IK, NI:2 * NI, :]).then_inc(prep_in, 16)
                    sp.dma_start(work[half + NI:half + 2 * NI, :], proj[B_IK, 0:NI, :]).then_inc(prep_in, 16)
                for f in range(2):
                    sp.dma_start(relus[f][:], trig[f]).then_inc(prep_in, 16)
                    sp.wait_ge(prep_in, 16 * (7 + 2 * f))
                    sp.dma_start(relus[f][ROWS_DSA, :], trig[f, 96:128, :]).then_inc(prep_in, 16)
                sp.dma_start(ident[:], ident_d).then_inc(prep_in, 16)
                for s in range(4):
                    part = slice(32 * s, 32 * s + 32)
                    cols = slice(QUARTER * s, QUARTER * s + QUARTER)
                    sp.dma_start(rot_table[part], trig.rearrange("f p s -> p f s")[ROWS_DSA, :, cols]).then_inc(prep_in, 16)

            def load_queries(u, half_no, first=False):
                n = 2 * u + half_no
                if not first:
                    sp.wait_ge(q_ready, n)
                h0 = 2 * B_IQ + HEADS_AT_ONCE * half_no
                heads = proj.rearrange("n (e d) s -> (n e) d s", e=2)[h0:h0 + HEADS_AT_ONCE]
                queries = heads.rearrange("h d s -> d h s")[:, :, ds((u + SEL0) * P, P)]
                for half in (0, IDX_DIM):
                    sp.dma_start(q_idx[half:half + IDX_DIM], queries).then_inc(queries_in, 16)
                    sp.dma_start(q_swap[half:half + NI], queries[NI:2 * NI]).then_inc(queries_in, 16)
                    sp.dma_start(q_swap[half + NI:half + 2 * NI], queries[0:NI]).then_inc(queries_in, 16)

            def load_tile(u, first):
                q0 = (u + SEL0) * P
                if first:
                    sp.wait_ge(k_rotated, 1)
                else:
                    sp.wait_ge(scored, IDX_HEADS * u)
                    sp.wait_ge(summed, IDX_HEADS * u)
                tables = trig.rearrange("f p s -> p f s")
                sp.dma_start(trig_q[0:32], tables[0:32, :, ds(q0, P)]).then_inc(tile_in, 16)
                sp.dma_start(trig_q[ROWS_DSA], tables[96:128, :, ds(q0, P)]).then_inc(tile_in, 16)
                sp.dma_start(trig_q[64:128], tables[64:128, :, ds(q0, P)]).then_inc(tile_in, 16)
                sp.dma_start(iw_t[0:IDX_HEADS, :], proj[B_IK, IDX_DIM:IDX_DIM + IDX_HEADS, ds(q0, P)]).then_inc(tile_in, 16)
                sp.dma_start(causal[:], window[:, ds(SEQ - P - q0, SEQ)]).then_inc(tile_in, 16)

            def load_rotated(u):
                blocks = proj[ds(B_DQ + ROT_PER_TILE * (u - 1), ROT_PER_TILE)].rearrange("b p s -> p b s")
                for s in range(4):
                    p0 = 32 * s
                    cols = slice(QUARTER * s, QUARTER * s + QUARTER)
                    sp.dma_start(rot[p0:p0 + 32], blocks[0:32, :, cols]).then_inc(rot_in, 16)
                    sp.dma_start(rot_swap[p0:p0 + NQ], blocks[NQ:2 * NQ, :, cols]).then_inc(rot_in, 16)
                    sp.dma_start(rot_swap[p0 + NQ:p0 + 2 * NQ], blocks[0:NQ, :, cols]).then_inc(rot_in, 16)

            def store_rotated(u):
                blocks = proj[ds(B_DQ + ROT_PER_TILE * (u - 1), ROT_PER_TILE)].rearrange("b p s -> p b s")
                sp.wait_ge(rot_made, u)
                for s in range(4):
                    cols = slice(QUARTER * s, QUARTER * s + QUARTER)
                    sp.dma_start(blocks[0:32, :, cols], rot[32 * s:32 * s + 32]).then_inc(rot_stored, 16)

            load_block(0, True)
            sp.dma_start(pos[:].bitcast(I32), positions.partition_broadcast(P)).then_inc(pos_in, 16)
            sp.dma_start(freq[:], inv_freq).then_inc(pos_in, 16)
            sp.dma_start(sign[:], sin_sign).then_inc(pos_in, 16)
            with sp.Fori(1, TRIG_BLKS + 1) as n:
                load_block(n)
                store_block(n - 1)
            sp.wait_ge(trig_step, 11)
            sp.dma_start(trig[0], pos[:]).then_inc(table_out, 16)
            sp.dma_start(trig[1], turns[:]).then_inc(table_out, 16)
            with sp.Fori(TRIG_BLKS + 1, IDX_BLKS) as n:
                load_block(n)
                store_block(n - 1)
            load_block(IDX_BLKS)
            store_block(IDX_BLKS - 1)
            load_keys()
            with sp.Fori(IDX_BLKS + 1, N_SEL0) as n:
                load_block(n)
                store_block(n - 1)

            load_tile(0, True)
            load_queries(0, 0, True)

            def selected(u, first=False, last=False):
                n = N_SEL0 + SEL_BLKS * u
                load_block(n)
                load_queries(u, 1)
                store_block(n - 1)
                if not first:
                    load_rotated(u)
                load_block(n + 1)
                store_block(n)
                if not last:
                    load_tile(u + 1, False)
                    load_queries(u + 1, 0)
                if not first:
                    store_rotated(u)
                with sp.Fori(2, SEL_BLKS) as j:
                    load_block(n + j)
                    store_block(n + j - 1)
                if not first:
                    sp.wait_ge(rot_stored, 64 * u)
                sp.wait_ge(bias_made, u + 1)
                sp.dma_start(sel_bias[u], bias_out[:]).then_inc(bias_stored, 16)

            selected(0, first=True)
            with sp.Fori(1, ST - SEL0 - 1) as u:
                selected(u)
            selected(ST - SEL0 - 1, last=True)
            store_block(NBLK - 1)
            sp.wait_ge(stored, 16 * NBLK)
            sp.wait_ge(bias_stored, 16 * (ST - SEL0))

        @block.gpsimd
        def _(pool):
            nc.gpsimd.memset(work[:], 0.0).then_inc(prep_set, 1)
            nc.gpsimd.memset(q_swap[:], 0.0).then_inc(prep_set, 1)
            nc.gpsimd.memset(iw_t[:], 0.0).then_inc(prep_set, 1)
            nc.gpsimd.memset(bias_out[:], 0.0).then_inc(prep_set, 1)

        @block.scalar
        def _(act):
            def hi_part(n, g, first=False):
                act.wait_ge(w_loaded[g], 16 * (n + 1))
                if not first:
                    if g == 0:
                        act.wait_ge(g0_used, n)
                    else:
                        act.wait_ge(half_done, 2 * n)
                nc.scalar.activation(w_hi[g][:], w_raw[g][:], ACT.Copy).then_inc(hi_made, 1)

            def evacuate(n, s, first=False):
                act.wait_ge(half_done, 2 * n + s + 1)
                if s == 0 and not first:
                    act.wait_ge(stored, 16 * n)
                nc.scalar.activation(stage[:, s * HALF:(s + 1) * HALF], acc[s][:], ACT.Copy).then_inc(evacuated, 1)

            def split_and_finish(n):
                hi_part(n, 0)
                hi_part(n, 1)
                evacuate(n - 1, 1)

            def query_parts(u, half_no):
                n = 2 * u + half_no
                act.wait_ge(q_rotated, n + 1)
                if half_no == 0:
                    wait(act, scored, IDX_HEADS * u)
                nc.scalar.activation(q_parts[:, HEADS_AT_ONCE * half_no:HEADS_AT_ONCE * (half_no + 1), :], q_idx[:],
                                     ACT.Copy).then_inc(q_hi_made, 1)

            def relu(u, h, keys, first):
                act.wait_ge(scored, IDX_HEADS * u + h + 1)
                if not (first and h < 2):
                    act.wait_ge(summed, IDX_HEADS * u + h - 1)
                nc.scalar.activation(relus[h % 2][:, 0:keys], rel[h % 2][:, 0:keys],
                                     ACT.Relu).then_inc(relued, 1)

            hi_part(0, 0, True)
            hi_part(0, 1, True)
            evacuate(0, 0, True)
            for n in range(1, TRIG_BLKS + 1):
                split_and_finish(n)
                evacuate(n, 0)
                if n == TRIG_BLKS - 1:
                    act.wait_ge(trig_step, 8)
                    nc.scalar.activation(turns[:], angle[:], ACT.Sin).then_inc(sines, 1)
                    nc.scalar.activation(half_sin, angle[:], ACT.Sin, scale=0.5).then_inc(sines, 1)
            with act.Fori(TRIG_BLKS + 1, IDX_BLKS + 1) as n:
                split_and_finish(n)
                evacuate(n, 0)
            act.wait_ge(k_rotated, 1)
            nc.scalar.activation(k_hi[:], work[:], ACT.Copy).then_inc(k_hi_made, 1)
            with act.Fori(IDX_BLKS + 1, N_SEL0) as n:
                split_and_finish(n)
                evacuate(n, 0)

            def selected(u, keys, first):
                n = N_SEL0 + SEL_BLKS * u
                query_parts(u, 0)
                hi_part(n, 0)
                hi_part(n, 1)
                evacuate(n - 1, 1)
                query_parts(u, 1)
                if first:
                    act.wait_ge(k_ready, 1)
                for h in range(IDX_HEADS):
                    if STEP_OF_HEAD0 + h == KT:
                        evacuate(n, 0)
                    relu(u, h, keys, first)
                with act.Fori(1, SEL_BLKS) as j:
                    split_and_finish(n + j)
                    evacuate(n + j, 0)

            for u0, count, keys in GROUPS:
                if u0 == 0:
                    selected(0, keys, True)
                    u0, count = 1, count - 1
                with act.Fori(u0, u0 + count) as u:
                    selected(u, keys, False)
            evacuate(NBLK - 1, 1)

        @block.vector
        def _(dve):
            def lo_part(n, g):
                dve.wait_ge(hi_made, 2 * n + g + 1)
                nc.vector.tensor_tensor(w_lo[g][:], w_raw[g][:], w_hi[g][:].bitcast(F32),
                                        ALU.subtract).then_inc(lo_made, 1)

            def trig_tables():
                done = [0]

                def link(ins):
                    done[0] += 1
                    ins.then_inc(trig_step, 1)
                    dve.wait_ge(trig_step, done[0])

                def part(which):
                    if which == 0:
                        dve.wait_ge(pos_in, 48)
                        link(nc.vector.tensor_copy(pos[:], pos[:].bitcast(I32)))
                        link(nc.vector.tensor_scalar(angle[:], pos[:], freq[:], None, ALU.mult))
                        link(nc.vector.tensor_scalar(turns[:], angle[:], 1.0 / TWO_PI, ROUNDER, ALU.mult, ALU.add))
                        link(nc.vector.tensor_scalar(turns[:], turns[:], ROUNDER, None, ALU.subtract))
                    elif which == 1:
                        for two_pi_part in TWO_PI_PARTS:
                            link(nc.vector.scalar_tensor_tensor(angle[:], turns[:], -two_pi_part, angle[:],
                                                                ALU.mult, ALU.add))
                        link(nc.vector.tensor_scalar(angle[:], angle[:], PI_BELOW, -PI_BELOW, ALU.min, ALU.max))
                    elif which == 2:
                        dve.wait_ge(sines, 2)
                        link(nc.vector.tensor_tensor(pos[:], half_sin, half_sin, ALU.mult))
                        link(nc.vector.tensor_scalar(pos[:], pos[:], -2.0, 1.0, ALU.mult, ALU.add))
                        nc.vector.tensor_scalar(turns[:], turns[:], sign[:], None, ALU.mult).then_inc(trig_step, 1)

                return part

            def rotate_keys():
                dve.wait_ge(prep_in, 16 * 15)
                nc.vector.tensor_tensor(work[:], work[:], relus[1][:], ALU.mult).then_inc(k_step, 1)
                nc.vector.tensor_tensor(keys_in[:], keys_in[:], relus[0][:], ALU.mult).then_inc(k_step, 1)
                dve.wait_ge(k_step, 2)
                nc.vector.tensor_tensor(work[:], keys_in[:], work[:], ALU.add).then_inc(k_rotated, 1)

            def split_keys():
                dve.wait_ge(k_hi_made, 1)
                nc.vector.tensor_tensor(k_lo[:], work[:], k_hi[:].bitcast(F32), ALU.subtract).then_inc(k_ready, 1)

            def rotate_queries(u, half_no):
                n = 2 * u + half_no
                if half_no == 0:
                    dve.wait_ge(tile_in, 16 * TILE_DMAS * (u + 1))
                dve.wait_ge(queries_in, 16 * QUERY_DMAS * (n + 1))
                for f, q in ((0, q_idx), (1, q_swap)):
                    table = trig_q[:, f:f + 1, :].broadcast_to([P, HEADS_AT_ONCE, P])
                    nc.vector.tensor_tensor(q[:], q[:], table, ALU.mult).then_inc(q_step, 1)
                dve.wait_ge(q_step, 2 * (n + 1))
                nc.vector.tensor_tensor(q_idx[:], q_idx[:], q_swap[:], ALU.add).then_inc(q_rotated, 1)

            def query_lo(u, half_no):
                n = 2 * u + half_no
                dve.wait_ge(q_hi_made, n + 1)
                lo = q_parts[IDX_DIM:P, HEADS_AT_ONCE * half_no:HEADS_AT_ONCE * (half_no + 1), :]
                nc.vector.tensor_tensor(lo, q_idx[IDX_DIM:P], lo.bitcast(F32), ALU.subtract).then_inc(q_ready, 1)

            def rotate_blocks(u):
                dve.wait_ge(rot_in, 16 * 12 * u)
                for f, q in ((0, rot), (1, rot_swap)):
                    table = rot_table[:, f:f + 1, :].broadcast_to([P, ROT_PER_TILE, QUARTER])
                    nc.vector.tensor_tensor(q[:], q[:], table, ALU.mult).then_inc(rot_step, 1)
                dve.wait_ge(rot_step, 2 * u)
                nc.vector.tensor_tensor(rot[:], rot[:], rot_swap[:], ALU.add).then_inc(rot_made, 1)

            def sum_heads(u, keys):
                dve.wait_ge(iw_turned, u + 1)
                nc.vector.tensor_scalar(iw[:], iw_ps[:, 0:IDX_HEADS], IDX_DIM ** -0.5 * IDX_HEADS ** -0.5,
                                        None, ALU.mult).then_inc(iw_ready, 1)
                dve.wait_ge(iw_ready, u + 1)
                for h in range(IDX_HEADS):
                    dve.wait_ge(relued, IDX_HEADS * u + h + 1)
                    if h:
                        dve.wait_ge(summed, IDX_HEADS * u + h)
                    so_far = work if h else causal
                    nc.vector.scalar_tensor_tensor(work[:, 0:keys], relus[h % 2][:, 0:keys], iw[:, h:h + 1],
                                                   so_far[:, 0:keys], ALU.mult, ALU.add).then_inc(summed, 1)

            def rounds(m, keys):
                for r in range(m):
                    nc.vector.max(best[:], work[:, 0:keys]).then_inc(topk_step, 1)
                    dve.wait_ge(topk_step, 2 * r + 1)
                    nc.vector.match_replace(work[:, 0:keys], best[:], work[:, 0:keys], TAKEN).then_inc(topk_step, 1)
                    dve.wait_ge(topk_step, 2 * r + 2)
                dve.sem_clear(topk_step)

            lo_part(0, 0)
            lo_part(0, 1)
            trig_ops = trig_tables()
            for n in range(1, TRIG_BLKS + 1):
                lo_part(n, 0)
                lo_part(n, 1)
                trig_ops(n - 1)
            with dve.Fori(TRIG_BLKS + 1, IDX_BLKS + 1) as n:
                lo_part(n, 0)
                lo_part(n, 1)
            rotate_keys()
            split_keys()
            with dve.Fori(IDX_BLKS + 1, N_SEL0) as n:
                lo_part(n, 0)
                lo_part(n, 1)

            def selected(u, keys, first):
                n = N_SEL0 + SEL_BLKS * u
                rotate_queries(u, 0)
                query_lo(u, 0)
                lo_part(n, 0)
                lo_part(n, 1)
                rotate_queries(u, 1)
                query_lo(u, 1)
                sum_heads(u, keys)
                dve.wait_ge(summed, IDX_HEADS * (u + 1))
                if not first:
                    rotate_blocks(u)
                lo_part(n + 1, 0)
                lo_part(n + 1, 1)
                rounds(FIRST_ROUNDS, keys)
                with dve.Fori(2, SEL_BLKS) as j:
                    lo_part(n + j, 0)
                    rounds(LATER_ROUNDS // 2, keys)
                    lo_part(n + j, 1)
                    rounds(LATER_ROUNDS - LATER_ROUNDS // 2, keys)
                if not first:
                    dve.wait_ge(bias_stored, 16 * u)
                nc.vector.tensor_scalar(bias_out[:, 0:keys], work[:, 0:keys], 0.5 * TAKEN, MASKED,
                                        ALU.is_gt, ALU.mult).then_inc(bias_made, 1)

            for u0, count, keys in GROUPS:
                if u0 == 0:
                    selected(0, keys, True)
                    u0, count = 1, count - 1
                with dve.Fori(u0, u0 + count) as u:
                    selected(u, keys, False)

        @block.tensor
        def _(pe):
            def project_block(n, first=False, beside=None):
                for s in range(2):
                    cols = slice(s * HALF, (s + 1) * HALF)
                    if not first:
                        pe.wait_ge(evacuated, 2 * n + s - 1)
                    for g in range(GRAN):
                        if s == 0:
                            pe.wait_ge(lo_made, 2 * n + g + 1)
                        for k in range(KG):
                            kk = g * KG + k
                            nc.tensor.matmul(acc[s][:], w_hi[g][:, k, :], y_hi[:, kk, cols],
                                             start=kk == 0, stop=False)
                            nc.tensor.matmul(acc[s][:], w_hi[g][:, k, :], y_lo[:, kk, cols],
                                             start=False, stop=False)
                            mm = nc.tensor.matmul(acc[s][:], w_lo[g][:, k, :], y_hi[:, kk, cols],
                                                  start=False, stop=kk == KT - 1)
                            if g == 0 and s == 1 and k == KG - 1:
                                mm.then_inc(g0_used, 1)
                            if kk == KT - 1:
                                mm.then_inc(half_done, 1)
                            if beside:
                                beside(KT * s + kk)

            def score(u, step, keys, first):
                h = step - STEP_OF_HEAD0
                if h == -1:
                    pe.wait_ge(tile_in, 16 * TILE_DMAS * (u + 1))
                    if first:
                        pe.wait_ge(prep_in, 16 * 15)
                    else:
                        pe.wait_ge(iw_ready, u)
                    nc.tensor.transpose(iw_ps[:, 0:P], iw_t[:], ident[:]).then_inc(iw_turned, 1)
                if not 0 <= h < IDX_HEADS:
                    return
                if h % HEADS_AT_ONCE == 0:
                    pe.wait_ge(q_ready, 2 * u + h // HEADS_AT_ONCE + 1)
                    if first:
                        pe.wait_ge(k_ready, 1)
                if not (first and h < 2):
                    pe.wait_ge(relued, IDX_HEADS * u + h - 1)
                for c in range(0, keys, HALF):
                    out = rel[h % 2][:, c:c + HALF]
                    nc.tensor.matmul(out, q_parts[:, h, :], k_hi[:, c:c + HALF], start=True, stop=False)
                    mm = nc.tensor.matmul(out, q_parts[:, h, :], k_lo[:, c:c + HALF], start=False, stop=True)
                mm.then_inc(scored, 1)

            project_block(0, True)
            with pe.Fori(1, N_SEL0) as n:
                project_block(n)

            def selected(u, keys, first):
                n = N_SEL0 + SEL_BLKS * u
                project_block(n, beside=lambda step: score(u, step, keys, first))
                with pe.Fori(1, SEL_BLKS) as j:
                    project_block(n + j)

            for u0, count, keys in GROUPS:
                if u0 == 0:
                    selected(0, keys, True)
                    u0, count = 1, count - 1
                with pe.Fori(u0, u0 + count) as u:
                    selected(u, keys, False)


LAG = 3
HEADS_PER_PASS = 2
UNITS = HEADS_PER_PASS * ST
RING = 8
SCALE = HEAD_DIM ** -0.5
CH = HALF // P


def events_of_pass(pe):
    ev = []
    for u in range(UNITS):
        ev.append((u, 1 if pe else 5, "scores", u))
        ev.append((u + 2, 0, "norm", u))
        ev.append((u + LAG, 2, "turn", u))
    for b in range(HEADS_PER_PASS):
        ev.append((ST * b + LAG - 1, 4, "turn_v", b))
        for c in range(2):
            last = ST * b + CH * c + CH - 1
            ev.append((last + LAG + 1, 3 if pe else 6, "values", (b, c)))
            ev.append((last + LAG + 4 - c, 7, "sumsq", (b, c)))
            ev.append((ST * b + ST - 1 + LAG + 5 + 2 * c, 9, "spread", (b, c)))
        ev.append((ST * b + ST - 1 + LAG + 3, 8, "root", b))
    return sorted(ev, key=lambda e: (e[0] % UNITS, e[1], -e[0]))


EVENTS = {pe: events_of_pass(pe) for pe in (False, True)}
IN_TIME = sorted(EVENTS[True], key=lambda e: e[:2])


def groups_of(kind, arg):
    if kind == "turn_v":
        return [0, CH]
    return [0, CH] if arg % ST >= CH else [0]


GROUP_NO = {}
for _, _, kind_, arg_ in IN_TIME:
    if kind_ in ("turn", "turn_v"):
        for j0_ in groups_of(kind_, arg_):
            GROUP_NO[kind_, arg_, j0_] = len(GROUP_NO)
GROUPS_PER_PASS = len(GROUP_NO)
assert GROUPS_PER_PASS % 2 == 0
STAT_NO = {(kind_, arg_): n_ for n_, (_, _, kind_, arg_) in
           enumerate(e for e in IN_TIME if e[2] in ("sumsq", "spread"))}
STATS = len(STAT_NO)
ROOT_STEPS = 10


def in_order(p, first, pe=False):
    for step, _, kind, arg in EVENTS[pe]:
        if step < UNITS:
            yield kind, p, arg
        elif not first:
            yield kind, p - 1, arg


def left_over(p, pe=False):
    for step, _, kind, arg in EVENTS[pe]:
        if step >= UNITS:
            yield kind, p, arg


def attend(nc, sem, kind_of_heads, b_q, b_k, b_v, b_g, proj, mixed_t, head_g, ident_d, strict_d, window,
           sel_bias):
    sb_heads = kind_of_heads == "sb"
    n_pass = 4
    k_ = kind_of_heads
    half_groups = GROUPS_PER_PASS // 2
    with ExitStack() as ctx:
        sb = lambda name, shape, dt=F32: ctx.enter_context(nc.sbuf_tensor(f"{k_}_{name}", shape, dt))
        ps = lambda name, shape: ctx.enter_context(nc.psum_tensor(f"{k_}_{name}", shape, F32))
        sm = lambda name: sem(f"{k_}_{name}")
        both = range(HEADS_PER_PASS)
        q = [sb(f"q{b}", [P, SEQ]) for b in both]
        k = [sb(f"k{b}", [P, SEQ]) for b in both]
        v_t = [sb(f"v_t{b}", [P, SEQ]) for b in both]
        gate = [sb(f"gate{b}", [P, SEQ]) for b in both]
        v = [sb(f"v{b}", [P, ST, P]) for b in both]
        w = [sb(f"w{r}", [P, SEQ]) for r in range(RING)]
        stay = [sb(f"stay{r}", [P, SEQ]) for r in range(RING)] if sb_heads else None
        w_t = [sb(f"w_t{c}", [P, ST, HALF]) for c in range(2)]
        o = [sb(f"o{b}", [P, SEQ]) for b in both]
        var = [sb(f"var{b}", [P, ST]) for b in both]
        rstd = [sb(f"rstd{b}", [P, ST]) for b in both]
        newton = sb("newton", [P, ST])
        silu = [sb(f"silu{b}", [P, SEQ]) for b in both]
        squares = [sb(f"squares{c}", [P, HALF]) for c in range(2)]
        ones = sb("ones", [P, 1])
        ident = sb("ident", [P, P])
        g_sb = sb("g", [P, 8])
        if sb_heads:
            ident16 = sb("ident16", [P, P], BF16)
            strict = sb("strict", [P, P], BF16)
        else:
            bias = sb("bias", [P, ST, SEQ], BF16)
            low = sb("low", [P, RING])
            den = sb("den", [P, RING])
            spare = sb("spare", [P, RING])
            inv = sb("inv", [P, RING])
        sc = [ps(f"sc{r}", [P, SEQ]) for r in range(2)]
        tr = [ps(f"tr{r}", [P, CH, P]) for r in range(2)]
        pv = ps("pv", [P, HALF])
        ss = ps("ss", [P, HALF])

        qkv_in = [sm(f"qkv_in{b}") for b in both]
        gate_in = [sm(f"gate_in{b}") for b in both]
        consts_in, set_up = sm("consts_in"), sm("set_up")
        scored, sc_read, scanned, w_ready = sm("scored"), sm("sc_read"), sm("scanned"), sm("w_ready")
        converted = sm("converted")
        exped, inverted = sm("exped"), sm("inverted")
        turned = [sm(f"turned{r}") for r in range(2)]
        copied = [sm(f"copied{r}") for r in range(2)]
        pv_done, pv_read, squared, ss_done, ss_read = sm("pv_done"), sm("pv_read"), sm("squared"), sm("ss_done"), sm("ss_read")
        sigmoided, root_step, rooted, gated = sm("sigmoided"), sm("root_step"), sm("rooted"), sm("gated")
        fin_step, mixed, stored = sm("fin_step"), sm("mixed"), [sm(f"stored{b}") for b in both]
        block = ctx.enter_context(nc.Block())
        QKV_DMAS = 3
        CONST_DMAS = 4 if sb_heads else 2 + ST

        def wait(eng, s, value):
            if not (isinstance(value, int) and value <= 0):
                eng.wait_ge(s, value)

        def group(p, kind, arg, j0):
            no = GROUP_NO[kind, arg, j0]
            return no % 2, half_groups * p + no // 2 + 1

        def tiles_in(kind, arg, j0):
            return CH if kind == "turn_v" else min(CH, arg % ST + 1 - j0)

        def wait_slot_free(eng, p, u):
            pu, uu = (p, u - RING) if u >= RING else (p - 1, u - RING + UNITS)
            bank, done = group(pu, "turn", uu, groups_of("turn", uu)[-1])
            wait(eng, turned[bank], done)

        def chunk_no(p, b, c):
            return 2 * HEADS_PER_PASS * p + 2 * b + c

        def copy_group(eng, op, bank, p, kind, arg):
            for j0 in groups_of(kind, arg):
                at, done = group(p, kind, arg, j0)
                if at != bank:
                    continue
                n = tiles_in(kind, arg, j0)
                wait(eng, turned[bank], done)
                if kind == "turn_v":
                    dst = v[arg][:, j0:j0 + n, :]
                else:
                    chunk = arg // CH
                    wait(eng, pv_done, 2 * HEADS_PER_PASS * p + chunk - 1)
                    c0 = arg % CH * P
                    dst = w_t[chunk % 2][:, j0:j0 + n, c0:c0 + P]
                op(dst, tr[bank][:, 0:n, :]).then_inc(copied[bank], 1)

        @block.sync
        def _(sp):
            sp.dma_start(ident[:], ident_d).then_inc(consts_in, 16)
            sp.dma_start(g_sb[:], head_g).then_inc(consts_in, 16)
            if sb_heads:
                sp.dma_start(squares[0][:, 0:P], ident_d).then_inc(consts_in, 16)
                sp.dma_start(squares[1][:, 0:P], strict_d).then_inc(consts_in, 16)
            else:
                for i in range(ST):
                    keys = (i + 1) * P
                    if i < SEL0:
                        sp.dma_start(squares[i][:, 0:keys], window[:, SEQ - keys:SEQ]).then_inc(consts_in, 16)
                    else:
                        sp.dma_start(bias[:, i, 0:keys], sel_bias[i - SEL0, :, 0:keys]).then_inc(consts_in, 16)

            def load_head(p, kv, b, first):
                n = HEADS_PER_PASS * p + b
                if not first:
                    sp.wait_ge(scored, UNITS * (p - 1) + ST * (b + 1))
                sp.dma_start(q[b][:], proj[b_q + n]).then_inc(qkv_in[b], 16)
                sp.dma_start(k[b][:], proj[b_k + kv]).then_inc(qkv_in[b], 16)
                sp.dma_start(v_t[b][:], proj[b_v + kv]).then_inc(qkv_in[b], 16)
                if not first:
                    sp.wait_ge(mixed, 2 * n - 2)
                    sp.dma_start(mixed_t[n - 2], o[b][:]).then_inc(stored[b], 16)
                sp.dma_start(gate[b][:], proj[b_g + n]).then_inc(gate_in[b], 16)

            def load_pass(p, g, first=False):
                for b in both:
                    load_head(p, HEADS_PER_PASS * p + b if sb_heads else g, b, first)

            load_pass(0, 0, True)
            if sb_heads:
                with sp.Fori(1, n_pass) as p:
                    load_pass(p, None)
            else:
                load_pass(1, 0)
                with sp.Fori(2, n_pass) as p:
                    load_pass(p, 1)
            for b in both:
                n = HEADS_PER_PASS * n_pass + b
                sp.wait_ge(mixed, 2 * n - 2)
                sp.dma_start(mixed_t[n - 2], o[b][:]).then_inc(stored[b], 16)
            for b in both:
                sp.wait_ge(stored[b], 16 * n_pass)

        def pool_events(pool, events):
            for kind, p, arg in events:
                if kind == "scores" and sb_heads:
                    r, n = arg % RING, (arg % ST + 1) * P
                    pool.wait_ge(scanned, UNITS * p + arg + 1)
                    nc.gpsimd.tensor_tensor(w[r][:, 0:n - 1], w[r][:, 0:n - 1], stay[r][:, 1:n],
                                            ALU.mult).then_inc(w_ready, 1)
                elif kind == "values":
                    b, c = arg
                    no = chunk_no(p, b, c)
                    part = o[b][:, c * HALF:(c + 1) * HALF]
                    pool.wait_ge(pv_read, no + 1)
                    wait(pool, ss_done, no - 1)
                    nc.gpsimd.tensor_tensor(squares[c][:], part, part, ALU.mult).then_inc(squared, 1)
                elif kind == "root":
                    pool.wait_ge(sigmoided, HEADS_PER_PASS * p + arg + 1)
                    nc.gpsimd.tensor_tensor(silu[arg][:], silu[arg][:], gate[arg][:], ALU.mult).then_inc(gated, 1)

        @block.gpsimd
        def _(pool):
            nc.gpsimd.memset(ones[:], 1.0).then_inc(set_up, 1)
            pool.wait_ge(converted, 2)
            pool_events(pool, in_order(0, True))
            with pool.Fori(1, n_pass) as p:
                pool_events(pool, in_order(p, False))
            pool_events(pool, left_over(n_pass - 1))

        @block.scalar
        def _(act):
            def copy(dst, src):
                return nc.scalar.activation(dst, src, ACT.Copy)

            def run(events):
                for kind, p, arg in events:
                    if kind == "scores":
                        r, n = arg % RING, (arg % ST + 1) * P
                        unit = UNITS * p + arg
                        if sb_heads:
                            act.wait_ge(scored, unit + 1)
                            wait_slot_free(act, p, arg)
                            nc.scalar.activation(w[r][:, 0:n], sc[arg % 2][:, 0:n], ACT.Sigmoid, scale=SCALE)
                            nc.scalar.activation(stay[r][:, 0:n], sc[arg % 2][:, 0:n], ACT.Sigmoid,
                                                 scale=-SCALE).then_inc(sc_read, 1)
                        else:
                            act.wait_ge(sc_read, unit + 1)
                            nc.scalar.activation(w[r][:, 0:n], w[r][:, 0:n], ACT.Exp, bias=low[:, r:r + 1],
                                                 scale=-1.0, accum_out=den[:, r:r + 1]).then_inc(exped, 1)
                    elif kind in ("turn", "turn_v"):
                        copy_group(act, copy, 0, p, kind, arg)
                    elif kind == "values":
                        b, c = arg
                        no = chunk_no(p, b, c)
                        act.wait_ge(pv_done, no + 1)
                        if c == 0:
                            wait(act, stored[b], 16 * p)
                        copy(o[b][:, c * HALF:(c + 1) * HALF], pv[:]).then_inc(pv_read, 1)
                    elif kind == "root":
                        b = arg
                        act.wait_ge(gate_in[b], 16 * (p + 1))
                        wait(act, mixed, 2 * (HEADS_PER_PASS * (p - 1) + b + 1))
                        nc.scalar.activation(silu[b][:], gate[b][:], ACT.Sigmoid).then_inc(sigmoided, 1)

            run(in_order(0, True))
            with act.Fori(1, n_pass) as p:
                run(in_order(p, False))
            run(left_over(n_pass - 1))

        @block.vector
        def _(dve):
            def run(events):
                for kind, p, arg in events:
                    r = arg % RING if kind in ("scores", "norm") else None
                    if kind == "scores":
                        n = (arg % ST + 1) * P
                        unit = UNITS * p + arg
                        if sb_heads:
                            dve.wait_ge(sc_read, unit + 1)
                            back = stay[r][:, 0:n][:, ::-1]
                            nc.vector.tensor_tensor_scan(back, back, back, 1.0, ALU.mult, ALU.bypass).then_inc(scanned, 1)
                        else:
                            dve.wait_ge(scored, unit + 1)
                            wait_slot_free(dve, p, arg)
                            nc.vector.memset(spare[:, r:r + 1], 0.0)
                            nc.vector.tensor_tensor_reduce(
                                out=w[r][:, 0:n], in0=sc[arg % 2][:, 0:n], in1=bias[:, arg % ST, 0:n], scale=-SCALE,
                                scalar=3.0e38, op0=ALU.add, op1=ALU.min, accum_out=low[:, r:r + 1]).then_inc(sc_read, 1)
                    elif kind == "norm" and not sb_heads:
                        n = (arg % ST + 1) * P
                        unit = UNITS * p + arg
                        dve.wait_ge(exped, unit + 1)
                        nc.vector.reciprocal(inv[:, r:r + 1], den[:, r:r + 1]).then_inc(inverted, 1)
                        dve.wait_ge(inverted, unit + 1)
                        nc.vector.tensor_scalar(w[r][:, 0:n], w[r][:, 0:n], inv[:, r:r + 1], None,
                                                ALU.mult).then_inc(w_ready, 1)
                    elif kind in ("turn", "turn_v"):
                        copy_group(dve, nc.vector.tensor_copy, 1, p, kind, arg)
                    elif kind == "sumsq":
                        b, c = arg
                        use = STATS * p + STAT_NO[kind, arg]
                        dve.wait_ge(ss_done, use + 1)
                        nc.vector.tensor_scalar(var[b][:, CH * c:CH * c + CH], ss[:, 0:CH], 1.0 / HEAD_DIM, EPS,
                                                ALU.mult, ALU.add).then_inc(ss_read, 1)
                    elif kind == "root":
                        root(p, arg)
                    elif kind == "spread":
                        b, c = arg
                        use = STATS * p + STAT_NO[kind, arg]
                        n = chunk_no(p, b, c)
                        part = o[b][:, c * HALF:(c + 1) * HALF]
                        dve.wait_ge(ss_done, use + 1)
                        nc.vector.scalar_tensor_tensor(part, part, g_sb[:, ds(HEADS_PER_PASS * p + b, 1)], ss[:],
                                                       ALU.mult, ALU.mult).then_inc(ss_read, 1)
                        dve.wait_ge(ss_read, use + 1)
                        dve.wait_ge(gated, HEADS_PER_PASS * p + b + 1)
                        nc.vector.tensor_tensor(part, part, silu[b][:, c * HALF:(c + 1) * HALF],
                                                ALU.mult).then_inc(mixed, 1)

            def root(p, b):
                n = HEADS_PER_PASS * p + b
                x, r, t = var[b][:], rstd[b][:], newton[:]
                done = [ROOT_STEPS * n]

                def link(ins):
                    done[0] = done[0] + 1
                    ins.then_inc(root_step, 1)
                    dve.wait_ge(root_step, done[0])

                dve.wait_ge(ss_read, STATS * p + STAT_NO["sumsq", (b, 1)] + 1)
                link(nc.vector.tensor_scalar(t.bitcast(I32), x.bitcast(I32), 1, None, ALU.logical_shift_right))
                link(nc.vector.tensor_scalar(r.bitcast(I32), t.bitcast(I32), -1.0, float(0x5f3759df), ALU.mult, ALU.add))
                for step in range(3):
                    link(nc.vector.scalar_tensor_tensor(t, r, -0.5, r, ALU.mult, ALU.mult))
                    link(nc.vector.tensor_tensor(t, t, x, ALU.mult))
                    last = nc.vector.scalar_tensor_tensor(r, t, 1.5, r, ALU.add, ALU.mult)
                    if step < 2:
                        link(last)
                last.then_inc(rooted, 1)

            dve.wait_ge(consts_in, 16 * CONST_DMAS)
            if sb_heads:
                nc.vector.tensor_copy(ident16[:], squares[0][:, 0:P]).then_inc(converted, 1)
                nc.vector.tensor_copy(strict[:], squares[1][:, 0:P]).then_inc(converted, 1)
            else:
                for i in range(SEL0):
                    keys = (i + 1) * P
                    nc.vector.tensor_copy(bias[:, i, 0:keys], squares[i][:, 0:keys]).then_inc(converted, 1)
                dve.wait_ge(converted, 2)
            run(in_order(0, True))
            with dve.Fori(1, n_pass) as p:
                run(in_order(p, False))
            run(left_over(n_pass - 1))

        @block.tensor
        def _(pe):
            def run(events):
                for kind, p, arg in events:
                    if kind == "scores":
                        b, i = divmod(arg, ST)
                        unit = UNITS * p + arg
                        if i == 0:
                            pe.wait_ge(qkv_in[b], 16 * QKV_DMAS * (p + 1))
                        wait(pe, sc_read, unit - 1)
                        keys = (i + 1) * P
                        for c in range(0, keys, HALF):
                            end = min(c + HALF, keys)
                            masked = sb_heads and end == keys
                            mm = nc.tensor.matmul(sc[arg % 2][:, c:end], q[b][:, i * P:(i + 1) * P], k[b][:, c:end],
                                                  start=True, stop=not masked)
                            if masked:
                                mm = nc.tensor.matmul(sc[arg % 2][:, i * P:keys], ident16[:], strict[:],
                                                      start=False, stop=True)
                        mm.then_inc(scored, 1)
                    elif kind in ("turn", "turn_v"):
                        if kind == "turn":
                            src = w[arg % RING]
                            pe.wait_ge(w_ready, UNITS * p + arg + 1)
                        else:
                            src = v_t[arg]
                            pe.wait_ge(qkv_in[arg], 16 * QKV_DMAS * (p + 1))
                        for j0 in groups_of(kind, arg):
                            bank, done = group(p, kind, arg, j0)
                            wait(pe, copied[bank], done - 1)
                            for j in range(j0, j0 + tiles_in(kind, arg, j0)):
                                mm = nc.tensor.transpose(tr[bank][:, j - j0, :], src[:, j * P:(j + 1) * P], ident[:])
                            mm.then_inc(turned[bank], 1)
                    elif kind == "values":
                        b, c = arg
                        last = ST * b + CH * c + CH - 1
                        newest = GROUP_NO["turn", last, groups_of("turn", last)[-1]]
                        for no in (newest, newest - 1):
                            pe.wait_ge(copied[no % 2], half_groups * p + no // 2 + 1)
                        wait(pe, pv_read, chunk_no(p, b, c))
                        tiles = CH * c + CH
                        for j in range(tiles):
                            c0 = max(0, j - CH * c) * P
                            mm = nc.tensor.matmul(pv[:, c0:HALF], v[b][:, j, :], w_t[c][:, j, c0:HALF],
                                                  start=j == 0, stop=j == tiles - 1)
                        mm.then_inc(pv_done, 1)
                    elif kind == "sumsq":
                        b, c = arg
                        pe.wait_ge(squared, chunk_no(p, b, c) + 1)
                        wait(pe, ss_read, STATS * p + STAT_NO[kind, arg])
                        for j in range(CH):
                            mm = nc.tensor.matmul(ss[:, j:j + 1], squares[c][:, j * P:(j + 1) * P], ones[:],
                                                  start=True, stop=True)
                        mm.then_inc(ss_done, 1)
                    elif kind == "spread":
                        b, c = arg
                        pe.wait_ge(rooted, HEADS_PER_PASS * p + b + 1)
                        wait(pe, ss_read, STATS * p + STAT_NO[kind, arg])
                        for j in range(CH):
                            i = CH * c + j
                            mm = nc.tensor.matmul(ss[:, j * P:(j + 1) * P], rstd[b][:, i:i + 1].broadcast_to([P, P]),
                                                  ident[:], start=True, stop=True)
                        mm.then_inc(ss_done, 1)

            pe.wait_ge(set_up, 1)
            pe.wait_ge(consts_in, 16 * CONST_DMAS)
            pe.wait_ge(converted, 2)
            run(in_order(0, True, pe=True))
            with pe.Fori(1, n_pass) as p:
                run(in_order(p, False, pe=True))
            run(left_over(n_pass - 1, pe=True))


def output(nc, sem, mixed_t, w_out, x, final_g, out):
    NC = D_MODEL // HALF
    HT = ST // 2
    WR = 4
    RAW = 4
    FIRST_ADD = WR - 1
    with ExitStack() as ctx:
        sb = lambda name, shape, dt=F32: ctx.enter_context(nc.sbuf_tensor(name, shape, dt))
        m_raw = sb("m_raw", [P, KT, HALF])
        m_hi = sb("m_hi", [P, KT, HALF], F32R)
        m_lo = sb("m_lo", [P, KT, HALF], F32R)
        w_raw = [sb(f"wo_raw{r}", [P, HALF]) for r in range(WR)]
        w_hi = [sb(f"wo_hi{r}", [P, HALF], F32R) for r in range(WR)]
        w_lo = [sb(f"wo_lo{r}", [P, HALF], F32R) for r in range(WR)]
        x2 = sb("x2", [P, ST, D_MODEL])
        g_sb = sb("final_g_sb", [P, D_MODEL])
        squares = sb("squares_o", [P, HT, HALF], BF16)
        eps = sb("eps_o", [P, 1])
        parts = sb("parts", [P, ST, NC])
        total = sb("total", [P, ST])
        stat = [sb(f"stat{t}", [P, 8]) for t in range(ST)]
        acc = [ctx.enter_context(nc.psum_tensor(f"oacc{t}", [P, HALF], F32)) for t in range(HT)]
        m_in = [[sem(f"m_in{h}_{k}") for k in range(KT // RAW)] for h in range(2)]
        x_in, g_in, eps_set = sem("x_in"), sem("fg_in"), sem("eps_o_set")
        w_in = [sem(f"wo_in{r}") for r in range(WR)]
        m_hi_made, m_lo_made, w_hi_made, w_lo_made = sem("m_hi_made"), sem("m_lo_made"), sem("wo_hi_made"), sem("wo_lo_made")
        k_done, added, squared = sem("k_done"), sem("added"), sem("o_squared")
        totalled, rooted, scaled, fin_step, stored = sem("totalled"), sem("o_rooted"), sem("o_scaled"), sem("o_fin_step"), sem("o_stored")
        block = ctx.enter_context(nc.Block())

        STEPS = KT - 1 + HT

        def k_used(it, k):
            if k < 0:
                return k_used(it - 1, KT + k)
            return STEPS * it + (STEPS if k == KT - 1 else k + 1)

        def load_m_tiles(eng, h, k):
            eng.dma_start(m_raw[:, k:k + RAW, :],
                          mixed_t[k:k + RAW, :, h * HALF:(h + 1) * HALF].rearrange("k p s -> p k s")).then_inc(m_in[h][k // RAW], 16)

        @block.sync
        def _(sp):
            def load_w(it, c):
                for k in range(KT):
                    sp.wait_ge(w_lo_made, KT * it + k - WR + 1)
                    sp.dma_start(w_raw[k % WR][:], w_out[c, k]).then_inc(w_in[k % WR], 16)

            for k in range(0, KT, RAW):
                load_m_tiles(sp, 0, k)
                for kk in range(k, k + RAW):
                    if kk >= WR:
                        sp.wait_ge(w_lo_made, kk - WR + 1)
                    sp.dma_start(w_raw[kk % WR][:], w_out[0, kk]).then_inc(w_in[kk % WR], 16)
            with sp.Fori(1, NC) as c:
                load_w(c, c)
            load_w(NC, 0)
            with sp.Fori(1, NC) as c:
                load_w(NC + c, c)

        @block.gpsimd
        def _(pool):
            nc.gpsimd.memset(eps[:], EPS).then_inc(eps_set, 1)
            pool.wait_ge(w_lo_made, KT // 2)
            for t in range(HT):
                pool.dma_start(x2[:, t, :], x[t * P:(t + 1) * P, :]).then_inc(x_in, 16)
            pool.dma_start(g_sb[:], final_g.partition_broadcast(P)).then_inc(g_in, 16)
            pool.wait_ge(m_lo_made, KT)
            for k in range(0, KT, RAW):
                load_m_tiles(pool, 1, k)
            pool.wait_ge(x_in, 16 * HT)
            for t in range(HT, ST):
                pool.dma_start(x2[:, t, :], x[t * P:(t + 1) * P, :]).then_inc(x_in, 16)
            for t in range(ST):
                pool.wait_ge(scaled, t + 1)
                pool.dma_start(out[t * P:(t + 1) * P, :], x2[:, t, :]).then_inc(stored, 16)
            pool.wait_ge(stored, 16 * ST)

        @block.scalar
        def _(act):
            act.wait_ge(eps_set, 1)

            def m_part(h, k):
                if k % RAW == 0:
                    act.wait_ge(m_in[h][k // RAW], 16)
                if h:
                    act.wait_ge(k_done, k_used(NC - 1, k))
                nc.scalar.activation(m_hi[:, k, :], m_raw[:, k, :], ACT.Copy).then_inc(m_hi_made, 1)

            def w_part(it, k, first=False):
                r = k % WR
                act.wait_ge(w_in[r], 16 * ((KT // WR) * it + k // WR + 1))
                if not (first and k < WR):
                    act.wait_ge(k_done, k_used(it, k - WR))
                nc.scalar.activation(w_hi[r][:], w_raw[r][:], ACT.Copy).then_inc(w_hi_made, 1)

            def square(it, h, c):
                for t in range(HT):
                    act.wait_ge(added, HT * it + t + 1)
                    if not (isinstance(it, int) and it == 0):
                        act.wait_ge(squared, HT * (it - 1) + t + 1)
                    nc.scalar.activation(squares[:, t, :], x2[:, HT * h + t, ds(c * HALF, HALF)], ACT.Square,
                                         accum_out=parts[:, HT * h + t, ds(c, 1)]).then_inc(squared, 1)

            def root(h):
                for t in range(HT * h, HT * h + HT):
                    act.wait_ge(totalled, t + 1)
                    nc.scalar.activation(stat[t][:, 1:2], total[:, t:t + 1], ACT.Sqrt, bias=eps[:],
                                         scale=1.0 / D_MODEL).then_inc(rooted, 1)

            def chunk(it, h, c):
                for k in range(KT):
                    w_part(it, k)
                    if k == WR - 1:
                        square(it - 1, h, c)

            for k in range(KT):
                m_part(0, k)
                w_part(0, k, True)
            chunk(1, 0, 0)
            with act.Fori(2, NC - 1) as it:
                chunk(it, 0, it - 1)
            for k in range(KT):
                w_part(NC - 1, k)
                if k == WR - 1:
                    square(NC - 2, 0, NC - 2)
                if k >= WR:
                    m_part(1, k - WR)
            for k in range(KT):
                w_part(NC, k)
                if k < WR:
                    m_part(1, KT - WR + k)
                if k == WR - 1:
                    square(NC - 1, 0, NC - 1)
                if k == WR:
                    root(0)
            with act.Fori(1, NC) as c:
                chunk(NC + c, 1, c - 1)
            square(2 * NC - 1, 1, NC - 1)
            root(1)

        @block.vector
        def _(dve):
            def m_part(h, k):
                dve.wait_ge(m_hi_made, KT * h + k + 1)
                nc.vector.tensor_tensor(m_lo[:, k, :], m_raw[:, k, :], m_hi[:, k, :].bitcast(F32),
                                        ALU.subtract).then_inc(m_lo_made, 1)

            def w_part(it, k):
                r = k % WR
                dve.wait_ge(w_hi_made, KT * it + k + 1)
                nc.vector.tensor_tensor(w_lo[r][:], w_raw[r][:], w_hi[r][:].bitcast(F32),
                                        ALU.subtract).then_inc(w_lo_made, 1)

            def add(it, h, c):
                dve.wait_ge(x_in, 16 * HT * (h + 1))
                for t in range(HT):
                    dve.wait_ge(k_done, STEPS * it + KT + t)
                    part = x2[:, HT * h + t, ds(c * HALF, HALF)]
                    nc.vector.tensor_tensor(part, acc[t][:], part, ALU.add).then_inc(added, 1)

            def norm(t):
                s = stat[t]
                n = 5 * t
                if t == 0:
                    dve.wait_ge(g_in, 16)
                dve.wait_ge(rooted, t + 1)
                nc.vector.reciprocal(s[:, 2:3], s[:, 1:2]).then_inc(fin_step, 1)
                nc.vector.tensor_scalar(s[:, 3:4], total[:, t:t + 1], 1.0 / D_MODEL, EPS, ALU.mult, ALU.add).then_inc(fin_step, 1)
                dve.wait_ge(fin_step, n + 2)
                nc.vector.tensor_scalar(s[:, 4:5], s[:, 2:3], s[:, 2:3], s[:, 3:4], ALU.mult, ALU.mult).then_inc(fin_step, 1)
                dve.wait_ge(fin_step, n + 3)
                nc.vector.tensor_scalar(s[:, 5:6], s[:, 4:5], -0.5, 1.5, ALU.mult, ALU.add).then_inc(fin_step, 1)
                dve.wait_ge(fin_step, n + 4)
                nc.vector.tensor_tensor(s[:, 6:7], s[:, 5:6], s[:, 2:3], ALU.mult).then_inc(fin_step, 1)
                dve.wait_ge(fin_step, n + 5)
                nc.vector.scalar_tensor_tensor(x2[:, t, :], x2[:, t, :], s[:, 6:7], g_sb[:],
                                               ALU.mult, ALU.mult).then_inc(scaled, 1)

            def sum_parts(h):
                for t in range(HT * h, HT * h + HT):
                    dve.wait_ge(squared, HT * NC * h + HT * (NC - 1) + t - HT * h + 1)
                    nc.vector.tensor_reduce(total[:, t:t + 1], parts[:, t, :], AX.X, ALU.add).then_inc(totalled, 1)

            def chunk(it, h, c):
                for k in range(KT):
                    if k == FIRST_ADD:
                        add(it - 1, h, c)
                    w_part(it, k)

            for k in range(KT):
                m_part(0, k)
                w_part(0, k)
            with dve.Fori(1, NC - 1) as it:
                chunk(it, 0, it - 1)
            for k in range(KT):
                if k == FIRST_ADD:
                    add(NC - 2, 0, NC - 2)
                w_part(NC - 1, k)
                if k >= WR:
                    m_part(1, k - WR)
            for k in range(KT):
                if k == FIRST_ADD:
                    add(NC - 1, 0, NC - 1)
                w_part(NC, k)
                if k < WR:
                    m_part(1, KT - WR + k)
                if k == WR:
                    sum_parts(0)
                if k > WR and k % 2 and (k - WR) // 2 < HT:
                    norm((k - WR) // 2)
            with dve.Fori(1, NC) as c:
                chunk(NC + c, 1, c - 1)
            add(2 * NC - 1, 1, NC - 1)
            sum_parts(1)
            for t in range(HT, ST):
                norm(t)

        @block.tensor
        def _(pe):
            def chunk(it, h, c0, first=False):
                for k in range(KT):
                    r = k % WR
                    pe.wait_ge(w_lo_made, KT * it + k + 1)
                    if c0:
                        pe.wait_ge(m_lo_made, KT * h + k + 1)
                    for t in range(HT):
                        rows = slice(t * P, (t + 1) * P)
                        if k == 0 and not first:
                            pe.wait_ge(added, HT * (it - 1) + t + 1)
                        nc.tensor.matmul(acc[t][:], m_hi[:, k, rows], w_hi[r][:], start=k == 0, stop=False)
                        nc.tensor.matmul(acc[t][:], m_hi[:, k, rows], w_lo[r][:], start=False, stop=False)
                        mm = nc.tensor.matmul(acc[t][:], m_lo[:, k, rows], w_hi[r][:], start=False, stop=k == KT - 1)
                        if k == KT - 1 or t == HT - 1:
                            mm.then_inc(k_done, 1)

            for h in range(2):
                chunk(NC * h, h, True, h == 0)
                with pe.Fori(1, NC) as c:
                    chunk(NC * h + c, h, False)


def hybrid_block(nc, x, positions, norm_g, w_in, head_g, w_out, final_g, inv_freq, sin_sign, ident, strict,
                 window, out):
    proj = nc.dram_tensor("proj", [NBLK, P, SEQ], F32, kind="Internal").ap()
    trig = nc.dram_tensor("trig", [2, P, SEQ], F32, kind="Internal").ap()
    sel_bias = nc.dram_tensor("sel_bias", [ST - SEL0, P, SEQ], BF16, kind="Internal").ap()
    mixed_t = nc.dram_tensor("mixed_t", [KT, P, SEQ], F32, kind="Internal").ap()
    with ExitStack() as ctx:
        sem = lambda name: ctx.enter_context(nc.semaphore(name))
        with ExitStack() as held:
            y_hi = held.enter_context(nc.sbuf_tensor("y_hi", [P, KT, SEQ], F32R))
            y_lo = held.enter_context(nc.sbuf_tensor("y_lo", [P, KT, SEQ], F32R))
            normalise(nc, sem, x, norm_g, ident, y_hi, y_lo)
            project(nc, sem, w_in, positions, inv_freq, sin_sign, trig, window, ident, y_hi, y_lo, proj, sel_bias)
        attend(nc, sem, "sb", B_SBQ, B_SBK, B_SBV, B_SBG, proj, mixed_t[0:SB_HEADS], head_g[0], ident, strict,
               window, sel_bias)
        attend(nc, sem, "dsa", B_DQ, B_DK, B_DV, B_DG, proj, mixed_t[SB_HEADS:KT], head_g[1], ident, strict,
               window, sel_bias)
        output(nc, sem, mixed_t, w_out, x, final_g, out)


def shape_constants():
    inv_freq = np.zeros((P, 1), np.float32)
    sin_sign = np.ones((P, 1), np.float32)

    def rotation(row, half):
        freq = np.power(np.float32(ROPE_THETA), -np.arange(half, dtype=np.float32) / np.float32(half))
        inv_freq[row:row + half, 0] = inv_freq[row + half:row + 2 * half, 0] = freq
        sin_sign[row:row + half, 0] = -1.0

    rotation(0, NI)
    rotation(IDX_DIM, NI)
    rotation(ROWS_DSA.start, NQ)
    rows, cols = np.arange(P)[:, None], np.arange(2 * SEQ - P)[None, :]
    window = np.where(cols <= rows + SEQ - P, 0.0, MASKED).astype(np.float32)
    strict = np.where(np.arange(P)[None, :] < rows, 0.0, MASKED)
    return {
        "inv_freq": inv_freq, "sin_sign": sin_sign, "ident": np.eye(P, dtype=np.float32),
        "strict": strict.astype(np.float32), "window": window,
    }


def kernel(x, positions, norm_g, w_in, sb_out_g, dsa_out_g, w_out, final_g):
    import concourse.bacc as bacc
    from concourse.bass_utils import run_bass_kernel_spmd

    w = np.zeros((D_MODEL, NBLK * P), np.float32)
    w[:, :D_IN] = np.asarray(w_in)[0]
    w = w.reshape(GRAN, KG, P, NBLK, P).transpose(3, 0, 2, 1, 4)[ORDER]
    wo = np.asarray(w_out)[0].reshape(KT, P, D_MODEL // HALF, HALF).transpose(2, 0, 1, 3)
    head_g = np.stack([np.asarray(g)[0].reshape(8, P).T for g in (sb_out_g, dsa_out_g)])
    arrays = {
        "x": np.asarray(x)[0], "positions": np.asarray(positions)[0], "norm_g": np.asarray(norm_g)[0],
        "w_in": w, "head_g": head_g, "w_out": wo, "final_g": np.asarray(final_g), **shape_constants(),
    }
    arrays = {f"in_{n}": np.ascontiguousarray(a) for n, a in arrays.items()}
    nc = bacc.Bacc("TRN2", target_bir_lowering=False, num_devices=1)
    args = {n[3:]: nc.dram_tensor(n, a.shape, mybir.dt.from_np(a.dtype), kind="ExternalInput").ap()
            for n, a in arrays.items()}
    out = nc.dram_tensor("out", (SEQ, D_MODEL), F32, kind="ExternalOutput").ap()
    hybrid_block(nc, out=out, **args)
    r = run_bass_kernel_spmd(nc, [arrays], core_ids=[0])
    return r.results[0]["out"].reshape(1, SEQ, D_MODEL)
```

```python
from contextlib import ExitStack

import numpy as np
import concourse.bass as bass
from concourse import mybir

F32 = mybir.dt.float32
F32R = mybir.dt.float32r
BF16 = mybir.dt.bfloat16
I32 = mybir.dt.int32
ALU = mybir.AluOpType
ACT = mybir.ActivationFunctionType
AX = mybir.AxisListType
ds = bass.ds

P = 128
SEQ = 1024
D_MODEL = 2048
HEAD_DIM = 128
SB_HEADS = 8
DSA_HEADS = 8
KV_HEADS = 2
REP = DSA_HEADS // KV_HEADS
IDX_HEADS = 16
IDX_DIM = 64
TOPK = 256
ROPE_THETA = 500000.0
EPS = 1e-6

KT = D_MODEL // P
ST = SEQ // P
HALF = SEQ // 2
QUARTER = SEQ // 4
GRAN = 2
KG = KT // GRAN
NQ = HEAD_DIM // 4 // 2
NI = IDX_DIM // 4 // 2

D_IN = 4 * 1024 + 2 * 1024 + 2 * 256 + IDX_HEADS * IDX_DIM + IDX_DIM + IDX_HEADS
NBLK = -(-D_IN // P)
IQ0 = 52
DQ0 = 32
ROT_BLKS = DSA_HEADS + KV_HEADS
IDX_BLKS = 1 + IDX_HEADS * IDX_DIM // P
ORDER = ([NBLK - 1] + list(range(IQ0, NBLK - 1)) + list(range(DQ0, DQ0 + ROT_BLKS)) + list(range(DQ0))
         + list(range(DQ0 + ROT_BLKS, IQ0)))
B_IK, B_IQ = 0, 1
B_DQ = IDX_BLKS
B_DK = B_DQ + DSA_HEADS
B_SBQ = B_DK + KV_HEADS
B_SBK, B_SBV, B_SBG = B_SBQ + 8, B_SBQ + 16, B_SBQ + 24
B_DV = B_SBQ + 32
B_DG = B_DV + KV_HEADS
FREE_BLKS = 4
SEL0 = TOPK // P
SEL_BLKS = 8
ROUNDS = TOPK // 8
LATER_ROUNDS = 5
FIRST_ROUNDS = ROUNDS - LATER_ROUNDS * (SEL_BLKS - 2)
HEADS_AT_ONCE = IDX_HEADS // 2
assert IDX_BLKS + FREE_BLKS + (ST - SEL0) * SEL_BLKS == NBLK

ROT_PER_TILE = 2
assert ROT_PER_TILE * (ST - SEL0 - 1) == ROT_BLKS

TRIG_BLKS = 3
TWO_PI = 2 * np.pi
TWO_PI_PARTS = [6.28125, float(np.floor((TWO_PI - 6.28125) * 2.0 ** 17) / 2.0 ** 17)]
TWO_PI_PARTS.append(TWO_PI - sum(TWO_PI_PARTS))
ROUNDER = 1.5 * 2.0 ** 23
PI_BELOW = 3.1415925

MASKED = -1.0e30
TAKEN = -3.0e38
ROWS_DSA = slice(32, 64)


def normalise(nc, sem, x, norm_g, ident_d, w_in, w_raw, w_loaded, y_hi, y_lo):
    with ExitStack() as ctx:
        sb = lambda name, shape, dt=F32: ctx.enter_context(nc.sbuf_tensor(name, shape, dt))
        x_sb = [sb(f"x_sb{b}", [P, D_MODEL]) for b in range(2)]
        y_sb = [sb(f"y_sb{b}", [P, D_MODEL]) for b in range(2)]
        g_sb = sb("g_sb", [P, D_MODEL])
        squares = sb("squares", [P, D_MODEL], BF16)
        sumsq = sb("sumsq", [P, 2])
        root = sb("root", [P, 2])
        rstd = sb("rstd", [P, 2])
        eps = sb("eps_n", [P, 1])
        ident = sb("ident_n", [P, P])
        turned = [ctx.enter_context(nc.psum_tensor(f"turned{j}", [P, 4, P], F32)) for j in range(4)]
        x_in = [sem("x_in0"), sem("x_in1")]
        g_in, ident_in, eps_set = sem("g_in"), sem("ident_in"), sem("eps_set")
        summed, rooted, inverted, y_made = sem("summed"), sem("rooted"), sem("inverted"), sem("y_made")
        tile_turned, hi_made, lo_made = sem("tile_turned"), sem("hi_made"), sem("lo_made")
        block = ctx.enter_context(nc.Block())

        @block.sync
        def _(sp):
            sp.dma_start(x_sb[0][:], x[0:P, :]).then_inc(x_in[0], 16)
            sp.dma_start(g_sb[:], norm_g.partition_broadcast(P)).then_inc(g_in, 16)
            sp.dma_start(ident[:], ident_d).then_inc(ident_in, 16)
            sp.dma_start(x_sb[1][:], x[P:2 * P, :]).then_inc(x_in[1], 16)
            with sp.Fori(1, ST // 2) as i:
                for b in range(2):
                    sp.wait_ge(y_made, 2 * i + b - 1)
                    sp.dma_start(x_sb[b][:], x[ds((2 * i + b) * P, P), :]).then_inc(x_in[b], 16)
            for g in range(GRAN):
                sp.dma_start(w_raw[g][:], w_in[0, g]).then_inc(w_loaded[g], 16)

        @block.gpsimd
        def _(pool):
            nc.gpsimd.memset(eps[:], EPS).then_inc(eps_set, 1)

        @block.scalar
        def _(act):
            act.wait_ge(eps_set, 1)

            def root_of_mean(i, b):
                t = 2 * i + b
                act.wait_ge(x_in[b], 16 * (i + 1))
                nc.scalar.activation(squares[:], x_sb[b][:], ACT.Square,
                                     accum_out=sumsq[:, b:b + 1]).then_inc(summed, 1)
                act.wait_ge(summed, t + 1)
                nc.scalar.activation(root[:, b:b + 1], sumsq[:, b:b + 1], ACT.Sqrt, bias=eps[:],
                                     scale=1.0 / D_MODEL).then_inc(rooted, 1)

            def hi_parts(t):
                for j in range(4):
                    act.wait_ge(tile_turned, 4 * t + j + 1)
                    nc.scalar.activation(y_hi[:, 4 * j:4 * j + 4, ds(t * P, P)], turned[j][:],
                                         ACT.Copy).then_inc(hi_made, 1)

            root_of_mean(0, 0)
            root_of_mean(0, 1)
            hi_parts(0)
            with act.Fori(1, ST // 2) as i:
                root_of_mean(i, 0)
                hi_parts(2 * i - 1)
                root_of_mean(i, 1)
                hi_parts(2 * i)
            hi_parts(ST - 1)

        @block.vector
        def _(dve):
            dve.wait_ge(g_in, 16)

            def make_y(i, b, first):
                t = 2 * i + b
                dve.wait_ge(rooted, t + 1)
                nc.vector.reciprocal(rstd[:, b:b + 1], root[:, b:b + 1]).then_inc(inverted, 1)
                dve.wait_ge(inverted, t + 1)
                if not first:
                    dve.wait_ge(tile_turned, 4 * (t - 1))
                nc.vector.scalar_tensor_tensor(y_sb[b][:], x_sb[b][:], rstd[:, b:b + 1], g_sb[:],
                                               ALU.mult, ALU.mult).then_inc(y_made, 1)

            def lo_parts(t):
                for j in range(4):
                    dve.wait_ge(hi_made, 4 * t + j + 1)
                    nc.vector.tensor_tensor(y_lo[:, 4 * j:4 * j + 4, ds(t * P, P)], turned[j][:],
                                            y_hi[:, 4 * j:4 * j + 4, ds(t * P, P)].bitcast(F32),
                                            ALU.subtract).then_inc(lo_made, 1)

            make_y(0, 0, True)
            make_y(0, 1, True)
            lo_parts(0)
            with dve.Fori(1, ST // 2) as i:
                make_y(i, 0, False)
                lo_parts(2 * i - 1)
                make_y(i, 1, False)
                lo_parts(2 * i)
            lo_parts(ST - 1)

        @block.tensor
        def _(pe):
            pe.wait_ge(ident_in, 16)

            def turn(i, b, first):
                t = 2 * i + b
                pe.wait_ge(y_made, t + 1)
                for j in range(4):
                    if not first:
                        pe.wait_ge(lo_made, 4 * t + j - 3)
                    for k in range(4):
                        mm = nc.tensor.transpose(turned[j][:, k, :],
                                                 y_sb[b][:, (4 * j + k) * P:(4 * j + k + 1) * P], ident[:])
                    mm.then_inc(tile_turned, 1)

            turn(0, 0, True)
            turn(0, 1, False)
            with pe.Fori(1, ST // 2) as i:
                turn(i, 0, False)
                turn(i, 1, False)


def project(nc, sem, w_in, w_raw, w_loaded, positions, inv_freq, sin_sign, trig, window, ident_d, y_hi, y_lo,
            proj, sel_bias):
    with ExitStack() as ctx:
        sb = lambda name, shape, dt=F32: ctx.enter_context(nc.sbuf_tensor(name, shape, dt))
        ps = lambda name, shape: ctx.enter_context(nc.psum_tensor(name, shape, F32))
        w_hi = [sb(f"w_hi{g}", [P, KG, P], F32R) for g in range(GRAN)]
        w_lo = [sb(f"w_lo{g}", [P, KG, P], F32R) for g in range(GRAN)]
        stage = sb("stage", [P, SEQ])
        q_idx = sb("q_idx", [P, HEADS_AT_ONCE, P])
        q_swap = sb("q_swap", [P, HEADS_AT_ONCE, P])
        q_parts = sb("q_parts", [P, IDX_HEADS, P], F32R)
        trig_q = sb("trig_q", [P, 2, P])
        k_hi = sb("k_hi", [P, SEQ], F32R)
        k_lo = sb("k_lo", [P, SEQ], F32R)
        iw_t = sb("iw_t", [P, P])
        iw = sb("iw", [P, IDX_HEADS])
        relus = [sb(f"relus{b}", [P, SEQ]) for b in range(2)]
        causal = sb("causal", [P, SEQ])
        work = sb("work", [P, SEQ])
        bias_out = sb("bias_out", [P, SEQ], BF16)
        best = sb("best", [P, 8])
        freq = sb("freq", [P, 1])
        sign = sb("sign", [P, 1])
        pos, angle, turns = causal, relus[0], relus[1]
        half_sin = q_idx[:].rearrange("p h s -> p (h s)")
        keys_in = causal
        rot = sb("rot", [P, ROT_PER_TILE, QUARTER])
        rot_swap = sb("rot_swap", [P, ROT_PER_TILE, QUARTER])
        rot_table = sb("rot_table", [P, 2, QUARTER])
        ident = sb("ident_p", [P, P])
        acc = [ps(f"acc{s}", [P, HALF]) for s in range(2)]
        rel = [ps(f"rel{b}", [P, SEQ]) for b in range(2)]
        iw_ps = ps("iw_ps", [P, HALF])

        hi_made, lo_made = sem("w_hi_made"), sem("w_lo_made")
        g0_used, half_done, evacuated, stored = sem("g0_used"), sem("half_done"), sem("evacuated"), sem("stored")
        prep_in, prep_set, k_step, k_rotated, k_ready = sem("prep_in"), sem("prep_set"), sem("k_step"), sem("k_rotated"), sem("k_ready")
        k_hi_made = sem("k_hi_made")
        tile_in, queries_in, q_step, q_rotated = sem("tile_in"), sem("queries_in"), sem("q_step"), sem("q_rotated")
        q_hi_made, q_ready = sem("q_hi_made"), sem("q_ready")
        iw_turned, iw_ready = sem("iw_turned"), sem("iw_ready")
        scored, relued, summed = sem("scored"), sem("relued"), sem("head_summed")
        pos_in, trig_step, sines, table_out = sem("pos_in"), sem("trig_step"), sem("sines"), sem("table_out")
        rot_in, rot_step, rot_made, rot_stored = sem("rot_in"), sem("rot_step"), sem("rot_made"), sem("rot_stored")
        topk_step, bias_made, bias_stored = sem("topk_step"), sem("bias_made"), sem("bias_stored")
        block = ctx.enter_context(nc.Block())
        TILE_DMAS = 5
        QUERY_DMAS = 6
        STEP_OF_HEAD0 = 6
        def wait(eng, s, value):
            if not (isinstance(value, int) and value <= 0):
                eng.wait_ge(s, value)

        GROUPS = [(0, 2, HALF), (2, 4, SEQ)]
        assert SEL0 + 2 == HALF // P and SEL0 + 6 == ST
        N_SEL0 = IDX_BLKS + FREE_BLKS
        N_KEYS = N_SEL0 - 1

        @block.sync
        def _(sp):
            def load_block(n):
                for g in range(GRAN):
                    sp.wait_ge(lo_made, 2 * n + g - 1)
                    sp.dma_start(w_raw[g][:], w_in[n, g]).then_inc(w_loaded[g], 16)

            def store_block(n):
                sp.wait_ge(evacuated, 2 * n + 2)
                sp.dma_start(proj[n], stage[:]).then_inc(stored, 16)

            def load_keys():
                sp.wait_ge(stored, 16 * IDX_BLKS)
                sp.wait_ge(table_out, 32)
                sp.wait_ge(prep_set, 4)
                for half in (0, IDX_DIM):
                    sp.dma_start(keys_in[half:half + IDX_DIM, :], proj[B_IK, 0:IDX_DIM, :]).then_inc(prep_in, 16)
                    sp.dma_start(work[half:half + NI, :], proj[B_IK, NI:2 * NI, :]).then_inc(prep_in, 16)
                    sp.dma_start(work[half + NI:half + 2 * NI, :], proj[B_IK, 0:NI, :]).then_inc(prep_in, 16)
                for f in range(2):
                    sp.dma_start(relus[f][:], trig[f]).then_inc(prep_in, 16)
                    sp.wait_ge(prep_in, 16 * (7 + 2 * f))
                    sp.dma_start(relus[f][ROWS_DSA, :], trig[f, 96:128, :]).then_inc(prep_in, 16)
                sp.dma_start(ident[:], ident_d).then_inc(prep_in, 16)
                for s in range(4):
                    part = slice(32 * s, 32 * s + 32)
                    cols = slice(QUARTER * s, QUARTER * s + QUARTER)
                    sp.dma_start(rot_table[part], trig.rearrange("f p s -> p f s")[ROWS_DSA, :, cols]).then_inc(prep_in, 16)

            def load_queries(u, half_no, first=False):
                n = 2 * u + half_no
                if not first:
                    sp.wait_ge(q_ready, n)
                h0 = 2 * B_IQ + HEADS_AT_ONCE * half_no
                heads = proj.rearrange("n (e d) s -> (n e) d s", e=2)[h0:h0 + HEADS_AT_ONCE]
                queries = heads.rearrange("h d s -> d h s")[:, :, ds((u + SEL0) * P, P)]
                for half in (0, IDX_DIM):
                    sp.dma_start(q_idx[half:half + IDX_DIM], queries).then_inc(queries_in, 16)
                    sp.dma_start(q_swap[half:half + NI], queries[NI:2 * NI]).then_inc(queries_in, 16)
                    sp.dma_start(q_swap[half + NI:half + 2 * NI], queries[0:NI]).then_inc(queries_in, 16)

            def load_tile(u, first):
                q0 = (u + SEL0) * P
                if first:
                    sp.wait_ge(k_rotated, 1)
                else:
                    sp.wait_ge(scored, IDX_HEADS * u)
                    sp.wait_ge(summed, IDX_HEADS * u)
                tables = trig.rearrange("f p s -> p f s")
                sp.dma_start(trig_q[0:32], tables[0:32, :, ds(q0, P)]).then_inc(tile_in, 16)
                sp.dma_start(trig_q[ROWS_DSA], tables[96:128, :, ds(q0, P)]).then_inc(tile_in, 16)
                sp.dma_start(trig_q[64:128], tables[64:128, :, ds(q0, P)]).then_inc(tile_in, 16)
                sp.dma_start(iw_t[0:IDX_HEADS, :], proj[B_IK, IDX_DIM:IDX_DIM + IDX_HEADS, ds(q0, P)]).then_inc(tile_in, 16)
                sp.dma_start(causal[:], window[:, ds(SEQ - P - q0, SEQ)]).then_inc(tile_in, 16)

            def load_rotated(u):
                blocks = proj[ds(B_DQ + ROT_PER_TILE * (u - 1), ROT_PER_TILE)].rearrange("b p s -> p b s")
                for s in range(4):
                    p0 = 32 * s
                    cols = slice(QUARTER * s, QUARTER * s + QUARTER)
                    sp.dma_start(rot[p0:p0 + 32], blocks[0:32, :, cols]).then_inc(rot_in, 16)
                    sp.dma_start(rot_swap[p0:p0 + NQ], blocks[NQ:2 * NQ, :, cols]).then_inc(rot_in, 16)
                    sp.dma_start(rot_swap[p0 + NQ:p0 + 2 * NQ], blocks[0:NQ, :, cols]).then_inc(rot_in, 16)

            def store_rotated(u):
                blocks = proj[ds(B_DQ + ROT_PER_TILE * (u - 1), ROT_PER_TILE)].rearrange("b p s -> p b s")
                sp.wait_ge(rot_made, u)
                for s in range(4):
                    cols = slice(QUARTER * s, QUARTER * s + QUARTER)
                    sp.dma_start(blocks[0:32, :, cols], rot[32 * s:32 * s + 32]).then_inc(rot_stored, 16)

            sp.dma_start(pos[:].bitcast(I32), positions.partition_broadcast(P)).then_inc(pos_in, 16)
            sp.dma_start(freq[:], inv_freq).then_inc(pos_in, 16)
            sp.dma_start(sign[:], sin_sign).then_inc(pos_in, 16)
            with sp.Fori(1, TRIG_BLKS + 1) as n:
                load_block(n)
                store_block(n - 1)
            sp.wait_ge(trig_step, 11)
            sp.dma_start(trig[0], pos[:]).then_inc(table_out, 16)
            sp.dma_start(trig[1], turns[:]).then_inc(table_out, 16)
            with sp.Fori(TRIG_BLKS + 1, IDX_BLKS) as n:
                load_block(n)
                store_block(n - 1)
            load_block(IDX_BLKS)
            store_block(IDX_BLKS - 1)
            load_keys()
            with sp.Fori(IDX_BLKS + 1, N_SEL0) as n:
                load_block(n)
                store_block(n - 1)

            load_tile(0, True)
            load_queries(0, 0, True)

            def selected(u, first=False, last=False):
                n = N_SEL0 + SEL_BLKS * u
                load_block(n)
                load_queries(u, 1)
                store_block(n - 1)
                if not first:
                    load_rotated(u)
                load_block(n + 1)
                store_block(n)
                if not last:
                    load_tile(u + 1, False)
                    load_queries(u + 1, 0)
                if not first:
                    store_rotated(u)
                with sp.Fori(2, SEL_BLKS) as j:
                    load_block(n + j)
                    store_block(n + j - 1)
                if not first:
                    sp.wait_ge(rot_stored, 64 * u)
                sp.wait_ge(bias_made, u + 1)
                sp.dma_start(sel_bias[u], bias_out[:]).then_inc(bias_stored, 16)

            selected(0, first=True)
            with sp.Fori(1, ST - SEL0 - 1) as u:
                selected(u)
            selected(ST - SEL0 - 1, last=True)
            store_block(NBLK - 1)
            sp.wait_ge(stored, 16 * NBLK)
            sp.wait_ge(bias_stored, 16 * (ST - SEL0))

        @block.gpsimd
        def _(pool):
            nc.gpsimd.memset(work[:], 0.0).then_inc(prep_set, 1)
            nc.gpsimd.memset(q_swap[:], 0.0).then_inc(prep_set, 1)
            nc.gpsimd.memset(iw_t[:], 0.0).then_inc(prep_set, 1)
            nc.gpsimd.memset(bias_out[:], 0.0).then_inc(prep_set, 1)

        @block.scalar
        def _(act):
            def hi_part(n, g, first=False):
                act.wait_ge(w_loaded[g], 16 * (n + 1))
                if not first:
                    if g == 0:
                        act.wait_ge(g0_used, n)
                    else:
                        act.wait_ge(half_done, 2 * n)
                nc.scalar.activation(w_hi[g][:], w_raw[g][:], ACT.Copy).then_inc(hi_made, 1)

            def evacuate(n, s, first=False):
                act.wait_ge(half_done, 2 * n + s + 1)
                if s == 0 and not first:
                    act.wait_ge(stored, 16 * n)
                nc.scalar.activation(stage[:, s * HALF:(s + 1) * HALF], acc[s][:], ACT.Copy).then_inc(evacuated, 1)

            def split_and_finish(n):
                hi_part(n, 0)
                hi_part(n, 1)
                evacuate(n - 1, 1)

            def query_parts(u, half_no):
                n = 2 * u + half_no
                act.wait_ge(q_rotated, n + 1)
                if half_no == 0:
                    wait(act, scored, IDX_HEADS * u)
                nc.scalar.activation(q_parts[:, HEADS_AT_ONCE * half_no:HEADS_AT_ONCE * (half_no + 1), :], q_idx[:],
                                     ACT.Copy).then_inc(q_hi_made, 1)

            def relu(u, h, keys, first):
                act.wait_ge(scored, IDX_HEADS * u + h + 1)
                if not (first and h < 2):
                    act.wait_ge(summed, IDX_HEADS * u + h - 1)
                nc.scalar.activation(relus[h % 2][:, 0:keys], rel[h % 2][:, 0:keys],
                                     ACT.Relu).then_inc(relued, 1)

            hi_part(0, 0, True)
            hi_part(0, 1, True)
            evacuate(0, 0, True)
            for n in range(1, TRIG_BLKS + 1):
                split_and_finish(n)
                evacuate(n, 0)
                if n == TRIG_BLKS - 1:
                    act.wait_ge(trig_step, 8)
                    nc.scalar.activation(turns[:], angle[:], ACT.Sin).then_inc(sines, 1)
                    nc.scalar.activation(half_sin, angle[:], ACT.Sin, scale=0.5).then_inc(sines, 1)
            with act.Fori(TRIG_BLKS + 1, N_KEYS) as n:
                split_and_finish(n)
                evacuate(n, 0)
            act.wait_ge(k_rotated, 1)
            nc.scalar.activation(k_hi[:], work[:], ACT.Copy).then_inc(k_hi_made, 1)
            with act.Fori(N_KEYS, N_SEL0) as n:
                split_and_finish(n)
                evacuate(n, 0)

            def selected(u, keys, first):
                n = N_SEL0 + SEL_BLKS * u
                query_parts(u, 0)
                hi_part(n, 0)
                hi_part(n, 1)
                evacuate(n - 1, 1)
                query_parts(u, 1)
                if first:
                    act.wait_ge(k_ready, 1)
                for h in range(IDX_HEADS):
                    if STEP_OF_HEAD0 + h == KT:
                        evacuate(n, 0)
                    relu(u, h, keys, first)
                with act.Fori(1, SEL_BLKS) as j:
                    split_and_finish(n + j)
                    evacuate(n + j, 0)

            for u0, count, keys in GROUPS:
                if u0 == 0:
                    selected(0, keys, True)
                    u0, count = 1, count - 1
                with act.Fori(u0, u0 + count) as u:
                    selected(u, keys, False)
            evacuate(NBLK - 1, 1)

        @block.vector
        def _(dve):
            def lo_part(n, g):
                dve.wait_ge(hi_made, 2 * n + g + 1)
                nc.vector.tensor_tensor(w_lo[g][:], w_raw[g][:], w_hi[g][:].bitcast(F32),
                                        ALU.subtract).then_inc(lo_made, 1)

            def trig_tables():
                done = [0]

                def link(ins):
                    done[0] += 1
                    ins.then_inc(trig_step, 1)
                    dve.wait_ge(trig_step, done[0])

                def part(which):
                    if which == 0:
                        dve.wait_ge(pos_in, 48)
                        link(nc.vector.tensor_copy(pos[:], pos[:].bitcast(I32)))
                        link(nc.vector.tensor_scalar(angle[:], pos[:], freq[:], None, ALU.mult))
                        link(nc.vector.tensor_scalar(turns[:], angle[:], 1.0 / TWO_PI, ROUNDER, ALU.mult, ALU.add))
                        link(nc.vector.tensor_scalar(turns[:], turns[:], ROUNDER, None, ALU.subtract))
                    elif which == 1:
                        for two_pi_part in TWO_PI_PARTS:
                            link(nc.vector.scalar_tensor_tensor(angle[:], turns[:], -two_pi_part, angle[:],
                                                                ALU.mult, ALU.add))
                        link(nc.vector.tensor_scalar(angle[:], angle[:], PI_BELOW, -PI_BELOW, ALU.min, ALU.max))
                    elif which == 2:
                        dve.wait_ge(sines, 2)
                        link(nc.vector.tensor_tensor(pos[:], half_sin, half_sin, ALU.mult))
                        link(nc.vector.tensor_scalar(pos[:], pos[:], -2.0, 1.0, ALU.mult, ALU.add))
                        nc.vector.tensor_scalar(turns[:], turns[:], sign[:], None, ALU.mult).then_inc(trig_step, 1)

                return part

            def rotate_keys():
                dve.wait_ge(prep_in, 16 * 15)
                nc.vector.tensor_tensor(work[:], work[:], relus[1][:], ALU.mult).then_inc(k_step, 1)
                nc.vector.tensor_tensor(keys_in[:], keys_in[:], relus[0][:], ALU.mult).then_inc(k_step, 1)
                dve.wait_ge(k_step, 2)
                nc.vector.tensor_tensor(work[:], keys_in[:], work[:], ALU.add).then_inc(k_rotated, 1)

            def split_keys():
                dve.wait_ge(k_hi_made, 1)
                nc.vector.tensor_tensor(k_lo[:], work[:], k_hi[:].bitcast(F32), ALU.subtract).then_inc(k_ready, 1)

            def rotate_queries(u, half_no):
                n = 2 * u + half_no
                if half_no == 0:
                    dve.wait_ge(tile_in, 16 * TILE_DMAS * (u + 1))
                dve.wait_ge(queries_in, 16 * QUERY_DMAS * (n + 1))
                for f, q in ((0, q_idx), (1, q_swap)):
                    table = trig_q[:, f:f + 1, :].broadcast_to([P, HEADS_AT_ONCE, P])
                    nc.vector.tensor_tensor(q[:], q[:], table, ALU.mult).then_inc(q_step, 1)
                dve.wait_ge(q_step, 2 * (n + 1))
                nc.vector.tensor_tensor(q_idx[:], q_idx[:], q_swap[:], ALU.add).then_inc(q_rotated, 1)

            def query_lo(u, half_no):
                n = 2 * u + half_no
                dve.wait_ge(q_hi_made, n + 1)
                lo = q_parts[IDX_DIM:P, HEADS_AT_ONCE * half_no:HEADS_AT_ONCE * (half_no + 1), :]
                nc.vector.tensor_tensor(lo, q_idx[IDX_DIM:P], lo.bitcast(F32), ALU.subtract).then_inc(q_ready, 1)

            def rotate_blocks(u):
                dve.wait_ge(rot_in, 16 * 12 * u)
                for f, q in ((0, rot), (1, rot_swap)):
                    table = rot_table[:, f:f + 1, :].broadcast_to([P, ROT_PER_TILE, QUARTER])
                    nc.vector.tensor_tensor(q[:], q[:], table, ALU.mult).then_inc(rot_step, 1)
                dve.wait_ge(rot_step, 2 * u)
                nc.vector.tensor_tensor(rot[:], rot[:], rot_swap[:], ALU.add).then_inc(rot_made, 1)

            def sum_heads(u, keys):
                dve.wait_ge(iw_turned, u + 1)
                nc.vector.tensor_scalar(iw[:], iw_ps[:, 0:IDX_HEADS], IDX_DIM ** -0.5 * IDX_HEADS ** -0.5,
                                        None, ALU.mult).then_inc(iw_ready, 1)
                dve.wait_ge(iw_ready, u + 1)
                for h in range(IDX_HEADS):
                    dve.wait_ge(relued, IDX_HEADS * u + h + 1)
                    if h:
                        dve.wait_ge(summed, IDX_HEADS * u + h)
                    so_far = work if h else causal
                    nc.vector.scalar_tensor_tensor(work[:, 0:keys], relus[h % 2][:, 0:keys], iw[:, h:h + 1],
                                                   so_far[:, 0:keys], ALU.mult, ALU.add).then_inc(summed, 1)

            def rounds(m, keys):
                for r in range(m):
                    nc.vector.max(best[:], work[:, 0:keys]).then_inc(topk_step, 1)
                    dve.wait_ge(topk_step, 2 * r + 1)
                    nc.vector.match_replace(work[:, 0:keys], best[:], work[:, 0:keys], TAKEN).then_inc(topk_step, 1)
                    dve.wait_ge(topk_step, 2 * r + 2)
                dve.sem_clear(topk_step)

            lo_part(0, 0)
            lo_part(0, 1)
            trig_ops = trig_tables()
            for n in range(1, TRIG_BLKS + 1):
                lo_part(n, 0)
                lo_part(n, 1)
                trig_ops(n - 1)
            with dve.Fori(TRIG_BLKS + 1, N_KEYS) as n:
                lo_part(n, 0)
                lo_part(n, 1)
            rotate_keys()
            split_keys()
            with dve.Fori(N_KEYS, N_SEL0) as n:
                lo_part(n, 0)
                lo_part(n, 1)

            def selected(u, keys, first):
                n = N_SEL0 + SEL_BLKS * u
                rotate_queries(u, 0)
                query_lo(u, 0)
                lo_part(n, 0)
                lo_part(n, 1)
                rotate_queries(u, 1)
                query_lo(u, 1)
                sum_heads(u, keys)
                dve.wait_ge(summed, IDX_HEADS * (u + 1))
                if not first:
                    rotate_blocks(u)
                lo_part(n + 1, 0)
                lo_part(n + 1, 1)
                rounds(FIRST_ROUNDS, keys)
                with dve.Fori(2, SEL_BLKS) as j:
                    lo_part(n + j, 0)
                    rounds(LATER_ROUNDS // 2, keys)
                    lo_part(n + j, 1)
                    rounds(LATER_ROUNDS - LATER_ROUNDS // 2, keys)
                if not first:
                    dve.wait_ge(bias_stored, 16 * u)
                nc.vector.tensor_scalar(bias_out[:, 0:keys], work[:, 0:keys], 0.5 * TAKEN, MASKED,
                                        ALU.is_gt, ALU.mult).then_inc(bias_made, 1)

            for u0, count, keys in GROUPS:
                if u0 == 0:
                    selected(0, keys, True)
                    u0, count = 1, count - 1
                with dve.Fori(u0, u0 + count) as u:
                    selected(u, keys, False)

        @block.tensor
        def _(pe):
            def project_block(n, first=False, beside=None):
                for s in range(2):
                    cols = slice(s * HALF, (s + 1) * HALF)
                    if not first:
                        pe.wait_ge(evacuated, 2 * n + s - 1)
                    for g in range(GRAN):
                        if s == 0:
                            pe.wait_ge(lo_made, 2 * n + g + 1)
                        for k in range(KG):
                            kk = g * KG + k
                            nc.tensor.matmul(acc[s][:], w_hi[g][:, k, :], y_hi[:, kk, cols],
                                             start=kk == 0, stop=False)
                            nc.tensor.matmul(acc[s][:], w_hi[g][:, k, :], y_lo[:, kk, cols],
                                             start=False, stop=False)
                            mm = nc.tensor.matmul(acc[s][:], w_lo[g][:, k, :], y_hi[:, kk, cols],
                                                  start=False, stop=kk == KT - 1)
                            if g == 0 and s == 1 and k == KG - 1:
                                mm.then_inc(g0_used, 1)
                            if kk == KT - 1:
                                mm.then_inc(half_done, 1)
                            if beside:
                                beside(KT * s + kk)

            def score(u, step, keys, first):
                h = step - STEP_OF_HEAD0
                if h == -1:
                    pe.wait_ge(tile_in, 16 * TILE_DMAS * (u + 1))
                    if first:
                        pe.wait_ge(prep_in, 16 * 15)
                    else:
                        pe.wait_ge(iw_ready, u)
                    nc.tensor.transpose(iw_ps[:, 0:P], iw_t[:], ident[:]).then_inc(iw_turned, 1)
                if not 0 <= h < IDX_HEADS:
                    return
                if h % HEADS_AT_ONCE == 0:
                    pe.wait_ge(q_ready, 2 * u + h // HEADS_AT_ONCE + 1)
                    if first:
                        pe.wait_ge(k_ready, 1)
                if not (first and h < 2):
                    pe.wait_ge(relued, IDX_HEADS * u + h - 1)
                for c in range(0, keys, HALF):
                    out = rel[h % 2][:, c:c + HALF]
                    nc.tensor.matmul(out, q_parts[:, h, :], k_hi[:, c:c + HALF], start=True, stop=False)
                    mm = nc.tensor.matmul(out, q_parts[:, h, :], k_lo[:, c:c + HALF], start=False, stop=True)
                mm.then_inc(scored, 1)

            project_block(0, True)
            with pe.Fori(1, N_SEL0) as n:
                project_block(n)

            def selected(u, keys, first):
                n = N_SEL0 + SEL_BLKS * u
                project_block(n, beside=lambda step: score(u, step, keys, first))
                with pe.Fori(1, SEL_BLKS) as j:
                    project_block(n + j)

            for u0, count, keys in GROUPS:
                if u0 == 0:
                    selected(0, keys, True)
                    u0, count = 1, count - 1
                with pe.Fori(u0, u0 + count) as u:
                    selected(u, keys, False)


WO_RING = 4
M_FIRST = 4
HEADS_PER_PASS = 2
SB, DSA = range(HEADS_PER_PASS)
PASSES = SB_HEADS
assert SB_HEADS == DSA_HEADS
UNITS = HEADS_PER_PASS * ST
SCALE = HEAD_DIM ** -0.5
MIN_COLS = 256
CH = HALF // P
RING = 8
STAY_RING = 4
TURNED_RING = 4
LAG = 3
ROOT_LAG = 3
SCALE_LAG = [4, 5]
GATE_AT = [7, 21]
SPLITS = [(12, SB, 0), (13, SB, 1), (1, DSA, 0), (3, DSA, 1)]


def events_of_pass(pe):
    ev = []
    for u in range(UNITS):
        ev.append((u, 1 if pe else 5, "scores", u))
        ev.append((u + 2, 0, "norm", u))
        ev.append((u + LAG, 2, "turn", u))
        ev.append((u + LAG + 1, 3, "value", u))
    for b in range(HEADS_PER_PASS):
        head_end = ST * b + ST - 1 + LAG
        ev.append((ST * b + LAG - 1, 4, "turn_v", b))
        for c in range(2):
            chunk_end = ST * b + CH * c + CH - 1 + LAG
            ev.append((chunk_end + 1, 6, "evacuate", (b, c)))
            ev.append((chunk_end + 2, 7, "sum", (b, c)))
            ev.append((head_end + SCALE_LAG[c], 9, "scale", (b, c)))
            ev.append((head_end + SCALE_LAG[c] + 1, 3.5, "turn_o", (b, c)))
            ev.append((head_end + SCALE_LAG[c] + 1, 9.5, "finish", (b, c)))
        ev.append((head_end + ROOT_LAG, 8, "root", b))
        ev.append((GATE_AT[b], 8, "gate", b))
    for step, b, operand in SPLITS:
        ev.append((step, 7, "split_hi", (b, operand)))
        ev.append((step + 1, 7, "split_lo", (b, operand)))
    return sorted(ev, key=lambda e: (e[0] % UNITS, e[1], -e[0]))


EVENTS = {pe: events_of_pass(pe) for pe in (False, True)}
IN_TIME = sorted(EVENTS[True], key=lambda e: e[:2])


def groups_of(kind, arg):
    if kind == "turn_v":
        return [0, CH]
    return [0, CH] if arg % ST >= CH else [0]


GROUP_NO = {}
for _, _, kind_, arg_ in IN_TIME:
    if kind_ in ("turn", "turn_v"):
        for j0_ in groups_of(kind_, arg_):
            GROUP_NO[kind_, arg_, j0_] = len(GROUP_NO)
GROUPS_PER_PASS = len(GROUP_NO)
assert GROUPS_PER_PASS % 2 == 0
ROOT_STEPS = 11


def in_order(p, first=False, last=False, pe=False):
    for step, _, kind, arg in EVENTS[pe]:
        if kind in ("split_hi", "split_lo") and arg[0] == SB:
            if not last:
                yield kind, p + 1, arg
        elif step < UNITS:
            yield kind, p, arg
        elif not first:
            yield kind, p - 1, arg


def left_over(p, pe=False):
    for step, _, kind, arg in EVENTS[pe]:
        if step >= UNITS:
            yield kind, p, arg


def attend(nc, sem, proj, mixed_t, head_g, ident_d, strict_d, window, sel_bias, w_out, m_first, m_first_in, wo_raw,
           wo_in):
    half_groups = GROUPS_PER_PASS // 2
    with ExitStack() as ctx:
        sb = lambda name, shape, dt=F32: ctx.enter_context(nc.sbuf_tensor(f"a_{name}", shape, dt))
        ps = lambda name, shape: ctx.enter_context(nc.psum_tensor(f"a_{name}", shape, F32))
        sm = lambda name: sem(f"a_{name}")
        both = range(HEADS_PER_PASS)
        qk = [[sb(f"qk{b}{x}", [P, SEQ]) for x in range(2)] for b in both]
        qk_hi = [[sb(f"qk_hi{b}{x}", [P, SEQ], F32R) for x in range(2)] for b in both]
        qk_lo = [[sb(f"qk_lo{b}{x}", [P, SEQ], F32R) for x in range(2)] for b in both]
        v_t = [sb(f"v_t{b}", [P, SEQ]) for b in both]
        gate = [sb(f"gate{b}", [P, SEQ]) for b in both]
        v = [sb(f"v{b}", [P, ST, P]) for b in both]
        w = [sb(f"w{r}", [P, SEQ]) for r in range(RING)]
        stay = [sb(f"stay{r}", [P, SEQ]) for r in range(STAY_RING)]
        w_t = [sb(f"w_t{r}", [P, ST, P]) for r in range(TURNED_RING)]
        o_q = [sb(f"o_q{b}", [P, ST, P]) for b in both]
        o = [sb(f"o{b}", [P, SEQ]) for b in both]
        var = [sb(f"var{b}", [P, ST]) for b in both]
        rstd = [sb(f"rstd{b}", [P, ST]) for b in both]
        newton = sb("newton", [P, ST])
        silu = [sb(f"silu{b}", [P, SEQ]) for b in both]
        squares = [sb(f"squares{c}", [P, HALF]) for c in range(2)]
        ident = sb("ident", [P, P])
        g_sb = [sb(f"g{b}", [P, 8]) for b in both]
        ident16 = sb("ident16", [P, P], BF16)
        strict = sb("strict", [P, P], BF16)
        bias = sb("bias", [P, ST, SEQ], BF16)
        low = sb("low", [P, RING])
        den = sb("den", [P, RING])
        spare = sb("spare", [P, RING])
        inv = sb("inv", [P, RING])
        sc = [ps(f"sc{r}", [P, SEQ]) for r in range(2)]
        tr = [ps(f"tr{r}", [P, CH, P]) for r in range(2)]
        pv = ps("pv", [P, CH, P])
        o_tr = ps("o_tr", [P, CH, P])

        qk_in = [[sm(f"qk_in{b}{x}") for x in range(2)] for b in both]
        v_in = [sm(f"v_in{b}") for b in both]
        gate_in = [sm(f"gate_in{b}") for b in both]
        hi_made = [sm(f"hi_made{b}") for b in both]
        lo_made = [sm(f"lo_made{b}") for b in both]
        small_in, consts_in, bias_in = sm("small_in"), sm("consts_in"), sm("bias_in")
        scored, scanned = sm("scored"), sm("scanned")
        sc_read = [sm(f"sc_read{b}") for b in both]
        w_ready = [sm(f"w_ready{b}") for b in both]
        converted = sm("converted")
        exped, inverted = sm("exped"), sm("inverted")
        turned = [sm(f"turned{r}") for r in range(2)]
        copied = [sm(f"copied{r}") for r in range(2)]
        valued, pv_read, squared, summed = sm("valued"), sm("pv_read"), sm("squared"), sm("summed")
        o_scaled, o_turned = sm("o_scaled"), sm("o_turned")
        sigmoided, root_step, rooted, gated = sm("sigmoided"), sm("root_step"), sm("rooted"), sm("gated")
        mixed, o_free = sm("mixed"), [sm(f"o_free{b}") for b in both]
        block = ctx.enter_context(nc.Block())
        CONST_DMAS = 2

        def wait(eng, s, value):
            if not (isinstance(value, int) and value <= 0):
                eng.wait_ge(s, value)

        def group(p, kind, arg, j0):
            no = GROUP_NO[kind, arg, j0]
            return no % 2, half_groups * p + no // 2 + 1

        def tiles_in(kind, arg, j0):
            return CH if kind == "turn_v" else min(CH, arg % ST + 1 - j0)

        def wait_slot_free(eng, p, u):
            pu, uu = (p, u - RING) if u >= RING else (p - 1, u - RING + UNITS)
            bank, done = group(pu, "turn", uu, groups_of("turn", uu)[-1])
            wait(eng, turned[bank], done)

        def chunk_no(p, b, c):
            return 2 * HEADS_PER_PASS * p + 2 * b + c

        def copy_group(eng, op, bank, p, kind, arg):
            for j0 in groups_of(kind, arg):
                at, done = group(p, kind, arg, j0)
                if at != bank:
                    continue
                n = tiles_in(kind, arg, j0)
                wait(eng, turned[bank], done)
                if kind == "turn_v":
                    dst = v[arg][:, j0:j0 + n, :]
                else:
                    wait(eng, valued, UNITS * p + arg - TURNED_RING + 1)
                    dst = w_t[arg % TURNED_RING][:, j0:j0 + n, :]
                op(dst, tr[bank][:, 0:n, :]).then_inc(copied[bank], 1)

        def wait_units(eng, sems, p, u):
            if u < 0:
                p, u = p - 1, u + UNITS
            wait(eng, sems[u // ST], ST * p + u % ST + 1 if not isinstance(p, int) or p >= 0 else 0)

        @block.sync
        def _(sp):
            def load_operands(p, b, kv, first=False):
                n_q, n_k, n_v = ((B_SBQ + p, B_SBK + p, B_SBV + p) if b == SB
                                 else (B_DQ + p, B_DK + kv, B_DV + kv))
                if not first:
                    sp.wait_ge(lo_made[b], 2 * p)
                sp.dma_start(qk[b][0][:], proj[n_q]).then_inc(qk_in[b][0], 16)
                sp.dma_start(qk[b][1][:], proj[n_k]).then_inc(qk_in[b][1], 16)
                if not first:
                    sp.wait_ge(scored, UNITS * (p - 1) + ST * b + LAG + 1)
                sp.dma_start(v_t[b][:], proj[n_v]).then_inc(v_in[b], 16)

            def load_gate(p, b, first=False):
                if not first:
                    sp.wait_ge(gated, HEADS_PER_PASS * (p - 1) + b + 1)
                sp.dma_start(gate[b][:], proj[(B_SBG, B_DG)[b] + p]).then_inc(gate_in[b], 16)

            def store(p, b):
                sp.wait_ge(mixed, 2 * (HEADS_PER_PASS * p + b + 1))
                sp.dma_start(mixed_t[SB_HEADS * b + p], o[b][:]).then_inc(o_free[b], 16)

            sp.dma_start(ident[:], ident_d).then_inc(small_in, 16)
            sp.dma_start(squares[0][:, 0:P], ident_d).then_inc(small_in, 16)
            sp.dma_start(squares[0][:, P:2 * P], strict_d).then_inc(small_in, 16)
            load_operands(0, SB, None, True)
            for i in range(SEL0):
                keys = (i + 1) * P
                sp.dma_start(squares[1][:, i * P:i * P + keys], window[:, SEQ - keys:SEQ]).then_inc(consts_in, 16)
            for b in both:
                sp.dma_start(g_sb[b][:], head_g[b]).then_inc(o_free[b], 16)
            load_operands(0, DSA, 0, True)
            for i in range(SEL0, ST):
                keys = (i + 1) * P
                sp.dma_start(bias[:, i, 0:keys], sel_bias[i - SEL0, :, 0:keys]).then_inc(bias_in, 16)
            for b in both:
                load_gate(0, b, True)

            def steady(p, kv, first=False):
                load_operands(p + 1, SB, None)
                if not first:
                    store(p - 1, SB)
                    load_gate(p, DSA)
                load_operands(p + 1, DSA, kv)
                if not first:
                    store(p - 1, DSA)
                load_gate(p + 1, SB)

            steady(0, 0, True)
            with sp.Fori(1, REP - 1) as p:
                steady(p, 0)
            with sp.Fori(REP - 1, PASSES - 1) as p:
                steady(p, 1)
            store(PASSES - 2, SB)
            load_gate(PASSES - 1, DSA)
            store(PASSES - 2, DSA)
            sp.wait_ge(o_free[SB], 16 * (M_FIRST + 1))
            for k in range(M_FIRST):
                sp.dma_start(m_first[:, k, :], mixed_t[k, :, 0:HALF]).then_inc(m_first_in, 16)
            for r in range(WO_RING):
                sp.dma_start(wo_raw[r][:], w_out[0, r]).then_inc(wo_in[r], 16)
            for b in both:
                store(PASSES - 1, b)
            for b in both:
                sp.wait_ge(o_free[b], 16 * (PASSES + 1))

        def lo_part(eng, unit, p, b, x):
            eng.wait_ge(hi_made[b], 2 * p + x + 1)
            unit.tensor_tensor(qk_lo[b][x][:], qk[b][x][:], qk_hi[b][x][:].bitcast(F32),
                               ALU.subtract).then_inc(lo_made[b], 1)

        def pool_events(pool, events):
            for kind, p, arg in events:
                if kind == "split_lo" and arg[0] == SB:
                    lo_part(pool, nc.gpsimd, p, *arg)
                if kind == "scores" and arg < ST:
                    r, n = arg % RING, (arg + 1) * P
                    pool.wait_ge(scanned, ST * p + arg + 1)
                    nc.gpsimd.tensor_tensor(w[r][:, 0:n - 1], w[r][:, 0:n - 1], stay[arg % STAY_RING][:, 1:n],
                                            ALU.mult).then_inc(w_ready[SB], 1)
                elif kind == "evacuate":
                    b, c = arg
                    no = chunk_no(p, b, c)
                    part = o_q[b][:, CH * c:CH * c + CH, :].rearrange("p j d -> p (j d)")
                    pool.wait_ge(pv_read, no + 1)
                    wait(pool, summed, no - 1)
                    nc.gpsimd.tensor_tensor(squares[c][:], part, part, ALU.mult).then_inc(squared, 1)
                elif kind == "gate":
                    pool.wait_ge(sigmoided, HEADS_PER_PASS * p + arg + 1)
                    nc.gpsimd.tensor_tensor(silu[arg][:], silu[arg][:], gate[arg][:], ALU.mult).then_inc(gated, 1)

        @block.gpsimd
        def _(pool):
            pool.wait_ge(converted, 4)
            pool_events(pool, in_order(0, first=True))
            with pool.Fori(1, PASSES - 1) as p:
                pool_events(pool, in_order(p))
            pool_events(pool, in_order(PASSES - 1, last=True))
            pool_events(pool, left_over(PASSES - 1))

        @block.scalar
        def _(act):
            def copy(dst, src):
                return nc.scalar.activation(dst, src, ACT.Copy)

            def hi_part(p, b, x):
                act.wait_ge(qk_in[b][x], 16 * (p + 1))
                if x == 0:
                    wait(act, scored, UNITS * (p - 1) + ST * (b + 1))
                copy(qk_hi[b][x][:], qk[b][x][:]).then_inc(hi_made[b], 1)

            def run(events):
                for kind, p, arg in events:
                    if kind == "scores":
                        r, n = arg % RING, (arg % ST + 1) * P
                        unit = UNITS * p + arg
                        if arg < ST:
                            act.wait_ge(scored, unit + 1)
                            wait_slot_free(act, p, arg)
                            wait(act, w_ready[SB], ST * p + arg - STAY_RING + 1)
                            nc.scalar.activation(w[r][:, 0:n], sc[arg % 2][:, 0:n], ACT.Sigmoid, scale=SCALE)
                            nc.scalar.activation(stay[arg % STAY_RING][:, 0:n], sc[arg % 2][:, 0:n], ACT.Sigmoid,
                                                 scale=-SCALE).then_inc(sc_read[SB], 1)
                        else:
                            act.wait_ge(sc_read[DSA], ST * p + arg - ST + 1)
                            nc.scalar.activation(w[r][:, 0:n], w[r][:, 0:n], ACT.Exp, bias=low[:, r:r + 1],
                                                 scale=-1.0, accum_out=den[:, r:r + 1]).then_inc(exped, 1)
                    elif kind in ("turn", "turn_v"):
                        copy_group(act, copy, 0, p, kind, arg)
                    elif kind == "split_hi":
                        hi_part(p, *arg)
                    elif kind == "evacuate":
                        b, c = arg
                        act.wait_ge(valued, UNITS * p + ST * b + CH * c + CH)
                        wait(act, o_turned, chunk_no(p, SB, 1) + 1 if (b, c) == (DSA, 1)
                             else chunk_no(p - 1, b, c) + 1)
                        copy(o_q[b][:, CH * c:CH * c + CH, :], pv[:]).then_inc(pv_read, 1)
                    elif kind == "gate":
                        b = arg
                        act.wait_ge(gate_in[b], 16 * (p + 1))
                        wait(act, mixed, 2 * (HEADS_PER_PASS * (p - 1 + b) + 1))
                        nc.scalar.activation(silu[b][:], gate[b][:], ACT.Sigmoid).then_inc(sigmoided, 1)

            for x in range(2):
                hi_part(0, SB, x)
            run(in_order(0, first=True))
            with act.Fori(1, PASSES - 1) as p:
                run(in_order(p))
            run(in_order(PASSES - 1, last=True))
            run(left_over(PASSES - 1))

        @block.vector
        def _(dve):
            def run(events):
                for kind, p, arg in events:
                    r = arg % RING if kind in ("scores", "norm") else None
                    if kind == "scores":
                        n = (arg % ST + 1) * P
                        unit = UNITS * p + arg
                        if arg < ST:
                            dve.wait_ge(sc_read[SB], ST * p + arg + 1)
                            back = stay[arg % STAY_RING][:, 0:n][:, ::-1]
                            nc.vector.tensor_tensor_scan(back, back, back, 1.0, ALU.mult, ALU.bypass).then_inc(scanned, 1)
                        else:
                            dve.wait_ge(scored, unit + 1)
                            if isinstance(p, int) and p == 0 and arg == ST:
                                dve.wait_ge(bias_in, 16 * (ST - SEL0))
                            wait_slot_free(dve, p, arg)
                            nc.vector.memset(spare[:, r:r + 1], 0.0)
                            nc.vector.tensor_tensor_reduce(
                                out=w[r][:, 0:n], in0=sc[arg % 2][:, 0:n], in1=bias[:, arg % ST, 0:n], scale=-SCALE,
                                scalar=3.0e38, op0=ALU.add, op1=ALU.min, accum_out=low[:, r:r + 1]).then_inc(sc_read[DSA], 1)
                    elif kind == "norm" and arg >= ST:
                        n = (arg % ST + 1) * P
                        unit = ST * p + arg - ST
                        dve.wait_ge(exped, unit + 1)
                        nc.vector.reciprocal(inv[:, r:r + 1], den[:, r:r + 1]).then_inc(inverted, 1)
                        dve.wait_ge(inverted, unit + 1)
                        nc.vector.tensor_scalar(w[r][:, 0:n], w[r][:, 0:n], inv[:, r:r + 1], None,
                                                ALU.mult).then_inc(w_ready[DSA], 1)
                    elif kind == "split_lo" and arg[0] == DSA:
                        lo_part(dve, nc.vector, p, *arg)
                    elif kind in ("turn", "turn_v"):
                        copy_group(dve, nc.vector.tensor_copy, 1, p, kind, arg)
                    elif kind == "sum":
                        b, c = arg
                        dve.wait_ge(squared, chunk_no(p, b, c) + 1)
                        nc.vector.tensor_reduce(var[b][:, CH * c:CH * c + CH],
                                                squares[c][:].rearrange("p (j d) -> p j d", j=CH),
                                                AX.X, ALU.add).then_inc(summed, 1)
                    elif kind == "root":
                        root(p, arg)
                    elif kind == "scale":
                        b, c = arg
                        if c == 0:
                            dve.wait_ge(rooted, HEADS_PER_PASS * p + b + 1)
                        part = o_q[b][:, CH * c:CH * c + CH, :]
                        by_query = rstd[b][:, CH * c:CH * c + CH].rearrange("p (j a) -> p j a", a=1)
                        nc.vector.tensor_tensor(part, part, by_query.broadcast_to([P, CH, P]),
                                                ALU.mult).then_inc(o_scaled, 1)
                    elif kind == "finish":
                        b, c = arg
                        if c == 0:
                            dve.wait_ge(o_free[b], 16 * (p + 1))
                            dve.wait_ge(gated, HEADS_PER_PASS * p + b + 1)
                        dve.wait_ge(o_turned, chunk_no(p, b, c) + 1)
                        cols = slice(c * HALF, (c + 1) * HALF)
                        nc.vector.scalar_tensor_tensor(o[b][:, cols], o_tr[:].rearrange("p j q -> p (j q)"),
                                                       g_sb[b][:, ds(p, 1)], silu[b][:, cols],
                                                       ALU.mult, ALU.mult).then_inc(mixed, 1)

            def root(p, b):
                n = HEADS_PER_PASS * p + b
                x, r, t = var[b][:], rstd[b][:], newton[:]
                done = [ROOT_STEPS * n]

                def link(ins):
                    done[0] = done[0] + 1
                    ins.then_inc(root_step, 1)
                    dve.wait_ge(root_step, done[0])

                dve.wait_ge(summed, chunk_no(p, b, 1) + 1)
                link(nc.vector.tensor_scalar(x, x, 1.0 / HEAD_DIM, EPS, ALU.mult, ALU.add))
                link(nc.vector.tensor_scalar(t.bitcast(I32), x.bitcast(I32), 1, None, ALU.logical_shift_right))
                link(nc.vector.tensor_scalar(r.bitcast(I32), t.bitcast(I32), -1.0, float(0x5f3759df), ALU.mult, ALU.add))
                for step in range(3):
                    link(nc.vector.scalar_tensor_tensor(t, r, -0.5, r, ALU.mult, ALU.mult))
                    link(nc.vector.tensor_tensor(t, t, x, ALU.mult))
                    last = nc.vector.scalar_tensor_tensor(r, t, 1.5, r, ALU.add, ALU.mult)
                    if step < 2:
                        link(last)
                last.then_inc(rooted, 1)

            dve.wait_ge(small_in, 48)
            nc.vector.tensor_copy(ident16[:], squares[0][:, 0:P]).then_inc(converted, 1)
            nc.vector.tensor_copy(strict[:], squares[0][:, P:2 * P]).then_inc(converted, 1)
            for x in range(2):
                lo_part(dve, nc.vector, 0, SB, x)
            dve.wait_ge(consts_in, 16 * CONST_DMAS)
            for i in range(SEL0):
                keys = (i + 1) * P
                nc.vector.tensor_copy(bias[:, i, 0:keys], squares[1][:, i * P:i * P + keys]).then_inc(converted, 1)
            dve.wait_ge(converted, 4)
            run(in_order(0, first=True))
            with dve.Fori(1, PASSES - 1) as p:
                run(in_order(p))
            run(in_order(PASSES - 1, last=True))
            run(left_over(PASSES - 1))

        @block.tensor
        def _(pe):
            def run(events):
                for kind, p, arg in events:
                    if kind == "scores":
                        b, i = divmod(arg, ST)
                        if i == 0:
                            pe.wait_ge(lo_made[b], 2 * (p + 1))
                        wait_units(pe, sc_read, p, arg - 2)
                        keys = (i + 1) * P
                        rows = slice(i * P, (i + 1) * P)
                        for c in range(0, keys, HALF):
                            end = max(min(c + HALF, keys), c + MIN_COLS)
                            masked = b == SB and c + HALF >= keys
                            out = sc[arg % 2][:, c:end]
                            (q_hi, k_hi), (q_lo, k_lo) = qk_hi[b], qk_lo[b]
                            nc.tensor.matmul(out, q_hi[:, rows], k_hi[:, c:end], start=True, stop=False)
                            nc.tensor.matmul(out, q_lo[:, rows], k_hi[:, c:end], start=False, stop=False)
                            mm = nc.tensor.matmul(out, q_hi[:, rows], k_lo[:, c:end], start=False, stop=not masked)
                            if masked:
                                mm = nc.tensor.matmul(sc[arg % 2][:, i * P:keys], ident16[:], strict[:],
                                                      start=False, stop=True)
                        mm.then_inc(scored, 1)
                    elif kind in ("turn", "turn_v"):
                        if kind == "turn":
                            src = w[arg % RING]
                            wait_units(pe, w_ready, p, arg)
                        else:
                            src = v_t[arg]
                            pe.wait_ge(v_in[arg], 16 * (p + 1))
                        for j0 in groups_of(kind, arg):
                            bank, done = group(p, kind, arg, j0)
                            wait(pe, copied[bank], done - 1)
                            for j in range(j0, j0 + tiles_in(kind, arg, j0)):
                                mm = nc.tensor.transpose(tr[bank][:, j - j0, :], src[:, j * P:(j + 1) * P], ident[:])
                            mm.then_inc(turned[bank], 1)
                    elif kind == "value":
                        b, i = divmod(arg, ST)
                        for j0 in groups_of("turn", arg):
                            bank, done = group(p, "turn", arg, j0)
                            pe.wait_ge(copied[bank], done)
                        if i == 0:
                            for j0 in groups_of("turn_v", b):
                                bank, done = group(p, "turn_v", b, j0)
                                pe.wait_ge(copied[bank], done)
                        if i % CH == 0:
                            wait(pe, pv_read, chunk_no(p, b, i // CH))
                        for j in range(i + 1):
                            mm = nc.tensor.matmul(pv[:, i % CH, :], w_t[arg % TURNED_RING][:, j, :], v[b][:, j, :],
                                                  start=j == 0, stop=j == i)
                        mm.then_inc(valued, 1)
                    elif kind == "turn_o":
                        b, c = arg
                        no = chunk_no(p, b, c)
                        pe.wait_ge(o_scaled, no + 1)
                        wait(pe, mixed, no)
                        for j in range(CH):
                            mm = nc.tensor.transpose(o_tr[:, j, :], o_q[b][:, CH * c + j, :], ident[:])
                        mm.then_inc(o_turned, 1)

            pe.wait_ge(small_in, 48)
            pe.wait_ge(converted, 2)
            run(in_order(0, first=True, pe=True))
            with pe.Fori(1, PASSES - 1) as p:
                run(in_order(p, pe=True))
            run(in_order(PASSES - 1, last=True, pe=True))
            run(left_over(PASSES - 1, pe=True))


def output(nc, sem, mixed_t, w_out, m_first, m_first_in, w_raw, w_in, x, final_g, out):
    NC = D_MODEL // HALF
    HT = ST // 2
    WR = WO_RING
    RAW = 4
    FIRST_ADD = WR - 1
    with ExitStack() as ctx:
        sb = lambda name, shape, dt=F32: ctx.enter_context(nc.sbuf_tensor(name, shape, dt))
        m_raw = sb("m_raw", [P, KT, HALF])
        m_hi = sb("m_hi", [P, KT, HALF], F32R)
        m_lo = sb("m_lo", [P, KT, HALF], F32R)
        w_hi = [sb(f"wo_hi{r}", [P, HALF], F32R) for r in range(WR)]
        w_lo = [sb(f"wo_lo{r}", [P, HALF], F32R) for r in range(WR)]
        x2 = sb("x2", [P, ST, D_MODEL])
        g_sb = sb("final_g_sb", [P, D_MODEL])
        squares = sb("squares_o", [P, HT, HALF], BF16)
        eps = sb("eps_o", [P, 1])
        parts = sb("parts", [P, ST, NC])
        total, deviation, inverse, step, rstd = (sb(n, [P, ST]) for n in ("total", "deviation", "inverse", "step", "rstd_o"))
        acc = [ctx.enter_context(nc.psum_tensor(f"oacc{t}", [P, HALF], F32)) for t in range(HT)]
        m_in = [[sem(f"m_in{h}_{k}") for k in range(0, KT, RAW)] for h in range(2)]
        x_in, g_in, eps_set = sem("x_in"), sem("fg_in"), sem("eps_o_set")
        m_hi_made, m_lo_made, w_hi_made, w_lo_made = sem("m_hi_made"), sem("m_lo_made"), sem("wo_hi_made"), sem("wo_lo_made")
        k_done, added, squared = sem("k_done"), sem("added"), sem("o_squared")
        totalled, rooted, scaled, fin_step, stored = sem("totalled"), sem("o_rooted"), sem("o_scaled"), sem("o_fin_step"), sem("o_stored")
        block = ctx.enter_context(nc.Block())
        assert M_FIRST == RAW == WR

        STEPS = KT - 1 + HT

        def k_used(it, k):
            if k < 0:
                return k_used(it - 1, KT + k)
            return STEPS * it + (STEPS if k == KT - 1 else k + 1)

        def load_m_tiles(eng, h, k):
            eng.dma_start(m_raw[:, k:k + RAW, :],
                          mixed_t[k:k + RAW, :, h * HALF:(h + 1) * HALF].rearrange("k p s -> p k s")).then_inc(m_in[h][k // RAW], 16)

        def m_tile(h, k):
            return m_first[:, k, :] if h == 0 and k < M_FIRST else m_raw[:, k, :]

        @block.sync
        def _(sp):
            def load_w(it, c):
                for k in range(KT):
                    sp.wait_ge(w_lo_made, KT * it + k - WR + 1)
                    sp.dma_start(w_raw[k % WR][:], w_out[c, k]).then_inc(w_in[k % WR], 16)

            for k in range(M_FIRST, KT):
                if k % RAW == 0:
                    load_m_tiles(sp, 0, k)
                sp.wait_ge(w_lo_made, k - WR + 1)
                sp.dma_start(w_raw[k % WR][:], w_out[0, k]).then_inc(w_in[k % WR], 16)
            with sp.Fori(1, NC) as c:
                load_w(c, c)
            load_w(NC, 0)
            with sp.Fori(1, NC) as c:
                load_w(NC + c, c)

        @block.gpsimd
        def _(pool):
            nc.gpsimd.memset(eps[:], EPS).then_inc(eps_set, 1)

            def load_x(it):
                h, c = divmod(it, NC)
                pool.wait_ge(w_lo_made, KT * it + KT // 2)
                if it:
                    pool.wait_ge(x_in, 16 * it)
                cols = slice(c * HALF, (c + 1) * HALF)
                rows = x.rearrange("(t p) d -> p t d", p=P)[:, HT * h:HT * h + HT, cols]
                pool.dma_start(x2[:, HT * h:HT * h + HT, cols], rows).then_inc(x_in, 16)

            def store(h):
                for t in range(HT * h, HT * h + HT):
                    pool.wait_ge(scaled, t + 1)
                    pool.dma_start(out[t * P:(t + 1) * P, :], x2[:, t, :]).then_inc(stored, 16)

            load_x(0)
            pool.wait_ge(m_lo_made, KT)
            for k in range(0, KT // 2, RAW):
                load_m_tiles(pool, 1, k)
            load_x(1)
            for k in range(KT // 2, KT, RAW):
                load_m_tiles(pool, 1, k)
            load_x(2)
            pool.dma_start(g_sb[:], final_g.partition_broadcast(P)).then_inc(g_in, 16)
            load_x(3)
            load_x(4)
            store(0)
            for it in range(NC + 1, 2 * NC):
                load_x(it)
            store(1)
            pool.wait_ge(stored, 16 * ST)

        @block.scalar
        def _(act):
            act.wait_ge(eps_set, 1)

            def m_part(h, k):
                if h == 0 and k < M_FIRST:
                    act.wait_ge(m_first_in, 16 * M_FIRST)
                elif k % RAW == 0:
                    act.wait_ge(m_in[h][k // RAW], 16)
                if h:
                    act.wait_ge(k_done, k_used(NC - 1, k))
                nc.scalar.activation(m_hi[:, k, :], m_tile(h, k), ACT.Copy).then_inc(m_hi_made, 1)

            def w_part(it, k, first=False):
                r = k % WR
                act.wait_ge(w_in[r], 16 * ((KT // WR) * it + k // WR + 1))
                if not (first and k < WR):
                    act.wait_ge(k_done, k_used(it, k - WR))
                nc.scalar.activation(w_hi[r][:], w_raw[r][:], ACT.Copy).then_inc(w_hi_made, 1)

            def square(it, h, c):
                for t in range(HT):
                    act.wait_ge(added, HT * it + t + 1)
                    if not (isinstance(it, int) and it == 0):
                        act.wait_ge(squared, HT * (it - 1) + t + 1)
                    nc.scalar.activation(squares[:, t, :], x2[:, HT * h + t, ds(c * HALF, HALF)], ACT.Square,
                                         accum_out=parts[:, HT * h + t, ds(c, 1)]).then_inc(squared, 1)

            def root(h):
                act.wait_ge(totalled, h + 1)
                tiles = slice(HT * h, HT * h + HT)
                nc.scalar.activation(deviation[:, tiles], total[:, tiles], ACT.Sqrt, bias=eps[:],
                                     scale=1.0 / D_MODEL).then_inc(rooted, 1)

            def chunk(it, h, c):
                for k in range(KT):
                    w_part(it, k)
                    if k == WR - 1:
                        square(it - 1, h, c)

            for k in range(KT):
                m_part(0, k)
                w_part(0, k, True)
            chunk(1, 0, 0)
            with act.Fori(2, NC - 1) as it:
                chunk(it, 0, it - 1)
            for k in range(KT):
                w_part(NC - 1, k)
                if k == WR - 1:
                    square(NC - 2, 0, NC - 2)
                if k >= WR:
                    m_part(1, k - WR)
            for k in range(KT):
                w_part(NC, k)
                if k < WR:
                    m_part(1, KT - WR + k)
                if k == WR - 1:
                    square(NC - 1, 0, NC - 1)
                if k == WR:
                    root(0)
            with act.Fori(1, NC) as c:
                chunk(NC + c, 1, c - 1)
            square(2 * NC - 1, 1, NC - 1)
            root(1)

        @block.vector
        def _(dve):
            def m_part(h, k):
                dve.wait_ge(m_hi_made, KT * h + k + 1)
                nc.vector.tensor_tensor(m_lo[:, k, :], m_tile(h, k), m_hi[:, k, :].bitcast(F32),
                                        ALU.subtract).then_inc(m_lo_made, 1)

            def w_part(it, k):
                r = k % WR
                dve.wait_ge(w_hi_made, KT * it + k + 1)
                nc.vector.tensor_tensor(w_lo[r][:], w_raw[r][:], w_hi[r][:].bitcast(F32),
                                        ALU.subtract).then_inc(w_lo_made, 1)

            def add(it, h, c):
                dve.wait_ge(x_in, 16 * (it + 1))
                for t in range(HT):
                    dve.wait_ge(k_done, STEPS * it + KT + t)
                    part = x2[:, HT * h + t, ds(c * HALF, HALF)]
                    nc.vector.tensor_tensor(part, acc[t][:], part, ALU.add).then_inc(added, 1)

            def sum_parts(h):
                dve.wait_ge(squared, HT * NC * (h + 1))
                tiles = slice(HT * h, HT * h + HT)
                nc.vector.tensor_reduce(total[:, tiles], parts[:, tiles, :], AX.X, ALU.add).then_inc(totalled, 1)

            def invert(h):
                tiles = slice(HT * h, HT * h + HT)
                v, d, r, t = total[:, tiles], deviation[:, tiles], inverse[:, tiles], step[:, tiles]
                dve.wait_ge(rooted, h + 1)
                nc.vector.reciprocal(r, d).then_inc(fin_step, 1)
                nc.vector.tensor_scalar(v, v, 1.0 / D_MODEL, EPS, ALU.mult, ALU.add).then_inc(fin_step, 1)
                dve.wait_ge(fin_step, 5 * h + 2)
                nc.vector.tensor_tensor(t, r, r, ALU.mult).then_inc(fin_step, 1)
                dve.wait_ge(fin_step, 5 * h + 3)
                nc.vector.scalar_tensor_tensor(t, t, -0.5, v, ALU.mult, ALU.mult).then_inc(fin_step, 1)
                dve.wait_ge(fin_step, 5 * h + 4)
                nc.vector.scalar_tensor_tensor(rstd[:, tiles], t, 1.5, r, ALU.add, ALU.mult).then_inc(fin_step, 1)
                dve.wait_ge(fin_step, 5 * h + 5)

            def norm(t):
                nc.vector.scalar_tensor_tensor(x2[:, t, :], x2[:, t, :], rstd[:, t:t + 1], g_sb[:],
                                               ALU.mult, ALU.mult).then_inc(scaled, 1)

            def chunk(it, h, c):
                for k in range(KT):
                    if k == FIRST_ADD:
                        add(it - 1, h, c)
                    w_part(it, k)

            for k in range(KT):
                m_part(0, k)
                w_part(0, k)
            with dve.Fori(1, NC - 1) as it:
                chunk(it, 0, it - 1)
            for k in range(KT):
                if k == FIRST_ADD:
                    add(NC - 2, 0, NC - 2)
                w_part(NC - 1, k)
                if k >= WR:
                    m_part(1, k - WR)
            for k in range(KT):
                if k == FIRST_ADD:
                    add(NC - 1, 0, NC - 1)
                w_part(NC, k)
                if k < WR:
                    m_part(1, KT - WR + k)
                if k == WR:
                    sum_parts(0)
                if k == WR + 1:
                    dve.wait_ge(g_in, 16)
                    invert(0)
                if k > WR and k % 2 and (k - WR) // 2 < HT:
                    norm((k - WR) // 2)
            with dve.Fori(1, NC) as c:
                chunk(NC + c, 1, c - 1)
            add(2 * NC - 1, 1, NC - 1)
            sum_parts(1)
            invert(1)
            for t in range(HT, ST):
                norm(t)

        @block.tensor
        def _(pe):
            def chunk(it, h, c0, first=False):
                for k in range(KT):
                    r = k % WR
                    pe.wait_ge(w_lo_made, KT * it + k + 1)
                    if c0:
                        pe.wait_ge(m_lo_made, KT * h + k + 1)
                    for t in range(HT):
                        rows = slice(t * P, (t + 1) * P)
                        if k == 0 and not first:
                            pe.wait_ge(added, HT * (it - 1) + t + 1)
                        nc.tensor.matmul(acc[t][:], m_hi[:, k, rows], w_hi[r][:], start=k == 0, stop=False)
                        nc.tensor.matmul(acc[t][:], m_hi[:, k, rows], w_lo[r][:], start=False, stop=False)
                        mm = nc.tensor.matmul(acc[t][:], m_lo[:, k, rows], w_hi[r][:], start=False, stop=k == KT - 1)
                        if k == KT - 1 or t == HT - 1:
                            mm.then_inc(k_done, 1)

            for h in range(2):
                chunk(NC * h, h, True, h == 0)
                with pe.Fori(1, NC) as c:
                    chunk(NC * h + c, h, False)


def hybrid_block(nc, x, positions, norm_g, w_in, head_g, w_out, final_g, inv_freq, sin_sign, ident, strict,
                 window, out):
    proj = nc.dram_tensor("proj", [NBLK, P, SEQ], F32, kind="Internal").ap()
    trig = nc.dram_tensor("trig", [2, P, SEQ], F32, kind="Internal").ap()
    sel_bias = nc.dram_tensor("sel_bias", [ST - SEL0, P, SEQ], BF16, kind="Internal").ap()
    mixed_t = nc.dram_tensor("mixed_t", [KT, P, SEQ], F32, kind="Internal").ap()
    with ExitStack() as ctx:
        sem = lambda name: ctx.enter_context(nc.semaphore(name))
        with ExitStack() as held:
            y_hi = held.enter_context(nc.sbuf_tensor("y_hi", [P, KT, SEQ], F32R))
            y_lo = held.enter_context(nc.sbuf_tensor("y_lo", [P, KT, SEQ], F32R))
            w_raw = [held.enter_context(nc.sbuf_tensor(f"w_raw{g}", [P, KG, P], F32)) for g in range(GRAN)]
            w_loaded = [sem(f"w_loaded{g}") for g in range(GRAN)]
            normalise(nc, sem, x, norm_g, ident, w_in, w_raw, w_loaded, y_hi, y_lo)
            project(nc, sem, w_in, w_raw, w_loaded, positions, inv_freq, sin_sign, trig, window, ident, y_hi, y_lo, proj, sel_bias)
        m_first = ctx.enter_context(nc.sbuf_tensor("m_first", [P, M_FIRST, HALF], F32))
        wo_raw = [ctx.enter_context(nc.sbuf_tensor(f"wo_raw{r}", [P, HALF], F32)) for r in range(WO_RING)]
        m_first_in, wo_in = sem("m_first_in"), [sem(f"wo_in{r}") for r in range(WO_RING)]
        attend(nc, sem, proj, mixed_t, head_g, ident, strict, window, sel_bias, w_out, m_first, m_first_in, wo_raw, wo_in)
        output(nc, sem, mixed_t, w_out, m_first, m_first_in, wo_raw, wo_in, x, final_g, out)


def shape_constants():
    inv_freq = np.zeros((P, 1), np.float32)
    sin_sign = np.ones((P, 1), np.float32)

    def rotation(row, half):
        freq = np.power(np.float32(ROPE_THETA), -np.arange(half, dtype=np.float32) / np.float32(half))
        inv_freq[row:row + half, 0] = inv_freq[row + half:row + 2 * half, 0] = freq
        sin_sign[row:row + half, 0] = -1.0

    rotation(0, NI)
    rotation(IDX_DIM, NI)
    rotation(ROWS_DSA.start, NQ)
    rows, cols = np.arange(P)[:, None], np.arange(2 * SEQ - P)[None, :]
    window = np.where(cols <= rows + SEQ - P, 0.0, MASKED).astype(np.float32)
    strict = np.where(np.arange(P)[None, :] < rows, 0.0, MASKED)
    return {
        "inv_freq": inv_freq, "sin_sign": sin_sign, "ident": np.eye(P, dtype=np.float32),
        "strict": strict.astype(np.float32), "window": window,
    }


def kernel(x, positions, norm_g, w_in, sb_out_g, dsa_out_g, w_out, final_g):
    import concourse.bacc as bacc
    from concourse.bass_utils import run_bass_kernel_spmd

    w = np.zeros((D_MODEL, NBLK * P), np.float32)
    w[:, :D_IN] = np.asarray(w_in)[0]
    w = w.reshape(GRAN, KG, P, NBLK, P).transpose(3, 0, 2, 1, 4)[ORDER]
    wo = np.asarray(w_out)[0].reshape(KT, P, D_MODEL // HALF, HALF).transpose(2, 0, 1, 3)
    head_g = np.stack([np.asarray(g)[0].reshape(8, P).T for g in (sb_out_g, dsa_out_g)])
    arrays = {
        "x": np.asarray(x)[0], "positions": np.asarray(positions)[0], "norm_g": np.asarray(norm_g)[0],
        "w_in": w, "head_g": head_g, "w_out": wo, "final_g": np.asarray(final_g), **shape_constants(),
    }
    arrays = {f"in_{n}": np.ascontiguousarray(a) for n, a in arrays.items()}
    nc = bacc.Bacc("TRN2", target_bir_lowering=False, num_devices=1)
    args = {n[3:]: nc.dram_tensor(n, a.shape, mybir.dt.from_np(a.dtype), kind="ExternalInput").ap()
            for n, a in arrays.items()}
    out = nc.dram_tensor("out", (SEQ, D_MODEL), F32, kind="ExternalOutput").ap()
    hybrid_block(nc, out=out, **args)
    r = run_bass_kernel_spmd(nc, [arrays], core_ids=[0])
    return r.results[0]["out"].reshape(1, SEQ, D_MODEL)
```
